# Optimizing a Trainium2 kernel written in Bass

```python
import math
import jax
import jax.numpy as jnp
from jax import lax
import numpy as np

"""One inference step (DEPTH=2 layers) of a hybrid autoregressive decoder, run for a prompt group
and a sample group that share the same weights.

Layer i uses token mixer (i mod 2): layer 0 = S5 diagonal complex state-space layer (MIMO groups of
16 channels, 64-dim complex state per group, ZOH discretisation, associative scan, Re(C x) + D u, GELU, GLU);
layer 1 = chunked causal spatial-gating MLP (gMLP SGU, chunks of 128 positions, per-head-group masked
lower-triangular 128x128 position mixing). Every layer: pre-RMSNorm -> mixer -> residual add ->
pre-RMSNorm -> hierarchical MoE (top-1 group, top-2 experts within group, SwiGLU experts) -> residual add.
One final RMSNorm.

Inputs:
  x_prompt     (BATCH, SEQ, D_MODEL)            positions 0..SEQ-1
  x_sample     (DEC_BATCH, DEC_SEQ, D_MODEL)    positions PAST_LEN..PAST_LEN+DEC_SEQ-1
  state_ssm_re (DEC_BATCH, SSM_GROUPS, SSM_STATE) real part of the S5 state after PAST_LEN tokens
  state_ssm_im (DEC_BATCH, SSM_GROUPS, SSM_STATE) imaginary part
  + weights
Returns the tuple
  (y_prompt      (BATCH, SEQ, D_MODEL),
   y_sample      (DEC_BATCH, DEC_SEQ, D_MODEL),
   ssm_re_prompt (BATCH, SSM_GROUPS, SSM_STATE),  ssm_im_prompt (BATCH, SSM_GROUPS, SSM_STATE),
   ssm_re_sample (DEC_BATCH, SSM_GROUPS, SSM_STATE), ssm_im_sample (DEC_BATCH, SSM_GROUPS, SSM_STATE),
   sgu_v_sample  (DEC_BATCH, DEC_SEQ, SGU_WIDTH))   normalised v rows opening the new 128-chunk
"""

D_MODEL = 1024
BATCH = 1
SEQ = 2048
DEPTH = 1
DEC_BATCH = 8
DEC_SEQ = 8
PAST_LEN = 16384
PAGE_SIZE = 128

N_MIXERS = 2
SSM_WIDTH = D_MODEL // 2
SSM_GROUP = 16
SSM_GROUPS = SSM_WIDTH // SSM_GROUP
SSM_STATE = 64
SGU_WIDTH = D_MODEL
SGU_HEADS = 8
SGU_HEAD_DIM = SGU_WIDTH // SGU_HEADS
CHUNK = 128
N_EXPERT_GROUPS = 4
EXPERTS_PER_GROUP = 4
N_EXPERTS = N_EXPERT_GROUPS * EXPERTS_PER_GROUP
TOP_K = 2
D_EXPERT = D_MODEL // 4
EPS = 1e-6

kernel_name = "hybrid_s5_sgu_hmoe_step"

def rmsnorm(x, g):
    xf = x.astype(jnp.float32)
    y = xf * lax.rsqrt(jnp.mean(xf * xf, axis=-1, keepdims=True) + EPS)
    return (y * g.astype(jnp.float32)).astype(x.dtype)

def layernorm(x, g, b):
    xf = x.astype(jnp.float32)
    xc = xf - jnp.mean(xf, axis=-1, keepdims=True)
    y = xc * lax.rsqrt(jnp.mean(xc * xc, axis=-1, keepdims=True) + EPS)
    return (y * g.astype(jnp.float32) + b.astype(jnp.float32)).astype(x.dtype)

def _linear_recurrence_combine(e1, e2):
    a1r, a1i, b1r, b1i = e1
    a2r, a2i, b2r, b2i = e2
    return (a2r * a1r - a2i * a1i,
            a2r * a1i + a2i * a1r,
            a2r * b1r - a2i * b1i + b2r,
            a2r * b1i + a2i * b1r + b2i)

def ssm_mixer(x, s0_re, s0_im, w_in, lam_re, lam_im, log_step, b_re, b_im, c_re, c_im, d, w_out):
    f32 = jnp.float32
    nb, ns, _ = x.shape
    u = (x @ w_in).astype(f32).reshape(nb, ns, SSM_GROUPS, SSM_GROUP)
    lr = lam_re.astype(f32)
    li = lam_im.astype(f32)
    dt = jnp.exp(log_step.astype(f32))[:, None]
    mag = jnp.exp(lr * dt)
    ang = li * dt
    lb_re = mag * jnp.cos(ang)
    lb_im = mag * jnp.sin(ang)
    den = lr * lr + li * li
    nr = lb_re - 1.0
    coef_re = (nr * lr + lb_im * li) / den
    coef_im = (lb_im * lr - nr * li) / den
    br = b_re.astype(f32)
    bi = b_im.astype(f32)
    bb_re = coef_re[..., None] * br - coef_im[..., None] * bi
    bb_im = coef_re[..., None] * bi + coef_im[..., None] * br
    bu_re = jnp.einsum('bsgc,gpc->bsgp', u, bb_re)
    bu_im = jnp.einsum('bsgc,gpc->bsgp', u, bb_im)
    s0r = s0_re.astype(f32)
    s0i = s0_im.astype(f32)
    bu_re = bu_re.at[:, 0].add(lb_re * s0r - lb_im * s0i)
    bu_im = bu_im.at[:, 0].add(lb_re * s0i + lb_im * s0r)
    a_re = jnp.broadcast_to(lb_re, bu_re.shape)
    a_im = jnp.broadcast_to(lb_im, bu_im.shape)
    _, _, st_re, st_im = lax.associative_scan(
        _linear_recurrence_combine, (a_re, a_im, bu_re, bu_im), axis=1)
    y = (jnp.einsum('gcp,bsgp->bsgc', c_re.astype(f32), st_re)
         - jnp.einsum('gcp,bsgp->bsgc', c_im.astype(f32), st_im)
         + d.astype(f32) * u)
    y = jax.nn.gelu(y.reshape(nb, ns, SSM_WIDTH)).astype(x.dtype)
    a = y @ w_out
    out = a[..., :D_MODEL] * jax.nn.sigmoid(a[..., D_MODEL:])
    return out, st_re[:, -1], st_im[:, -1]

def sgu_mixer(x, w_in, norm_g, norm_b, w_s, b_s, w_out, chunk_len):
    nb, ns, _ = x.shape
    h = jax.nn.gelu(x @ w_in)
    u, v = jnp.split(h, 2, axis=-1)
    v = layernorm(v, norm_g, norm_b)
    L = chunk_len
    vc = v.reshape(nb, ns // L, L, SGU_HEADS, SGU_HEAD_DIM)
    mask = jnp.tril(jnp.ones((L, L), dtype=bool))
    wm = jnp.where(mask, w_s[:, :L, :L], jnp.zeros((), w_s.dtype))
    z = jnp.einsum('hts,bnshd->bnthd', wm, vc) + b_s[:, :L].T[None, None, :, :, None]
    z = z.reshape(nb, ns, SGU_WIDTH)
    return (u * z) @ w_out, v

def hier_moe(x, w_rg, w_re, w_gate, w_up, w_down):
    nb, ns, dm = x.shape
    xt = x.reshape(nb * ns, dm)
    nt = xt.shape[0]
    rows = jnp.arange(nt)
    pg = jax.nn.softmax((xt @ w_rg).astype(jnp.float32), axis=-1)
    g_idx = jnp.argmax(pg, axis=-1)
    g_w = pg[rows, g_idx]
    le = (xt @ w_re).astype(jnp.float32).reshape(nt, N_EXPERT_GROUPS, EXPERTS_PER_GROUP)
    pe = jax.nn.softmax(le[rows, g_idx], axis=-1)
    top_w, top_i = lax.top_k(pe, TOP_K)
    top_w = top_w / jnp.sum(top_w, axis=-1, keepdims=True)
    eid = g_idx[:, None] * EXPERTS_PER_GROUP + top_i
    combine = jnp.sum(jax.nn.one_hot(eid, N_EXPERTS, dtype=jnp.float32)
                      * (g_w[:, None] * top_w)[..., None], axis=1)
    h = jax.nn.silu(jnp.einsum('td,edf->tef', xt, w_gate)) * jnp.einsum('td,edf->tef', xt, w_up)
    h = h * combine.astype(h.dtype)[..., None]
    return jnp.einsum('tef,efd->td', h, w_down).reshape(nb, ns, dm)

def _normal(k, shape, scale):
    return scale * jax.random.normal(k, shape, jnp.float32)

def setup_inputs(seed: int = 0) -> dict:
    key = jax.random.key(seed)
    ks = jax.random.split(key, 32)
    f32 = jnp.float32
    n = jnp.arange(SSM_STATE, dtype=f32)
    return {
        "x_prompt": _normal(ks[0], (BATCH, SEQ, D_MODEL), 1.0),
        "x_sample": _normal(ks[1], (DEC_BATCH, DEC_SEQ, D_MODEL), 1.0),
        "state_ssm_re": _normal(ks[2], (DEC_BATCH, SSM_GROUPS, SSM_STATE), 0.1),
        "state_ssm_im": _normal(ks[3], (DEC_BATCH, SSM_GROUPS, SSM_STATE), 0.1),
        "norm_mix": 1.0 + _normal(ks[4], (DEPTH, D_MODEL), 0.05),
        "norm_ffn": 1.0 + _normal(ks[5], (DEPTH, D_MODEL), 0.05),
        "norm_final": 1.0 + _normal(ks[6], (D_MODEL,), 0.05),
        "ssm_w_in": _normal(ks[7], (D_MODEL, SSM_WIDTH), D_MODEL ** -0.5),
        "ssm_lambda_re": -0.5 + _normal(ks[8], (SSM_GROUPS, SSM_STATE), 0.01),
        "ssm_lambda_im": math.pi * n[None, :] + _normal(ks[9], (SSM_GROUPS, SSM_STATE), 0.01),
        "ssm_log_step": jax.random.uniform(ks[10], (SSM_GROUPS,), f32, math.log(1e-3), math.log(1e-1)),
        "ssm_b_re": _normal(ks[11], (SSM_GROUPS, SSM_STATE, SSM_GROUP), (2 * SSM_GROUP) ** -0.5),
        "ssm_b_im": _normal(ks[12], (SSM_GROUPS, SSM_STATE, SSM_GROUP), (2 * SSM_GROUP) ** -0.5),
        "ssm_c_re": _normal(ks[13], (SSM_GROUPS, SSM_GROUP, SSM_STATE), (2 * SSM_STATE) ** -0.5),
        "ssm_c_im": _normal(ks[14], (SSM_GROUPS, SSM_GROUP, SSM_STATE), (2 * SSM_STATE) ** -0.5),
        "ssm_d": 1.0 + _normal(ks[15], (SSM_GROUPS, SSM_GROUP), 0.1),
        "ssm_w_out": _normal(ks[16], (SSM_WIDTH, 2 * D_MODEL), SSM_WIDTH ** -0.5),
        "sgu_w_in": _normal(ks[17], (D_MODEL, 2 * SGU_WIDTH), D_MODEL ** -0.5),
        "sgu_norm_g": 1.0 + _normal(ks[18], (SGU_WIDTH,), 0.05),
        "sgu_norm_b": _normal(ks[19], (SGU_WIDTH,), 0.02),
        "sgu_w_s": _normal(ks[20], (SGU_HEADS, CHUNK, CHUNK), CHUNK ** -0.5),
        "sgu_b_s": 1.0 + _normal(ks[21], (SGU_HEADS, CHUNK), 0.1),
        "sgu_w_out": _normal(ks[22], (SGU_WIDTH, D_MODEL), SGU_WIDTH ** -0.5),
        "moe_router_group": _normal(ks[23], (DEPTH, D_MODEL, N_EXPERT_GROUPS), D_MODEL ** -0.5),
        "moe_router_expert": _normal(ks[24], (DEPTH, D_MODEL, N_EXPERTS), D_MODEL ** -0.5),
        "moe_w_gate": _normal(ks[25], (DEPTH, N_EXPERTS, D_MODEL, D_EXPERT), D_MODEL ** -0.5),
        "moe_w_up": _normal(ks[26], (DEPTH, N_EXPERTS, D_MODEL, D_EXPERT), D_MODEL ** -0.5),
        "moe_w_down": _normal(ks[27], (DEPTH, N_EXPERTS, D_EXPERT, D_MODEL), D_EXPERT ** -0.5),
    }

def reference(x_prompt, x_sample, state_ssm_re, state_ssm_im, norm_mix, norm_ffn, norm_final,
              ssm_w_in, ssm_lambda_re, ssm_lambda_im, ssm_log_step, ssm_b_re, ssm_b_im,
              ssm_c_re, ssm_c_im, ssm_d, ssm_w_out,
              sgu_w_in, sgu_norm_g, sgu_norm_b, sgu_w_s, sgu_b_s, sgu_w_out,
              moe_router_group, moe_router_expert, moe_w_gate, moe_w_up, moe_w_down):
    xp = x_prompt
    xs = x_sample
    ssm_re_prompt = ssm_im_prompt = ssm_re_sample = ssm_im_sample = sgu_v_sample = None
    for i in range(DEPTH):
        hp = rmsnorm(xp, norm_mix[i])
        hs = rmsnorm(xs, norm_mix[i])
        if i % N_MIXERS == 0:
            zero_state = jnp.zeros((xp.shape[0], SSM_GROUPS, SSM_STATE), jnp.float32)
            mp, ssm_re_prompt, ssm_im_prompt = ssm_mixer(
                hp, zero_state, zero_state, ssm_w_in, ssm_lambda_re, ssm_lambda_im, ssm_log_step,
                ssm_b_re, ssm_b_im, ssm_c_re, ssm_c_im, ssm_d, ssm_w_out)
            ms, ssm_re_sample, ssm_im_sample = ssm_mixer(
                hs, state_ssm_re, state_ssm_im, ssm_w_in, ssm_lambda_re, ssm_lambda_im, ssm_log_step,
                ssm_b_re, ssm_b_im, ssm_c_re, ssm_c_im, ssm_d, ssm_w_out)
        else:
            mp, _ = sgu_mixer(hp, sgu_w_in, sgu_norm_g, sgu_norm_b, sgu_w_s, sgu_b_s, sgu_w_out, CHUNK)
            ms, sgu_v_sample = sgu_mixer(hs, sgu_w_in, sgu_norm_g, sgu_norm_b, sgu_w_s, sgu_b_s,
                                         sgu_w_out, DEC_SEQ)
        xp = xp + mp
        xs = xs + ms
        xp = xp + hier_moe(rmsnorm(xp, norm_ffn[i]), moe_router_group[i], moe_router_expert[i],
                           moe_w_gate[i], moe_w_up[i], moe_w_down[i])
        xs = xs + hier_moe(rmsnorm(xs, norm_ffn[i]), moe_router_group[i], moe_router_expert[i],
                           moe_w_gate[i], moe_w_up[i], moe_w_down[i])
    y_prompt = rmsnorm(xp, norm_final)
    y_sample = rmsnorm(xs, norm_final)
    return (y_prompt, y_sample, ssm_re_prompt, ssm_im_prompt, ssm_re_sample, ssm_im_sample, sgu_v_sample)


_drawn_inputs = setup_inputs


def setup_inputs(seed=0):
    import zlib

    import numpy as np

    out = dict(_drawn_inputs(seed))
    spreads = {}
    factors = {}
    for name, (base, spread) in spreads.items():
        noise = np.random.default_rng([zlib.crc32(name.encode()), seed]).standard_normal(out[name].shape)
        drawn = base * np.exp(spread * noise) if base else spread * noise
        out[name] = jnp.asarray(drawn.astype(out[name].dtype))
    for name, factor in factors.items():
        out[name] = (out[name] * factor).astype(out[name].dtype)
    return out
```

```python
from contextlib import ExitStack

import concourse.bass as bass
from concourse import mybir

F32 = mybir.dt.float32
I32 = mybir.dt.int32
U32 = mybir.dt.uint32
F32R = mybir.dt.float32r
ALU = mybir.AluOpType
ACT = mybir.ActivationFunctionType
AX = mybir.AxisListType.X
ds = bass.ds

P = 128
D = 1024
SEQ, DECB, DECS = 2048, 8, 8
L = 8
NCH = DECB + SEQ // L
NP_CH = SEQ // L
NT = NCH * L
KD = D // P
W = 512
G, GC, ST = 32, 16, 64
PR = G // 2
CB = W // P
TT = -(-NT // P)
TF = NT // P
LAST = NT - TF * P
NG, NEG, NE = 4, 4, 16
DE = 256
SLOTS = (2 * NT + NE * (P - 1)) // P
EPS = 1e-6
INV_2PI = 0.15915494309189535
ROUND = 12582912.0
PI_HI, PI_MID, PI_LO = 6.28125, 0.0019350051879882812, 3.0199159819e-07
PI_IN = 3.1415925
RSQRT_SEED = 1597463007.0
EW = KD * 2 * DE + (DE // P) * D
CUTS, UP_CUTS = 3, 2
CW = EW // CUTS
C_EXP, C_AT, C_NEXT = (i * SLOTS for i in range(3))
SKIP = 1


def hybrid_kernel(nc, x_rows, x_cols, s0, par, b_in, c_in, d_in, gmix, gffn, gfin, w_in, w_out, w_route,
                  w_gu, w_dn, y_out, st_out):
    uD = nc.dram_tensor("u_by_step", (L, P, CB, NCH), F32, kind="Internal").ap()
    yD = nc.dram_tensor("y_by_block", (CB, P, 8, NCH), F32, kind="Internal").ap()
    x2D = nc.dram_tensor("x_after_mixer", (NT, D), F32, kind="Internal").ap()
    xnD = nc.dram_tensor("x_normed", (NT, D), F32, kind="Internal").ap()
    moD = nc.dram_tensor("expert_rows", (SLOTS * P, D), F32, kind="Internal").ap()

    outer = ExitStack()
    with outer:
        scope = [outer]

        def sb(name, shape, dt=F32):
            return scope[0].enter_context(nc.sbuf_tensor(name, shape, dt))

        def sem(name):
            return outer.enter_context(nc.semaphore(name))

        def cut(ap, n):
            return ap[0:n]

        pbig = outer.enter_context(nc.psum_tensor("pbig", [P, 8, 512], F32))

        ident = sb("ident", [P, P])
        ones = sb("ones", [P, P])
        upper = sb("upper", [P, P])
        gf_b = sb("gf_b", [P, D])
        gl_b = sb("gl_b", [P, D])
        wr_sb = sb("wr_sb", [P, KD, 20])
        logit = sb("logit", [P, TT, 20])
        slot_i = sb("slot_i", [P, 2, TT], I32)
        cw = sb("cw", [P, 2, TT])
        token_of = sb("token_of", [P, SLOTS], U32)
        ctrl = sb("ctrl", [1, 3 * SLOTS], I32)
        epsc = sb("epsc", [P, 1])

        mix = ExitStack()
        scope[0] = mix
        U = sb("U", [P, G, NCH])
        PAR = sb("PAR", [P, 3, PR])
        s0_sb = sb("s0_sb", [P, 2, PR, DECB])
        BC = sb("BC", [P, 4, PR, GC])
        d_sb = sb("d_sb", [P, G])
        gm_sb = sb("gm_sb", [P, KD])
        sm = sb("sm", [P, 24, PR])
        PW = sb("PW", [P, 3, L + 1, PR])
        PH = sb("PH", [P, 2, 8, PR])
        tq = sb("tq", [P, 4, PR * 4])
        BB = sb("BB", [P, 2, PR, GC])
        WT = sb("WT", [P, 2, PR, NP_CH])
        E = sb("E", [P, 2, PR, L * GC])
        CL = sb("CL", [P, 2, PR, (L + 1) * GC])
        T = sb("T", [P, G, L * GC])
        F0 = sb("F0", [P, 2, PR, DECB])
        FO = sb("FO", [P, 2, PR, DECB + 1])
        aonly = ExitStack()
        scope[0] = aonly
        xT = [sb(f"xT{b}", [P, KD, NCH]) for b in range(2)]
        sq = sb("sq", [P, KD, NCH])
        red = [sb(f"red{b}", [P, NCH]) for b in range(2)]
        std = [sb(f"std{b}", [P, NCH]) for b in range(2)]
        rst = [sb(f"rst{b}", [P, NCH]) for b in range(2)]
        uT = [sb(f"uT{b}", [P, CB, NCH]) for b in range(2)]
        w1 = sb("w1", [P, KD, W])
        p1 = sb("p1", [P, (L + 1) * PR * GC])
        p2 = p1
        aonly.close()
        bonly = ExitStack()
        scope[0] = bonly
        Kst = sb("Kst", [GC, G, L * GC])
        ES = [sb(f"ES{b}", [P, 2, P]) for b in range(2)]
        NS = [sb(f"NS{b}", [P, 2, P]) for b in range(2)]
        TS = [sb(f"TS{b}", [P, 2, P]) for b in range(2)]
        MZ = [sb(f"MZ{b}", [P, 2, 2, P]) for b in range(2)]
        Sp = [sb(f"Sp{b}", [P, 2, NCH + 1]) for b in range(2)]
        r1 = sb("r1", [P, 2, NP_CH])
        r2 = sb("r2", [P, 2, NP_CH])
        z = sb("z", [P, 2, NP_CH])
        yt = [sb(f"yt{b}", [P, NCH]) for b in range(2)]
        bonly.close()
        mix.close()

        cst = ExitStack()
        scope[0] = cst
        pad = sb("pad", [P, G * NCH])
        yT = sb("yT", [P, CB, L, NCH])
        w2 = sb("w2", [P, CB, 2 * D])
        ys = [sb(f"ys{b}", [P, CB, P]) for b in range(2)]
        xr = [sb(f"xr{b}", [P, D]) for b in range(2)]
        sg = sb("sg", [P, D])
        x2 = [sb(f"x2{b}", [P, D]) for b in range(2)]
        xn = [sb(f"xn{b}", [P, D]) for b in range(2)]
        junk = sb("junk", [P, D])
        xnT = sb("xnT", [P, KD, P])
        ssq = sb("ssq", [P, TT])
        nv = sb("nv", [P, 8])
        nvi = sb("nvi", [P, 2], I32)
        cst.close()

        dst = ExitStack()
        scope[0] = dst
        R3 = [sb(f"R3{i}", [P, TT, 4]) for i in range(10)]
        R1 = [sb(f"R1{i}", [P, TT]) for i in range(12)]
        L4 = sb("L4", [P, TT, NG, NEG])
        E1 = sb("E1", [P, TT, NG, NEG])
        E2 = sb("E2", [P, TT, NG, NEG])
        EE = sb("EE", [P, TT, NG, NEG])
        cnt = sb("cnt", [P, NE, TT])
        inc_t = sb("inc_t", [P, NE, TT])
        exc_t = sb("exc_t", [P, NE, TT])
        rst_t = sb("rst_t", [P, NE, TT])
        spos = sb("spos", [P, TT, NE])
        te = sb("te", [P, 6, NE])
        tei = sb("tei", [P, 2, NE], I32)
        desc = sb("desc", [P, 4])
        iot = sb("iot", [P, P])
        tokid = sb("tokid", [P, TT])
        si = sb("si", [P, 2, 2, TT], I32)
        sf = sb("sf", [P, 2, 2, TT])
        oh_lo = [sb(f"oh_lo{b}", [P, P]) for b in range(4)]
        oh_hi = [sb(f"oh_hi{b}", [P, SLOTS]) for b in range(4)]
        cmpe = sb("cmpe", [1, SLOTS, NE])
        eof = sb("eof", [1, 6, SLOTS])
        dst.close()

        est = ExitStack()
        scope[0] = est
        xg = [sb(f"xg{b}", [P, D]) for b in range(2)]
        xgH = [sb(f"xgH{b}", [P, KD, P], F32R) for b in range(2)]
        xgL = [sb(f"xgL{b}", [P, KD, P], F32R) for b in range(2)]
        sl = sb("sl", [P, DE])
        hh = [sb(f"hh{b}", [P, DE]) for b in range(2)]
        hTH = [sb(f"hTH{b}", [P, 2, P], F32R) for b in range(2)]
        hTL = [sb(f"hTL{b}", [P, 2, P], F32R) for b in range(2)]
        yo = [sb(f"yo{b}", [P, D]) for b in range(2)]
        fx = [sb(f"fx{b}", [P, D]) for b in range(2)]
        fss = sb("fss", [P, TT])
        fnv = sb("fnv", [P, 2, 4])
        wst = ExitStack()
        scope[0] = wst
        WR = sb("WR", [P, 2 * EW])
        WH = sb("WH", [P, 2 * EW], F32R)
        WL = sb("WL", [P, 2 * EW], F32R)
        wst.close()
        scope[0] = est
        f1 = [sb(f"f1{b}", [P, D]) for b in range(2)]
        f2 = [sb(f"f2{b}", [P, D]) for b in range(2)]
        fo = [sb(f"fo{b}", [P, D]) for b in range(2)]
        fj = sb("fj", [P, D])
        est.close()

        names = """par_in win_in con_in c_g1 c_pool dch w_scaled act_small pws_ready pool_chain tabs_ready
            x_in0 x_in1 sq_done red_done ss_done var_done std_done um_done u_evac u_stored u_in
            k_done k_evac t_in t_zero tr_done mz_done v_done cp_done sp_done y_done yp_done gelu_done fo_done
            y_stored y_in dchb mz_zero st_stored
            wout_in ys_done a_done sig_done x2_done xn_done xr_in0 xr_in1 x2_st0 x2_st1 xn_st0 xn_st1 xt_done xt_evac rl_done rl_evac ssq_done dchc
            dchd dche exp_d cnt_done one_hot_done tbl_done ctl_done d_iota d_ready exp_in
            g_idx gat0 gat1 xgt_done xgt_evac xgt_lo gu_done h_done sl_done ht_done ht_evac hi_split lo_split dn_done dn_evac wts mo_st0 mo_st1
            fx_in0 fx_in1 f_in0 f_in1 f_sum f_sq f_rs f_out f_st0 f_st1 dchf f_std f_idx""".split()
        S = {n: sem(n) for n in names}
        block = outer.enter_context(nc.Block())

        def steps(eng, n, step):
            step(0, 0)
            step(1, 1)
            with eng.Fori(1, n // 2) as i:
                step(2 * i, 0)
                step(2 * i + 1, 1)

        def early(t, n=2):
            return isinstance(t, int) and t < n

        class Chain:
            def __init__(self, eng, s):
                self.eng, self.s, self.n = eng, s, 0

            def __call__(self, ins):
                self.n += 1
                ins.then_inc(self.s, 1)
                self.eng.wait_ge(self.s, self.n)

        @block.sync
        def _(sp):
            for dst_, src in ((PAR[:, :, :], par), (s0_sb[:, :, :, :], s0), (BC[:, :, :, :], b_in),
                              (d_sb[:, :], d_in), (gm_sb[:, :], gmix)):
                sp.dma_start(dst_, src).then_inc(S["par_in"], 16)
            sp.dma_start(w1[:, :, :], w_in).then_inc(S["win_in"], 16)
            for j in range(2):
                sp.dma_start(xT[j][:, :, :], x_cols[j]).then_inc(S[f"x_in{j}"], 16)
            sp.dma_start(gf_b[:, :], gffn.partition_broadcast(P)).then_inc(S["con_in"], 16)
            sp.dma_start(gl_b[:, :], gfin.partition_broadcast(P)).then_inc(S["con_in"], 16)
            sp.dma_start(wr_sb[:, :, :], w_route).then_inc(S["con_in"], 16)
            for j in range(L):
                sp.wait_ge(S["u_evac"], CB * (j + 1))
                if j + 2 < L:
                    sp.wait_ge(S["sq_done"], j + 1)
                    sp.dma_start(xT[j % 2][:, :, :], x_cols[j + 2]).then_inc(S[f"x_in{j % 2}"], 16)
                sp.dma_start(uD[j], uT[j % 2][:, :, :]).then_inc(S["u_stored"], 16)
                sp.wait_ge(S["u_stored"], 16 * (j + 1))
                for cb in range(CB):
                    sp.dma_start(U[j * GC:(j + 1) * GC, cb * 8:(cb + 1) * 8, :],
                                 uD[j].rearrange("(g c) b k -> b c g k", c=GC)[cb]).then_inc(S["u_in"], 16)
            sp.wait_ge(S["k_evac"], 8)
            sp.wait_ge(S["t_zero"], 1)
            for j in range(L):
                sp.dma_start(T[j * GC:(j + 1) * GC, :, j * GC:L * GC],
                             Kst[:, :, 0:(L - j) * GC]).then_inc(S["t_in"], 16)
            for cb in range(CB):
                sp.wait_ge(S["gelu_done"], 8 * (cb + 1))
                sp.dma_start(yD[cb], U[:, cb * 8:(cb + 1) * 8, :]).then_inc(S["y_stored"], 16)
            sp.wait_ge(S["fo_done"], PR)
            sp.wait_ge(S["y_done"], G)
            sp.wait_ge(S["y_stored"], 16 * CB)
            sp.dma_start(st_out, FO[:, :, :, :]).then_inc(S["st_stored"], 16)
            sp.wait_ge(S["st_stored"], 16)
            sp.dma_start(w2[:, :, :], w_out).then_inc(S["wout_in"], 16)
            for cb in range(CB):
                for g in range(8):
                    sp.dma_start(yT[g * GC:(g + 1) * GC, cb, :, :],
                                 yD[cb].rearrange("(i c) g k -> g c i k", c=GC)[g]).then_inc(S["y_in"], 16)

            def c_load(t, b, rows=P):
                if not early(t):
                    sp.wait_ge(S["x2_done"], t - 1)
                sp.dma_start(cut(xr[b], rows)[:, :], x_rows[ds(t * P, rows), :]).then_inc(S[f"xr_in{b}"], 16)

            def c_store(t, b, rows=P):
                sp.wait_ge(S["x2_done"], t + 1)
                sp.dma_start(x2D[ds(t * P, rows), :], cut(x2[b], rows)[:, :]).then_inc(S[f"x2_st{b}"], 16)
                sp.wait_ge(S["xn_done"], t + 1)
                sp.dma_start(xnD[ds(t * P, rows), :], cut(xn[b], rows)[:, :]).then_inc(S[f"xn_st{b}"], 16)

            c_load(0, 0)
            c_load(1, 1)
            c_store(0, 0)
            c_load(2, 0)
            c_store(1, 1)
            c_load(3, 1)
            with sp.Fori(1, TF // 2 - 1) as i:
                c_store(2 * i, 0)
                c_load(2 * i + 2, 0)
                c_store(2 * i + 1, 1)
                c_load(2 * i + 3, 1)
            c_store(TF - 2, 0)
            c_load(TF, 0, LAST)
            c_store(TF - 1, 1)
            c_store(TF, 0, LAST)

            sp.wait_ge(S["ctl_done"], 1)
            for e in range(NE):
                if e >= 1:
                    sp.wait_ge(S["wts"], 32 * e)
                if e >= 2:
                    sp.wait_ge(S["lo_split"], CUTS * (e - 1))
                at = e % 2 * EW
                sp.dma_start(WR[:, at:at + KD * 2 * DE], w_gu[e]).then_inc(S["wts"], 16)
                sp.dma_start(WR[:, at + KD * 2 * DE:at + EW], w_dn[e]).then_inc(S["wts"], 16)

            def f_load(t, b, rows=P):
                if not early(t):
                    sp.wait_ge(S["f_sum"], t - 1)
                sp.dma_start(cut(fx[b], rows)[:, :], x2D[ds(t * P, rows), :]).then_inc(S[f"fx_in{b}"], 16)

            def f_store(t, b, rows=P):
                sp.wait_ge(S["f_out"], t + 1)
                sp.dma_start(y_out[ds(t * P, rows), :], cut(fo[b], rows)[:, :]).then_inc(S[f"f_st{b}"], 16)

            f_load(0, 0)
            f_load(1, 1)
            with sp.Fori(0, TF // 2 - 1) as i:
                f_store(2 * i, 0)
                f_load(2 * i + 2, 0)
                f_store(2 * i + 1, 1)
                f_load(2 * i + 3, 1)
            f_store(TF - 2, 0)
            f_load(TF, 0, LAST)
            f_store(TF - 1, 1)
            f_store(TF, 0, LAST)
            sp.wait_ge(S["f_st0"], 16 * (TF // 2 + 1))
            sp.wait_ge(S["f_st1"], 16 * (TF // 2))

        @block.gpsimd
        def _(pool):
            ch = Chain(pool, S["pool_chain"])
            ch(pool.memset(ident[:, :], 0.0))
            ch(pool.affine_select(out=ident[:, :], in_=ident[:, :], compare_op=ALU.not_equal, fill=1.0, base=0,
                                  pattern=[[-1, P]], channel_multiplier=1))
            pool.memset(ones[:, :], 1.0).then_inc(S["c_pool"], 1)
            ch(pool.memset(upper[:, :], 1.0))
            ch(pool.affine_select(out=upper[:, :], in_=upper[:, :], compare_op=ALU.is_gt, fill=0.0, base=0,
                                  pattern=[[1, P]], channel_multiplier=-1))
            pool.memset(T[:, :, :], 0.0).then_inc(S["t_zero"], 1)
            pool.wait_ge(S["pws_ready"], 1)

            def cmul(ore, oim, are, aim, bre, bim, ta, tb):
                ch(pool.tensor_tensor(ta, are, bre, ALU.mult))
                ch(pool.tensor_tensor(ore, aim, bim, ALU.mult))
                ch(pool.tensor_tensor(ore, ta, ore, ALU.subtract))
                ch(pool.tensor_tensor(ta, are, bim, ALU.mult))
                ch(pool.tensor_tensor(oim, aim, bre, ALU.mult))
                ch(pool.tensor_tensor(oim, ta, oim, ALU.add))

            def v4(ap):
                return ap.rearrange("p r (d c) -> p r d c", c=GC)

            def t4(n, m):
                return p1[:, 0:n * m * GC].rearrange("p (r d c) -> p r d c", d=m, c=GC)

            def over_c(ap, m):
                return ap.rearrange("p d r -> p r d").unsqueeze(3).to_broadcast([P, PR, m, GC])

            def over_d(ap, m):
                return ap.unsqueeze(2).to_broadcast([P, PR, m, GC])

            m = L + 1
            cre, cim = over_d(BC[:, 2, :, :], m), over_d(BC[:, 3, :, :], m)
            wre, wimn = over_c(PW[:, 0, :, :], m), over_c(PW[:, 2, :, :], m)
            lre, lim = v4(CL[:, 0, :, :]), v4(CL[:, 1, :, :])
            ta = t4(PR, m)
            ch(pool.tensor_tensor(ta, cre, wre, ALU.mult))
            ch(pool.tensor_tensor(lre, cim, wimn, ALU.mult))
            ch(pool.tensor_tensor(lre, lre, ta, ALU.add))
            ch(pool.tensor_tensor(ta, cre, wimn, ALU.mult))
            ch(pool.tensor_tensor(lim, cim, wre, ALU.mult))
            ch(pool.tensor_tensor(lim, ta, lim, ALU.subtract))
            for j in range(L):
                bre, bim = BB[:, 0, :, :], BB[:, 1, :, :]
                pre = PW[:, 0, L - 1 - j, :].unsqueeze(2).to_broadcast([P, PR, GC])
                pim = PW[:, 1, L - 1 - j, :].unsqueeze(2).to_broadcast([P, PR, GC])
                tj = p1[:, 0:PR * GC].rearrange("p (r c) -> p r c", c=GC)
                cmul(E[:, 0, :, j * GC:(j + 1) * GC], E[:, 1, :, j * GC:(j + 1) * GC], bre, bim, pre, pim, tj, None)
            ch(pool.memset(WT[:, 0, :, 0:1], 1.0))
            ch(pool.memset(WT[:, 1, :, 0:1], 0.0))
            for l in range(8):
                n = 1 << l
                pre = PH[:, 0, l, :].unsqueeze(2).to_broadcast([P, PR, n])
                pim = PH[:, 1, l, :].unsqueeze(2).to_broadcast([P, PR, n])
                tl = p1[:, 0:PR * n].rearrange("p (r k) -> p r k", k=n)
                cmul(WT[:, 0, :, n:2 * n], WT[:, 1, :, n:2 * n], WT[:, 0, :, 0:n], WT[:, 1, :, 0:n], pre, pim, tl, None)
            pre = PW[:, 0, L, :].unsqueeze(2).to_broadcast([P, PR, DECB])
            pim = PW[:, 1, L, :].unsqueeze(2).to_broadcast([P, PR, DECB])
            cmul(F0[:, 0, :, :], F0[:, 1, :, :], s0_sb[:, 0, :, :], s0_sb[:, 1, :, :], pre, pim,
                 p1[:, 0:PR * DECB].rearrange("p (r k) -> p r k", k=DECB), None)
            pool.memset(p1[:, 0:1], 0.0).then_inc(S["tabs_ready"], 1)

            pool.wait_ge(S["um_done"], CB * L)
            pool.wait_ge(S["u_evac"], CB * L)
            pool.wait_ge(S["u_stored"], 16 * L)
            pool.wait_ge(S["k_done"], 8)
            for b in range(2):
                pool.memset(MZ[b][:, :, :, :], 0.0).then_inc(S["mz_zero"], 1)
                pool.memset(Sp[b][:, :, DECB:DECB + 1], 0.0).then_inc(S["mz_zero"], 1)
            pool.wait_ge(S["t_in"], 16 * L)

            def b_copy(r, b):
                if not early(r):
                    pool.wait_ge(S["tr_done"], r - 1)
                pool.tensor_copy(ES[b][:, :, :], E[:, :, ds(r, 1), :].rearrange("p a o k -> p a (o k)")).then_inc(S["cp_done"], 1)
                if not early(r):
                    pool.wait_ge(S["y_done"], 2 * r - 2)
                pool.tensor_copy(NS[b][:, :, :], CL[:, :, ds(r, 1), GC:(L + 1) * GC].rearrange("p a o k -> p a (o k)")).then_inc(S["cp_done"], 1)
                pool.tensor_copy(TS[b][:, :, :], T[:, ds(2 * r, 2), :]).then_inc(S["cp_done"], 1)
                pool.tensor_copy(Sp[b][:, :, 0:DECB], s0_sb[:, :, ds(r, 1), :].rearrange("p a o k -> p a (o k)")).then_inc(S["cp_done"], 1)
            steps(pool, PR, b_copy)

            pool.wait_ge(S["y_in"], 16 * CB * 8)
            yflat = yT[:, :, :, :].rearrange("p b i k -> p b (i k)")

            def c_copy(t, b, rows=P):
                if not early(t):
                    pool.wait_ge(S["a_done"], 4 * t - 4)
                pool.tensor_copy(ys[b][:, :, 0:rows], yflat[:, :, ds(t * P, rows)]).then_inc(S["ys_done"], 1)
            steps(pool, TF, c_copy)
            c_copy(TF, 0, LAST)

            pool.wait_ge(S["rl_evac"], TT)
            pool.wait_ge(S["xn_done"], TT)
            for b in range(2):
                pool.wait_ge(S[f"xn_st{b}"], 16 * (TF // 2 + 1 - b))
                pool.wait_ge(S[f"x2_st{b}"], 16 * (TF // 2 + 1 - b))
            pool.iota(iot[:, :], [[1, P]], base=0, channel_multiplier=0, allow_small_or_imprecise_dtypes=True).then_inc(S["d_iota"], 1)
            pool.iota(tokid[:, :], [[P, TT]], base=0, channel_multiplier=1, allow_small_or_imprecise_dtypes=True).then_inc(S["d_iota"], 1)
            pool.iota(desc[:, :], [[-1, 4]], base=4, channel_multiplier=0, allow_small_or_imprecise_dtypes=True).then_inc(S["d_iota"], 1)

            pool.wait_ge(S["ctl_done"], 1)

            for t in range(SLOTS):
                if t >= 2:
                    pool.wait_ge(S["xgt_done"], 2 * t - 2)
                pool.indirect_dma_start(xg[t % 2][:, :], None, xnD,
                                        bass.IndirectOffsetOnAxis(ap=token_of[:, t:t + 1], axis=0)).then_inc(S[f"gat{t % 2}"], 16)

            for b in range(2):
                pool.wait_ge(S[f"mo_st{b}"], 8 * SLOTS)
            for t in range(TT):
                rows = P if t < TF else LAST
                if t >= 2:
                    pool.wait_ge(S["f_sum"], t - 1)
                for c, dst_ in enumerate((f1[t % 2], f2[t % 2])):
                    pool.indirect_dma_start(dst_[0:rows, :], None, moD,
                                            bass.IndirectOffsetOnAxis(ap=slot_i[0:rows, c, t:t + 1], axis=0)).then_inc(S[f"f_in{t % 2}"], 16)

        @block.scalar
        def _(act):
            act.wait_ge(S["par_in"], 80)
            act.activation(sm[:, 0, :], PAR[:, 2, :], ACT.Exp).then_inc(S["act_small"], 1)
            act.wait_ge(S["dch"], 2)
            act.activation(sm[:, 3, :], sm[:, 1, :], ACT.Exp).then_inc(S["act_small"], 1)
            act.activation(sm[:, 4, :], sm[:, 1, :], ACT.Exp, scale=float(L)).then_inc(S["act_small"], 1)
            act.wait_ge(S["c_g1"], 1)
            act.activation(sm[:, 8, :], sm[:, 6, :], ACT.Sin).then_inc(S["act_small"], 1)
            act.activation(sm[:, 9, :], sm[:, 7, :], ACT.Sin).then_inc(S["act_small"], 1)

            def a_step(j, b):
                i = j // 2 if isinstance(j, int) else None
                act.wait_ge(S[f"x_in{b}"], 8 * (j - b) + 16)
                if not (isinstance(j, int) and j == 0):
                    act.wait_ge(S["red_done"], j)
                act.activation(sq[:, :, :], xT[b][:, :, :], ACT.Square).then_inc(S["sq_done"], 1)
                act.wait_ge(S["var_done"], j + 1)
                act.activation(std[b][:, :], rst[b][:, :], ACT.Sqrt).then_inc(S["std_done"], 1)
            for j in range(L):
                a_step(j, j % 2)

            for n in range(8):
                act.wait_ge(S["k_done"], n + 1)
                if n == 0:
                    act.wait_ge(S["u_stored"], 16 * L)
                    act.wait_ge(S["u_evac"], CB * L)
                    act.wait_ge(S["tabs_ready"], 1)
                act.activation(Kst[:, :, :].rearrange("c (r h) k -> c r h k", h=2)[:, n % 4 * 4:n % 4 * 4 + 4, n // 4, :], pbig[0:GC, n, :].rearrange("p (g k) -> p g k", g=4),
                               ACT.Copy).then_inc(S["k_evac"], 1)

            act.wait_ge(S["mz_zero"], 4)

            def b_mz(r, b):
                act.wait_ge(S["tr_done"], r + 1)
                if not early(r):
                    act.wait_ge(S["v_done"], r - 1)
                tr = pbig[:, 4, 0:2 * P].rearrange("p (a m) -> p a m", a=2)
                act.activation(MZ[b][:, 0, :, 0:ST], tr[:, :, 0:ST], ACT.Copy).then_inc(S["mz_done"], 1)
                act.activation(MZ[b][:, 1, :, ST:P], tr[:, :, ST:P], ACT.Copy).then_inc(S["mz_done"], 1)

            def b_gelu(r):
                for g in range(2):
                    act.wait_ge(S["yp_done"], 2 * r + g + 1)
                    act.activation(U[:, ds(2 * r + g, 1), :].rearrange("p o k -> p (o k)"), yt[g][:, :],
                                   ACT.Gelu_apprx_tanh).then_inc(S["gelu_done"], 1)

            b_mz(0, 0)
            b_mz(1, 1)
            b_mz(2, 0)
            b_gelu(0)
            b_mz(3, 1)
            b_gelu(1)
            with act.Fori(1, PR // 2 - 1) as i:
                b_mz(2 * i + 2, 0)
                b_gelu(2 * i)
                b_mz(2 * i + 3, 1)
                b_gelu(2 * i + 1)
            b_gelu(PR - 2)
            b_gelu(PR - 1)

            act.wait_ge(S["wout_in"], 16)

            def c_gate(t, b, rows=P):
                if not early(t, 1):
                    act.wait_ge(S["x2_done"], t)
                for n in range(2):
                    act.wait_ge(S["a_done"], 4 * t + 3 + n)
                    act.activation(sg[0:rows, n * 512:(n + 1) * 512], pbig[0:rows, 2 + n, :], ACT.Sigmoid).then_inc(S["sig_done"], 1)
                act.wait_ge(S["x2_done"], t + 1)
                act.activation(junk[0:rows, :], x2[b][0:rows, :], ACT.Square, accum_out=ssq[0:rows, ds(t, 1)]).then_inc(S["ssq_done"], 1)

            def c_turned(t, rows=P):
                for n in range(2):
                    act.wait_ge(S["xt_done"], 2 * t + n + 1)
                    if n == 0 and not early(t, 1):
                        act.wait_ge(S["rl_done"], t)
                    act.activation(xnT[:, 4 * n:4 * n + 4, 0:rows],
                                   pbig[:, 4 + n, :].rearrange("p (a m) -> p a m", a=4)[:, :, 0:rows], ACT.Copy).then_inc(S["xt_evac"], 1)

            def c_routed(t, rows=P):
                act.wait_ge(S["rl_done"], t + 1)
                act.activation(logit[0:rows, ds(t, 1), :].rearrange("p o k -> p (o k)"), pbig[0:rows, 6, 0:20], ACT.Copy).then_inc(S["rl_evac"], 1)

            c_gate(0, 0)
            c_gate(1, 1)
            c_turned(0)
            with act.Fori(1, TF // 2) as i:
                c_gate(2 * i, 0)
                c_routed(2 * i - 2)
                c_turned(2 * i - 1)
                c_gate(2 * i + 1, 1)
                c_routed(2 * i - 1)
                c_turned(2 * i)
            c_gate(TF, 0, LAST)
            c_routed(TF - 2)
            c_turned(TF - 1)
            c_routed(TF - 1)
            c_turned(TF, LAST)
            c_routed(TF, LAST)

            act.wait_ge(S["exp_in"], 1)
            act.activation(R3[1][:, :, :], R3[0][:, :, :], ACT.Exp).then_inc(S["exp_d"], 1)
            act.wait_ge(S["exp_in"], 2)
            act.activation(R1[5][:, :], R1[4][:, :], ACT.Exp).then_inc(S["exp_d"], 1)

            act.wait_ge(S["ctl_done"], 1)

            def e_x(s, b):
                if not early(s):
                    act.wait_ge(S["gu_done"], s - 1)
                for n in range(2):
                    act.wait_ge(S["xgt_done"], 2 * s + n + 1)
                    act.activation(xgH[b][:, 4 * n:4 * n + 4, :], pbig[:, 4 + n, :].rearrange("p (a m) -> p a m", a=4), ACT.Copy).then_inc(S["xgt_evac"], 1)

            def e_silu(s, b):
                act.wait_ge(S["gu_done"], s + 1)
                if not early(s, 1):
                    act.wait_ge(S["h_done"], s)
                act.activation(sl[:, :], pbig[:, 6, 0:DE], ACT.Silu).then_inc(S["sl_done"], 1)

            def e_y(s, b):
                if not early(s):
                    act.wait_ge(S[f"mo_st{b}"], 8 * (s - b))
                act.wait_ge(S["dn_done"], s + 2)
                act.activation(yo[b][:, :].rearrange("p (a m) -> p a m", a=2), pbig[:, 0:2, :], ACT.Copy).then_inc(S["dn_evac"], 1)
                act.wait_ge(S["dn_evac"], s + 1)
                act.dma_start(moD[ds(s * P, P), :], yo[b][:, :]).then_inc(S[f"mo_st{b}"], 16)

            def e_word(s):
                return act.value_load(ctrl[0:1, ds(C_NEXT + s, 1)], min_val=0, max_val=EW)

            def e_split(s, to, part):
                with act.If(to != SKIP):
                    if part == 0:
                        e = act.value_load(ctrl[0:1, ds(C_EXP + s, 1)], min_val=0, max_val=NE - 1)
                        act.wait_ge(S["wts"], e * 32 + 64)
                    if not early(s, 1):
                        act.wait_ge(S["dn_done"] if part else S["gu_done"], s + part)
                    act.wait_ge(S["ctl_done"], 1)
                    for c in (range(UP_CUTS), range(UP_CUTS, CUTS))[part]:
                        act.activation(WH[:, ds(to + c * CW, CW)], WR[:, ds(to + c * CW, CW)], ACT.Copy).then_inc(S["hi_split"], 1)

            act.wait_ge(S["wts"], 32)
            for c in range(CUTS):
                act.activation(WH[:, c * CW:(c + 1) * CW], WR[:, c * CW:(c + 1) * CW], ACT.Copy).then_inc(S["hi_split"], 1)
            def e_act(s, b, to, ahead=True, last=False):
                then = None
                if not last:
                    e_split(s, to, 0)
                e_silu(s, b)
                if not last:
                    e_x(s + 1, 1 - b)
                    if ahead:
                        then = e_word(s + 1)
                if not early(s, 1):
                    e_y(s - 1, 1 - b)
                if not last:
                    e_split(s, to, 1)
                return then

            e_x(0, 0)
            to = e_act(0, 0, e_word(0))
            e_act(1, 1, to, ahead=False)
            with act.Fori(0, SLOTS // 4 - 1) as i:
                to = e_word(4 * i + 2)
                for n in range(2, 6):
                    to = e_act(4 * i + n, n % 2, to, ahead=n < 5)
            e_act(SLOTS - 2, 0, e_word(SLOTS - 2), ahead=False)
            e_act(SLOTS - 1, 1, None, last=True)
            e_y(SLOTS - 1, 1)

            def f_sq(t, b, rows=P):
                act.wait_ge(S["f_sum"], t + 1)
                act.activation(fj[0:rows, :], fx[b][0:rows, :], ACT.Square, accum_out=fss[0:rows, ds(t, 1)]).then_inc(S["f_sq"], 1)
                act.wait_ge(S["f_rs"], t + 1)
                act.activation(fnv[0:rows, b, 1:2], fnv[0:rows, b, 0:1], ACT.Sqrt).then_inc(S["f_std"], 1)
            steps(act, TF, f_sq)
            f_sq(TF, 0, LAST)

        @block.tensor
        def _(pe):
            pe.wait_ge(S["w_scaled"], KD)
            pe.wait_ge(S["c_pool"], 1)
            for j in range(L):
                b = j % 2
                pe.wait_ge(S[f"x_in{b}"], 16 * (j // 2 + 1))
                for cb in range(CB):
                    if j >= 1:
                        pe.wait_ge(S["u_evac"], CB * (j - 1) + cb + 1)
                    for k in range(KD):
                        mm = pe.matmul(pbig[:, cb, 0:NCH], w1[:, k, cb * P:(cb + 1) * P], xT[b][:, k, :],
                                       start=(k == 0), stop=(k == KD - 1))
                    mm.then_inc(S["um_done"], 1)
                    if cb == 0:
                        pe.wait_ge(S["red_done"], j + 1)
                        pe.matmul(pbig[:, 4 + b, 0:NCH], ones[:, :], red[b][:, :], start=True, stop=True).then_inc(S["ss_done"], 1)
            pe.wait_ge(S["tabs_ready"], 1)
            pe.wait_ge(S["u_evac"], CB * L)
            for n in range(8):
                h = n // 4 * ST
                for q in range(4):
                    r = n % 4 * 4 + q
                    for a in range(2):
                        mm = pe.matmul(pbig[0:GC, n, q * P:(q + 1) * P], BB[h:h + ST, a, r, :],
                                       CL[h:h + ST, a, r, 0:L * GC], start=(a == 0), stop=(a == 1))
                mm.then_inc(S["k_done"], 1)

            pe.wait_ge(S["k_evac"], 8)
            pe.wait_ge(S["u_in"], 16 * L * CB)

            def b_state(r, b):
                pe.wait_ge(S["cp_done"], 4 * r + 1)
                if not early(r, 1):
                    pe.wait_ge(S["mz_done"], 2 * r)
                for a in range(2):
                    mm = pe.transpose(pbig[:, 4, a * P:(a + 1) * P], ES[b][:, a, :], ident[:, :])
                mm.then_inc(S["tr_done"], 1)
                pe.wait_ge(S["mz_done"], 2 * r + 2)
                if not early(r):
                    pe.wait_ge(S["fo_done"], r - 1)
                for a in range(2):
                    for g in range(2):
                        mm = pe.matmul(pbig[:, 2 * b + a, 0:NCH], MZ[b][:, g, a, :],
                                       U[:, ds(2 * r + g, 1), :].rearrange("p o k -> p (o k)"),
                                       start=(g == 0), stop=(g == 1))
                mm.then_inc(S["v_done"], 1)

            def b_out(r, b):
                pe.wait_ge(S["cp_done"], 4 * r + 4)
                pe.wait_ge(S["sp_done"], r + 1)
                for g in range(2):
                    if not early(r, 1):
                        pe.wait_ge(S["yp_done"], 2 * r - 1 + g)
                    h = g * ST
                    out = pbig[:, 5 + g, 0:NCH]
                    pe.matmul(out, TS[b][:, g, :], U[:, ds(2 * r + g, 1), :].rearrange("p o k -> p (o k)"), start=True, stop=False)
                    pe.matmul(out, NS[b][h:h + ST, 0, :], Sp[b][h:h + ST, 0, 0:NCH], start=False, stop=False)
                    pe.matmul(out, NS[b][h:h + ST, 1, :], Sp[b][h:h + ST, 1, 0:NCH], start=False, stop=True).then_inc(S["y_done"], 1)

            b_state(0, 0)
            b_state(1, 1)
            b_out(0, 0)
            b_state(2, 0)
            b_out(1, 1)
            b_state(3, 1)
            with pe.Fori(1, PR // 2 - 1) as i:
                b_out(2 * i, 0)
                b_state(2 * i + 2, 0)
                b_out(2 * i + 1, 1)
                b_state(2 * i + 3, 1)
            b_out(PR - 2, 0)
            b_out(PR - 1, 1)

            pe.wait_ge(S["wout_in"], 16)
            pe.wait_ge(S["yp_done"], G)
            pe.wait_ge(S["con_in"], 48)

            def c_proj(t, b, ns, rows=P):
                if 2 in ns:
                    pe.wait_ge(S["ys_done"], t + 1)
                for n in ns:
                    if not early(t, 1):
                        pe.wait_ge(S["sig_done" if n >= 2 else "x2_done"], 2 * t - 3 + n if n >= 2 else t)
                    for k in range(CB):
                        mm = pe.matmul(pbig[0:rows, n, :], ys[b][:, k, 0:rows], w2[:, k, n * 512:(n + 1) * 512],
                                       start=(k == 0), stop=(k == CB - 1))
                    mm.then_inc(S["a_done"], 1)

            def c_turn(t, b, rows=P):
                pe.wait_ge(S["xn_done"], t + 1)
                for n in range(2):
                    if not early(t, 1):
                        pe.wait_ge(S["xt_evac"], 2 * t - 1 + n)
                    for k in range(4):
                        mm = pe.transpose(pbig[:, 4 + n, k * P:k * P + rows], xn[b][0:rows, (4 * n + k) * P:(4 * n + k + 1) * P],
                                          ident[0:rows, 0:rows])
                    mm.then_inc(S["xt_done"], 1)

            def c_logit(t, rows=P):
                pe.wait_ge(S["xt_evac"], 2 * t + 2)
                if not early(t, 1):
                    pe.wait_ge(S["rl_evac"], t)
                for k in range(KD):
                    mm = pe.matmul(pbig[0:rows, 6, 0:20], xnT[:, k, 0:rows], wr_sb[:, k, :], start=(k == 0), stop=(k == KD - 1))
                mm.then_inc(S["rl_done"], 1)

            def c_step(t, b, rows=P, prev=2):
                c_proj(t, b, (2, 3), rows)
                if prev > 1:
                    c_logit(t - 2)
                c_proj(t, b, (0, 1), rows)
                if prev > 0:
                    c_turn(t - 1, 1 - b)

            c_step(0, 0, prev=0)
            c_step(1, 1, prev=1)
            with pe.Fori(1, TF // 2) as i:
                c_step(2 * i, 0)
                c_step(2 * i + 1, 1)
            c_step(TF, 0, LAST)
            c_logit(TF - 1)
            c_turn(TF, 0, LAST)
            c_logit(TF, LAST)

            pe.wait_ge(S["d_ready"], 1)
            pe.matmul(pbig[:, 0, 0:TT * NE], upper[:, :], EE[:, :, :, :].rearrange("p t g e -> p (t g e)"), start=True, stop=True)
            pe.matmul(pbig[:, 1, 0:TT * NE], ones[:, :], EE[:, :, :, :].rearrange("p t g e -> p (t g e)"), start=True, stop=True).then_inc(S["cnt_done"], 1)
            for n in range(2 * TT):
                pe.wait_ge(S["one_hot_done"], n + 1)
                mm = pe.matmul(pbig[:, 2, 0:SLOTS], oh_lo[n % 4][:, :], oh_hi[n % 4][:, :], start=(n == 0), stop=(n == 2 * TT - 1))
                mm.then_inc(S["tbl_done"], 1)

            pe.wait_ge(S["ctl_done"], 1)
            pe.nop().then_inc(S["dn_done"], 1)

            def e_turn(s, b):
                pe.wait_ge(S[f"gat{b}"], 8 * (s - b) + 16)
                for n in range(2):
                    if not early(s, 1):
                        pe.wait_ge(S["xgt_evac"], 2 * s - 1 + n)
                        pe.wait_ge(S["xgt_lo"], 2 * s - 1 + n)
                    for k in range(4):
                        mm = pe.transpose(pbig[:, 4 + n, k * P:(k + 1) * P], xg[b][:, (4 * n + k) * P:(4 * n + k + 1) * P], ident[:, :])
                    mm.then_inc(S["xgt_done"], 1)

            def e_up(s, b, off, e):
                pe.wait_ge(S["xgt_evac"], 2 * s + 2)
                if not early(s, 1):
                    pe.wait_ge(S["h_done"], s)
                pe.wait_ge(S["lo_split"], e * CUTS + UP_CUTS)
                pe.wait_ge(S["ctl_done"], 1)
                for k in range(KD):
                    w = ds(off + k * 2 * DE, 2 * DE)
                    pe.matmul(pbig[:, 6, :], xgH[b][:, k, :], WH[:, w], start=(k == 0), stop=False)
                    pe.matmul(pbig[:, 6, :], xgH[b][:, k, :], WL[:, w], start=False, stop=False)
                pe.wait_ge(S["xgt_lo"], 2 * s + 2)
                for k in range(KD):
                    mm = pe.matmul(pbig[:, 6, :], xgL[b][:, k, :], WH[:, ds(off + k * 2 * DE, 2 * DE)], start=False, stop=(k == KD - 1))
                mm.then_inc(S["gu_done"], 1)

            def e_hturn(s, b):
                pe.wait_ge(S["h_done"], s + 1)
                if not early(s, 1):
                    pe.wait_ge(S["ht_evac"], s)
                for k in range(2):
                    mm = pe.transpose(pbig[:, 7, k * P:(k + 1) * P], hh[b][:, k * P:(k + 1) * P], ident[:, :])
                mm.then_inc(S["ht_done"], 1)

            def e_down(s, b, off, e):
                pe.wait_ge(S["ht_evac"], s + 1)
                if not early(s, 1):
                    pe.wait_ge(S["dn_evac"], s)
                pe.wait_ge(S["lo_split"], e * CUTS + CUTS)
                pe.wait_ge(S["ctl_done"], 1)
                for n in range(2):
                    for k in range(2):
                        w = ds(off + (KD * 2 * DE + k * D + n * 512), 512)
                        pe.matmul(pbig[:, n, :], hTH[b][:, k, :], WH[:, w], start=(k == 0), stop=False)
                        pe.matmul(pbig[:, n, :], hTH[b][:, k, :], WL[:, w], start=False, stop=False)
                        mm = pe.matmul(pbig[:, n, :], hTL[b][:, k, :], WH[:, w], start=False, stop=(k == 1))
                mm.then_inc(S["dn_done"], 1)

            def words(s):
                return (pe.value_load(ctrl[0:1, ds(C_AT + s, 1)], min_val=0, max_val=EW),
                        pe.value_load(ctrl[0:1, ds(C_EXP + s, 1)], min_val=0, max_val=NE - 1))

            def e_step(s, b, before, last=False):
                now = words(s)
                if before:
                    e_hturn(s - 1, 1 - b)
                e_up(s, b, *now)
                if not last:
                    e_turn(s + 1, 1 - b)
                if before:
                    e_down(s - 1, 1 - b, *before)
                return now

            e_turn(0, 0)
            now = e_step(0, 0, None)
            e_step(1, 1, now)
            with pe.Fori(0, SLOTS // 4 - 1) as i:
                now = words(4 * i + 1)
                for n in range(2, 6):
                    now = e_step(4 * i + n, n % 2, now)
            now = e_step(SLOTS - 2, 0, words(SLOTS - 3))
            now = e_step(SLOTS - 1, 1, now, last=True)
            e_hturn(SLOTS - 1, 1)
            e_down(SLOTS - 1, 1, *now)

        @block.vector
        def _(dve):
            ch = Chain(dve, S["dch"])
            tt, ts, stt = dve.tensor_tensor, dve.tensor_scalar, dve.scalar_tensor_tensor
            dve.wait_ge(S["par_in"], 80)
            lr, li = PAR[:, 0, :], PAR[:, 1, :]
            dve.wait_ge(S["act_small"], 1)
            dt_, lrdt, ang, mag, mag8 = (sm[:, k, :] for k in range(5))
            ch(tt(lrdt, lr, dt_, ALU.mult))
            ch(tt(ang, li, dt_, ALU.mult))
            n_, r_, rh, sn, sh, cs, t_ = sm[:, 5, :], sm[:, 6, :], sm[:, 7, :], sm[:, 8, :], sm[:, 9, :], sm[:, 10, :], sm[:, 11, :]
            ch(ts(n_, ang, INV_2PI, ROUND, ALU.mult, ALU.add))
            ch(ts(n_, n_, ROUND, None, ALU.subtract))
            ch(stt(r_, n_, -PI_HI, ang, ALU.mult, ALU.add))
            ch(stt(r_, n_, -PI_MID, r_, ALU.mult, ALU.add))
            ch(stt(r_, n_, -PI_LO, r_, ALU.mult, ALU.add))
            ch(ts(r_, r_, PI_IN, -PI_IN, ALU.min, ALU.max))
            ch(ts(rh, r_, 0.5, None, ALU.mult))
            dve.memset(t_, 0.0).then_inc(S["c_g1"], 1)
            dve.wait_ge(S["win_in"], 16)
            for k in range(KD):
                ts(w1[:, k, :], w1[:, k, :], gm_sb[:, k:k + 1], None, ALU.mult).then_inc(S["w_scaled"], 1)
            dve.wait_ge(S["act_small"], 5)
            ch(tt(t_, sh, sh, ALU.mult))
            ch(ts(cs, t_, -2.0, 1.0, ALU.mult, ALU.add))

            def cmul(ore, oim, are, aim, bre, bim, ta, tb):
                ch(tt(ta, are, bre, ALU.mult))
                ch(tt(tb, aim, bim, ALU.mult))
                ch(tt(ore, ta, tb, ALU.subtract))
                ch(tt(ta, are, bim, ALU.mult))
                ch(tt(tb, aim, bre, ALU.mult))
                ch(tt(oim, ta, tb, ALU.add))

            def unit(re, im, ore, oim):
                ta, tb = tq[:, 2, 0:PR], tq[:, 3, 0:PR]
                ch(tt(ta, re, re, ALU.mult))
                ch(tt(tb, im, im, ALU.mult))
                ch(tt(ta, ta, tb, ALU.add))
                ch(ts(ta, ta, -0.5, 1.5, ALU.mult, ALU.add))
                ch(tt(ore, re, ta, ALU.mult))
                ch(tt(oim, im, ta, ALU.mult))

            q0, q1 = tq[:, 0, 0:PR], tq[:, 1, 0:PR]
            ch(dve.memset(PW[:, 0, 0, :], 1.0))
            ch(dve.memset(PW[:, 1, 0, :], 0.0))
            ch(tt(PW[:, 0, 1, :], mag, cs, ALU.mult))
            ch(tt(PW[:, 1, 1, :], mag, sn, ALU.mult))
            for lo in (1, 2, 4):
                def bc(a):
                    return PW[:, a, lo:lo + 1, :].to_broadcast([P, lo, PR])
                v0 = tq[:, 0, 0:lo * PR].rearrange("p (d r) -> p d r", r=PR)
                v1 = tq[:, 1, 0:lo * PR].rearrange("p (d r) -> p d r", r=PR)
                cmul(PW[:, 0, lo + 1:2 * lo + 1, :], PW[:, 1, lo + 1:2 * lo + 1, :], PW[:, 0, 1:lo + 1, :], PW[:, 1, 1:lo + 1, :],
                     bc(0), bc(1), v0, v1)
            ch(ts(PW[:, 2, :, :], PW[:, 1, :, :], -1.0, None, ALU.mult))
            den, nr, cr, ci = sm[:, 12, :], sm[:, 13, :], sm[:, 14, :], sm[:, 15, :]
            ch(tt(q0, lr, lr, ALU.mult))
            ch(tt(q1, li, li, ALU.mult))
            ch(tt(q0, q0, q1, ALU.add))
            ch(dve.reciprocal(den, q0))
            ch(ts(nr, PW[:, 0, 1, :], -1.0, None, ALU.add))
            ch(tt(q0, nr, lr, ALU.mult))
            ch(tt(q1, PW[:, 1, 1, :], li, ALU.mult))
            ch(tt(q0, q0, q1, ALU.add))
            ch(tt(cr, q0, den, ALU.mult))
            ch(tt(q0, PW[:, 1, 1, :], lr, ALU.mult))
            ch(tt(q1, nr, li, ALU.mult))
            ch(tt(q0, q0, q1, ALU.subtract))
            ch(tt(ci, q0, den, ALU.mult))
            crb, cib = cr.unsqueeze(2).to_broadcast([P, PR, GC]), ci.unsqueeze(2).to_broadcast([P, PR, GC])
            bt0 = uT[0][:, 0, 0:PR * GC].rearrange("p (r c) -> p r c", c=GC)
            bt1 = uT[0][:, 1, 0:PR * GC].rearrange("p (r c) -> p r c", c=GC)
            cmul(BB[:, 0, :, :], BB[:, 1, :, :], BC[:, 0, :, :], BC[:, 1, :, :], crb, cib, bt0, bt1)
            ure, uim, vre, vim = (sm[:, k, :] for k in range(16, 20))
            unit(cs, sn, ure, uim)
            for k in range(3 + 7):
                cmul(vre, vim, ure, uim, ure, uim, q0, q1)
                unit(vre, vim, ure, uim)
                if k >= 2:
                    ch(dve.tensor_copy(PH[:, 0, k - 2, :], ure))
                    ch(dve.tensor_copy(PH[:, 1, k - 2, :], uim))
            dve.memset(t_, 0.0).then_inc(S["pws_ready"], 1)

            for j in range(L):
                b = j % 2
                dve.wait_ge(S["sq_done"], j + 1)
                dve.tensor_reduce(red[b][:, :], sq[:, :, :].rearrange("p k n -> p n k"), AX, ALU.add).then_inc(S["red_done"], 1)
                dve.wait_ge(S["ss_done"], j + 1)
                ts(rst[b][:, :], pbig[:, 4 + b, 0:NCH], 1.0 / D, EPS, ALU.mult, ALU.add).then_inc(S["var_done"], 1)
                dve.wait_ge(S["std_done"], j + 1)
                ch(dve.reciprocal(rst[b][:, :], std[b][:, :]))
                if j >= 2:
                    dve.wait_ge(S["u_stored"], 16 * (j - 1))
                for cb in range(CB):
                    dve.wait_ge(S["um_done"], CB * j + cb + 1)
                    tt(uT[b][:, cb, :], pbig[:, cb, 0:NCH], rst[b][:, :], ALU.mult).then_inc(S["u_evac"], 1)

            dve.wait_ge(S["tabs_ready"], 1)
            dve.wait_ge(S["u_stored"], 16 * L)
            dve.wait_ge(S["um_done"], CB * L)
            dve.wait_ge(S["mz_zero"], 4)
            NB = 12

            def b_scan(r, b):
                at = [0]

                def lk(ins, n=1):
                    at[0] += 1
                    ins.then_inc(S["dchb"], 1)
                    dve.wait_ge(S["dchb"], NB * r + at[0])
                dve.wait_ge(S["v_done"], r + 1)
                if not early(r):
                    dve.wait_ge(S["y_done"], 2 * r - 2)
                v = pbig[:, 2 * b:2 * b + 2, DECB:NCH]
                wc = WT[:, 0:1, ds(r, 1), :].rearrange("p a o k -> p a (o k)").to_broadcast([P, 2, NP_CH])
                ws = WT[:, 1:2, ds(r, 1), :].rearrange("p a o k -> p a (o k)").to_broadcast([P, 2, NP_CH])
                lk(tt(r1[:, :, :], v, wc, ALU.mult))
                lk(tt(r2[:, :, :], v, ws, ALU.mult))
                lk(tt(z[:, 0, :], r1[:, 0, :], r2[:, 1, :], ALU.add))
                lk(tt(z[:, 1, :], r1[:, 1, :], r2[:, 0, :], ALU.subtract))
                mg = mag8[:, ds(r, 1)].to_broadcast([P, NP_CH])
                lk(dve.tensor_tensor_scan(r1[:, 0, :], mg, z[:, 0, :], 0.0, ALU.mult, ALU.add))
                lk(dve.tensor_tensor_scan(r1[:, 1, :], mg, z[:, 1, :], 0.0, ALU.mult, ALU.add))
                lk(tt(z[:, :, :], r1[:, :, :], wc, ALU.mult))
                lk(tt(r2[:, :, :], r1[:, :, :], ws, ALU.mult))
                lk(tt(Sp[b][:, 0, DECB + 1:NCH + 1], z[:, 0, :], r2[:, 1, :], ALU.subtract))
                lk(tt(Sp[b][:, 1, DECB + 1:NCH + 1], z[:, 1, :], r2[:, 0, :], ALU.add))
                dve.nop().then_inc(S["sp_done"], 1)
                lk(tt(FO[:, :, ds(r, 1), 0:DECB].rearrange("p a o k -> p a (o k)"), pbig[:, 2 * b:2 * b + 2, 0:DECB],
                      F0[:, :, ds(r, 1), :].rearrange("p a o k -> p a (o k)"), ALU.add))
                lk(dve.tensor_copy(FO[:, :, ds(r, 1), DECB:DECB + 1].rearrange("p a o k -> p a (o k)"), Sp[b][:, :, NCH:NCH + 1]))
                dve.nop().then_inc(S["fo_done"], 1)

            def b_y(r):
                for g in range(2):
                    dve.wait_ge(S["y_done"], 2 * r + g + 1)
                    if not early(r, 1):
                        dve.wait_ge(S["gelu_done"], 2 * r - 1 + g)
                    stt(yt[g][:, :], U[:, ds(2 * r + g, 1), :].rearrange("p o k -> p (o k)"), d_sb[:, ds(2 * r + g, 1)],
                        pbig[:, 5 + g, 0:NCH], ALU.mult, ALU.add).then_inc(S["yp_done"], 1)

            b_scan(0, 0)
            b_scan(1, 1)
            b_y(0)
            with dve.Fori(1, PR // 2) as i:
                b_scan(2 * i, 0)
                b_y(2 * i - 1)
                b_scan(2 * i + 1, 1)
                b_y(2 * i)
            b_y(PR - 1)

            dve.wait_ge(S["con_in"], 48)
            dve.wait_ge(S["gelu_done"], G)
            dve.wait_ge(S["st_stored"], 16)
            NC = 12

            def c_mix(t, b, rows=P):
                at = [0]

                def lk(ins):
                    at[0] += 1
                    ins.then_inc(S["dchc"], 1)
                    dve.wait_ge(S["dchc"], NC * t + at[0])
                dve.wait_ge(S[f"xr_in{b}"], 8 * (t - b) + 16)
                if not early(t):
                    dve.wait_ge(S[f"x2_st{b}"], 8 * (t - b))
                    dve.wait_ge(S[f"xn_st{b}"], 8 * (t - b))
                dve.wait_ge(S["sig_done"], 2 * t + 2)
                dve.wait_ge(S["a_done"], 4 * t + 4)
                lk(tt(x2[b][0:rows, :].rearrange("p (a m) -> p a m", a=2), pbig[0:rows, 0:2, :],
                      sg[0:rows, :].rearrange("p (a m) -> p a m", a=2), ALU.mult))
                lk(tt(x2[b][0:rows, :], x2[b][0:rows, :], xr[b][0:rows, :], ALU.add))
                dve.nop().then_inc(S["x2_done"], 1)
                dve.wait_ge(S["ssq_done"], t + 1)
                mean, y_, h_, t2 = nv[0:rows, 0:1], nv[0:rows, 1:2], nv[0:rows, 2:3], nv[0:rows, 3:4]
                lk(ts(mean, ssq[0:rows, ds(t, 1)], 1.0 / D, EPS, ALU.mult, ALU.add))
                lk(ts(nvi[0:rows, 0:1], mean.bitcast(I32), 1, None, ALU.logical_shift_right))
                lk(ts(nvi[0:rows, 1:2], nvi[0:rows, 0:1], -1.0, RSQRT_SEED, ALU.mult, ALU.add))
                lk(ts(h_, mean, -0.5, None, ALU.mult))
                yy = nvi[0:rows, 1:2].bitcast(F32)
                for k in range(3):
                    lk(stt(t2, yy, h_, yy, ALU.mult, ALU.mult))
                    lk(stt(y_, t2, 1.5, yy, ALU.add, ALU.mult))
                    yy = y_
                stt(xn[b][0:rows, :], x2[b][0:rows, :], y_, gf_b[0:rows, :], ALU.mult, ALU.mult).then_inc(S["xn_done"], 1)
            steps(dve, TF, c_mix)
            c_mix(TF, 0, LAST)

            dch = Chain(dve, S["dchd"])
            dve.wait_ge(S["d_iota"], 3)
            n3 = [P, TT, 4]

            def b4(ap):
                return ap.unsqueeze(2).to_broadcast(n3)

            def first_max(oh, src, mx, ta):
                dch(dve.tensor_reduce(mx, src, AX, ALU.max))
                dch(tt(ta, src, b4(mx), ALU.is_equal))
                dch(tt(ta, ta, desc[:, :].unsqueeze(1).to_broadcast(n3), ALU.mult))
                dch(dve.tensor_reduce(R1[11][:, :], ta, AX, ALU.max))
                dch(tt(oh, ta, b4(R1[11][:, :]), ALU.is_equal))

            dch(dve.memset(logit[LAST:P, TF, :], 0.0))
            lg = logit[:, :, 0:NG]
            ohg, oh1, oh2 = R3[2][:, :, :], R3[3][:, :, :], R3[4][:, :, :]
            gm = R1[0][:, :]
            first_max(ohg, lg, gm, R3[5][:, :, :])
            dch(tt(R3[0][:, :, :], lg, b4(gm), ALU.subtract))
            dve.nop().then_inc(S["exp_in"], 1)
            for g in range(NG):
                dch(tt(L4[:, :, g, :], logit[:, :, NG + g * NEG:NG + (g + 1) * NEG], ohg[:, :, g:g + 1].to_broadcast(n3), ALU.mult))
            le = R3[6][:, :, :]
            dch(dve.tensor_reduce(le, L4[:, :, :, :].rearrange("p t g e -> p t e g"), AX, ALU.add))
            m1, m2 = R1[1][:, :], R1[2][:, :]
            first_max(oh1, le, m1, R3[5][:, :, :])
            dch(stt(R3[7][:, :, :], oh1, -1e30, le, ALU.mult, ALU.add))
            first_max(oh2, R3[7][:, :, :], m2, R3[5][:, :, :])
            dch(tt(R1[4][:, :], m2, m1, ALU.subtract))
            dve.nop().then_inc(S["exp_in"], 1)
            dve.wait_ge(S["exp_d"], 2)
            sg_, gw, w1_ = R1[3][:, :], R1[6][:, :], R1[7][:, :]
            dch(dve.tensor_reduce(sg_, R3[1][:, :, :], AX, ALU.add))
            dch(ts(w1_, R1[5][:, :], 1.0, None, ALU.add))
            dch(tt(gw, sg_, w1_, ALU.mult))
            dch(dve.reciprocal(cw[:, 0, :], gw))
            dch(tt(cw[:, 1, :], cw[:, 0, :], R1[5][:, :], ALU.mult))
            for EX, oh in ((E1, oh1), (E2, oh2)):
                for g in range(NG):
                    dch(tt(EX[:, :, g, :], oh, ohg[:, :, g:g + 1].to_broadcast(n3), ALU.mult))
                dch(dve.memset(EX[LAST:P, TF, :, :], 0.0))
            dch(tt(EE[:, :, :, :], E1[:, :, :, :], E2[:, :, :, :], ALU.add))
            dve.nop().then_inc(S["d_ready"], 1)
            dch(dve.memset(rst_t[:, :, :], 1.0))
            dch(dve.memset(rst_t[:, :, 0:1], 0.0))
            dve.wait_ge(S["cnt_done"], 1)
            dch(dve.tensor_copy(cnt[:, :, :], pbig[:, 1, 0:TT * NE].rearrange("p (t e) -> p e t", e=NE)))
            flat = lambda a: a[:, :, :].rearrange("p e t -> p (e t)")
            dch(dve.tensor_tensor_scan(flat(inc_t), flat(rst_t), flat(cnt), 0.0, ALU.mult, ALU.add))
            dch(tt(exc_t[:, :, :], inc_t[:, :, :], cnt[:, :, :], ALU.subtract))
            ne, nti, ntf, cum, bas = tei[:, 0, :], tei[:, 1, :], te[:, 1, :], te[:, 2, :], te[:, 3, :]
            dch(ts(ne, inc_t[:, :, TT - 1], float(P - 1), None, ALU.add))
            dch(ts(nti, ne, 7, None, ALU.logical_shift_right))
            dch(ts(ntf, nti, 1.0, None, ALU.max))
            dch(dve.memset(te[:, 0, :], 1.0))
            dch(dve.tensor_tensor_scan(cum, te[:, 0, :], ntf, 0.0, ALU.mult, ALU.add))
            beg = te[:, 4, :]
            dch(tt(beg, cum, ntf, ALU.subtract))
            dch(ts(bas, beg, float(P), 1.0, ALU.mult, ALU.add))
            dch(tt(exc_t[:, :, :], exc_t[:, :, :], bas.unsqueeze(2).to_broadcast([P, NE, TT]), ALU.add))
            dch(tt(spos[:, :, :], pbig[:, 0, 0:TT * NE].rearrange("p (t e) -> p t e", e=NE), exc_t[:, :, :].rearrange("p e t -> p t e"), ALU.add))
            for c, EX in enumerate((E1, E2)):
                ef = EX[:, :, :, :].rearrange("p t g e -> p t (g e)")
                dch(tt(ef, ef, spos[:, :, :], ALU.mult))
                dch(dve.tensor_reduce(R1[8 + c][:, :], ef, AX, ALU.add))
                dch(ts(slot_i[:, c, :], R1[8 + c][:, :], -1.0, None, ALU.add))
                dch(ts(si[:, c, 0, :], slot_i[:, c, :], 7, None, ALU.arith_shift_right))
                dch(ts(si[:, c, 1, :], slot_i[:, c, :], P - 1, None, ALU.bitwise_and))
            dch(dve.tensor_copy(sf[:, :, :, :], si[:, :, :, :]))
            for n in range(2 * TT):
                c, t = n % 2, n // 2
                if n >= 4:
                    dve.wait_ge(S["tbl_done"], n - 3)
                dch(ts(oh_lo[n % 4][:, :], iot[:, :], sf[:, c, 1, t:t + 1], None, ALU.is_equal))
                ts(oh_hi[n % 4][:, :], iot[:, 0:SLOTS], sf[:, c, 0, t:t + 1], tokid[:, t:t + 1], ALU.is_equal, ALU.mult).then_inc(S["one_hot_done"], 1)
            dch(tt(cmpe[:, :, :], cum[0:1, :].unsqueeze(1).to_broadcast([1, SLOTS, NE]), iot[0:1, 0:SLOTS].unsqueeze(2).to_broadcast([1, SLOTS, NE]), ALU.is_le))
            e_ = eof[:, 0, :]
            dch(dve.tensor_reduce(e_, cmpe[:, :, :], AX, ALU.add))
            dch(ts(e_, e_, float(NE - 1), None, ALU.min))
            def word(c):
                return ctrl[:, c:c + SLOTS]
            dch(dve.tensor_copy(word(C_EXP), e_))
            dch(ts(word(C_AT), word(C_EXP), 1, None, ALU.bitwise_and))
            f_, n_ = eof[:, 1, :], eof[:, 2, :]
            dch(tt(cmpe[:, :, :], beg[0:1, :].unsqueeze(1).to_broadcast([1, SLOTS, NE]), iot[0:1, 0:SLOTS].unsqueeze(2).to_broadcast([1, SLOTS, NE]), ALU.is_equal))
            dch(dve.tensor_reduce(f_, cmpe[:, :, 0:NE - 1], AX, ALU.add))
            dch(ts(n_, word(C_AT), -float(EW), float(EW - SKIP), ALU.mult, ALU.add))
            dch(tt(n_, n_, f_, ALU.mult))
            dch(ts(word(C_NEXT), n_, float(SKIP), None, ALU.add))
            dch(ts(word(C_AT), word(C_AT), float(EW), None, ALU.mult))
            dve.wait_ge(S["tbl_done"], 2 * TT)
            dch(dve.tensor_copy(token_of[:, :], pbig[:, 2, 0:SLOTS]))
            dve.nop().then_inc(S["ctl_done"], 1)

            def e_x_lo(s, b):
                for n in range(2):
                    dve.wait_ge(S["xgt_evac"], 2 * s + n + 1)
                    if n == 0 and not early(s):
                        dve.wait_ge(S["gu_done"], s - 1)
                    tt(xgL[b][:, 4 * n:4 * n + 4, :], pbig[:, 4 + n, :].rearrange("p (a m) -> p a m", a=4),
                       xgH[b][:, 4 * n:4 * n + 4, :].bitcast(F32), ALU.subtract).then_inc(S["xgt_lo"], 1)

            def e_h(s, b):
                dve.wait_ge(S["sl_done"], s + 1)
                if not early(s):
                    dve.wait_ge(S["ht_done"], s - 1)
                tt(hh[b][:, :], sl[:, :], pbig[:, 6, DE:2 * DE], ALU.mult).then_inc(S["h_done"], 1)

            def e_ht(s, b):
                dve.wait_ge(S["ht_done"], s + 1)
                if not early(s):
                    dve.wait_ge(S["dn_done"], s)
                ht = pbig[:, 7, 0:2 * P].rearrange("p (a m) -> p a m", a=2)
                dve.tensor_copy(hTH[b][:, :, :], ht).then_inc(S["dche"], 1)
                dve.wait_ge(S["dche"], s + 1)
                tt(hTL[b][:, :, :], ht, hTH[b][:, :, :].bitcast(F32), ALU.subtract).then_inc(S["ht_evac"], 1)

            def e_word(s):
                return dve.value_load(ctrl[0:1, ds(C_NEXT + s, 1)], min_val=0, max_val=EW)

            def e_split(s, to, part):
                with dve.If(to != SKIP):
                    e = dve.value_load(ctrl[0:1, ds(C_EXP + s, 1)], min_val=0, max_val=NE - 1)
                    for c in (range(UP_CUTS), range(UP_CUTS, CUTS))[part]:
                        dve.wait_ge(S["hi_split"], e * CUTS + (CUTS + c + 1))
                        dve.wait_ge(S["ctl_done"], 1)
                        w = ds(to + c * CW, CW)
                        tt(WL[:, w], WR[:, w], WH[:, w].bitcast(F32), ALU.subtract).then_inc(S["lo_split"], 1)

            for c in range(CUTS):
                dve.wait_ge(S["hi_split"], c + 1)
                w = ds(c * CW, CW)
                tt(WL[:, w], WR[:, w], WH[:, w].bitcast(F32), ALU.subtract).then_inc(S["lo_split"], 1)
            e_x_lo(0, 0)

            def e_step(s, b, to, ahead=True, last=False):
                then = None
                if not last:
                    e_split(s, to, 0)
                e_h(s, b)
                if not last:
                    e_x_lo(s + 1, 1 - b)
                    if ahead:
                        then = e_word(s + 1)
                e_ht(s, b)
                if not last:
                    e_split(s, to, 1)
                return then

            to = e_step(0, 0, e_word(0))
            e_step(1, 1, to, ahead=False)
            with dve.Fori(0, SLOTS // 4 - 1) as i:
                to = e_word(4 * i + 2)
                for n in range(2, 6):
                    to = e_step(4 * i + n, n % 2, to, ahead=n < 5)
            e_step(SLOTS - 2, 0, e_word(SLOTS - 2), ahead=False)
            e_step(SLOTS - 1, 1, None, last=True)

            NF = 2

            def f_step(t, b, rows=P):
                at = [0]

                def lk(ins):
                    at[0] += 1
                    ins.then_inc(S["dchf"], 1)
                    dve.wait_ge(S["dchf"], NF * t + at[0])
                dve.wait_ge(S[f"fx_in{b}"], 8 * (t - b) + 16)
                dve.wait_ge(S[f"f_in{b}"], 16 * (t - b) + 32)
                x = fx[b][0:rows, :]
                lk(stt(x, f1[b][0:rows, :], cw[0:rows, 0, ds(t, 1)], x, ALU.mult, ALU.add))
                if not early(t):
                    dve.wait_ge(S[f"f_st{b}"], 8 * (t - b))
                stt(x, f2[b][0:rows, :], cw[0:rows, 1, ds(t, 1)], x, ALU.mult, ALU.add).then_inc(S["f_sum"], 1)
                dve.wait_ge(S["f_sq"], t + 1)
                ts(fnv[0:rows, b, 0:1], fss[0:rows, ds(t, 1)], 1.0 / D, EPS, ALU.mult, ALU.add).then_inc(S["f_rs"], 1)
                dve.wait_ge(S["f_std"], t + 1)
                lk(dve.reciprocal(fnv[0:rows, b, 2:3], fnv[0:rows, b, 1:2]))
                stt(fo[b][0:rows, :], x, fnv[0:rows, b, 2:3], gl_b[0:rows, :], ALU.mult, ALU.mult).then_inc(S["f_out"], 1)
            steps(dve, TF, f_step)
            f_step(TF, 0, LAST)


def kernel(**inputs):
    import numpy as np
    import concourse.bacc as bacc
    from concourse.bass_utils import run_bass_kernel_spmd as run

    a = {k: np.asarray(v) for k, v in inputs.items()}

    def order(p, s):
        rows = np.concatenate([s.reshape(NCH - NP_CH, L, -1), p.reshape(NP_CH, L, -1)], 0)
        return np.ascontiguousarray(rows.transpose(1, 0, 2))

    def states(x):
        x = x.reshape(x.shape[:-2] + (PR, 2, ST))
        x = np.moveaxis(x, (-2, -1, -3), (0, 1, 2))
        x = x.reshape((P, PR) + x.shape[3:])
        return x

    x = order(a["x_prompt"], a["x_sample"])
    x_rows = x.reshape(NT, D)
    x_cols = x.reshape(L, NCH, KD, P).transpose(0, 3, 2, 1)
    s0 = np.stack([states(a["state_ssm_re"]), states(a["state_ssm_im"])], 1)
    step = np.broadcast_to(a["ssm_log_step"][:, None], (G, ST))
    par = np.stack([states(v) for v in (a["ssm_lambda_re"], a["ssm_lambda_im"], step)], 1)

    def chans(v):
        return v.reshape(PR, 2, ST, GC).transpose(1, 2, 0, 3).reshape(P, PR, GC)

    bc = np.stack([chans(a["ssm_b_re"]), chans(a["ssm_b_im"]),
                   chans(a["ssm_c_re"].transpose(0, 2, 1)), chans(a["ssm_c_im"].transpose(0, 2, 1))], 1)
    dd = np.broadcast_to(a["ssm_d"].T[None], (L, GC, G)).reshape(P, G)
    route = np.concatenate([a["moe_router_group"][0], a["moe_router_expert"][0]], 1)
    gu = np.stack([a["moe_w_gate"][0], a["moe_w_up"][0]], 2)
    arrays = {
        "x_rows": x_rows, "x_cols": x_cols, "s0": s0, "par": par, "bc": bc, "dd": dd,
        "gmix": a["norm_mix"][0].reshape(KD, P).T, "gffn": a["norm_ffn"][0], "gfin": a["norm_final"],
        "w_in": a["ssm_w_in"].reshape(KD, P, W).transpose(1, 0, 2),
        "w_out": a["ssm_w_out"].reshape(CB, P, 2 * D).transpose(1, 0, 2),
        "route": route.reshape(KD, P, 20).transpose(1, 0, 2),
        "w_gu": gu.reshape(NE, KD, P, 2 * DE).transpose(0, 2, 1, 3).reshape(NE, P, KD * 2 * DE),
        "w_dn": a["moe_w_down"][0].reshape(NE, DE // P, P, D).transpose(0, 2, 1, 3).reshape(NE, P, DE // P * D),
    }
    arrays = {k: np.ascontiguousarray(v) for k, v in arrays.items()}
    nc = bacc.Bacc("TRN2", target_bir_lowering=False, num_devices=1)
    ins = {k: nc.dram_tensor(f"in_{k}", v.shape, mybir.dt.from_np(v.dtype), kind="ExternalInput").ap()
           for k, v in arrays.items()}
    y_out = nc.dram_tensor("out_y", (NT, D), F32, kind="ExternalOutput").ap()
    st_out = nc.dram_tensor("out_st", (P, 2, PR, DECB + 1), F32, kind="ExternalOutput").ap()
    hybrid_kernel(nc, ins["x_rows"], ins["x_cols"], ins["s0"], ins["par"], ins["bc"], None, ins["dd"], ins["gmix"],
                  ins["gffn"], ins["gfin"], ins["w_in"], ins["w_out"], ins["route"], ins["w_gu"], ins["w_dn"], y_out, st_out)
    r = run(nc, [{f"in_{k}": v for k, v in arrays.items()}], core_ids=[0])
    y = np.asarray(r.results[0]["out_y"]).reshape(L, NCH, D).transpose(1, 0, 2)
    st = np.asarray(r.results[0]["out_st"]).reshape(2, ST, 2, PR, DECB + 1)
    st = st.transpose(2, 4, 3, 0, 1).reshape(2, DECB + 1, G, ST)
    c = np.ascontiguousarray
    return (c(y[DECB:].reshape(1, SEQ, D)), c(y[:DECB].reshape(DECB, DECS, D)),
            c(st[0, DECB:]), c(st[1, DECB:]), c(st[0, :DECB]), c(st[1, :DECB]), None)
```

```python
from contextlib import ExitStack

import concourse.bass as bass
from concourse import mybir

F32 = mybir.dt.float32
I32 = mybir.dt.int32
U32 = mybir.dt.uint32
F32R = mybir.dt.float32r
ALU = mybir.AluOpType
ACT = mybir.ActivationFunctionType
AX = mybir.AxisListType.X
ds = bass.ds

P = 128
D = 1024
SEQ, DECB, DECS = 2048, 8, 8
L = 8
NCH = DECB + SEQ // L
NP_CH = SEQ // L
NT = NCH * L
KD = D // P
W = 512
G, GC, ST = 32, 16, 64
PR = G // 2
CB = W // P
TT = -(-NT // P)
TF = NT // P
LAST = NT - TF * P
NG, NEG, NE = 4, 4, 16
DE = 256
SLOTS = (2 * NT + NE * (P - 1)) // P
EPS = 1e-6
INV_2PI = 0.15915494309189535
ROUND = 12582912.0
PI_HI, PI_MID, PI_LO = 6.28125, 0.0019350051879882812, 3.0199159819e-07
PI_IN = 3.1415925
RSQRT_SEED = 1597463007.0
EW = KD * 2 * DE + (DE // P) * D
CUTS, UP_CUTS = 3, 2
CW = EW // CUTS
FULL = 2 * NT // P
C_EXP, C_AT, C_NEXT = (i * SLOTS for i in range(3))
SKIP = 1
NF = 4


def hybrid_kernel(nc, x_rows, x_cols, s0, par, b_in, c_in, d_in, gmix, gffn, gfin, w_in, w_out, w_route,
                  w_gu, w_dn, y_out, st_out):
    uD = nc.dram_tensor("u_by_step", (L, P, CB, NCH), F32, kind="Internal").ap()
    yD = nc.dram_tensor("y_by_block", (CB, P, 8, NCH), F32, kind="Internal").ap()
    x2D = nc.dram_tensor("x_sums", (NT + P, D), F32, kind="Internal").ap()
    xnD = nc.dram_tensor("x_normed", (NT, D), F32, kind="Internal").ap()

    outer = ExitStack()
    with outer:
        scope = [outer]

        def sb(name, shape, dt=F32):
            return scope[0].enter_context(nc.sbuf_tensor(name, shape, dt))

        def sem(name):
            return outer.enter_context(nc.semaphore(name))

        def cut(ap, n):
            return ap[0:n]

        pbig = outer.enter_context(nc.psum_tensor("pbig", [P, 8, 512], F32))

        ident = sb("ident", [P, P])
        ones = sb("ones", [P, P])
        upper = sb("upper", [P, P])
        gf_b = sb("gf_b", [P, D])
        gl_b = sb("gl_b", [P, D])
        wr_sb = sb("wr_sb", [P, KD, 20])
        logit = sb("logit", [P, TT, 20])
        token_of = sb("token_of", [P, SLOTS], U32)
        sum_of = sb("sum_of", [P, SLOTS], U32)
        cw_of = sb("cw_of", [P, SLOTS])
        ctrl = sb("ctrl", [1, 3 * SLOTS], I32)
        epsc = sb("epsc", [P, 1])

        umix = ExitStack()
        scope[0] = umix
        U = sb("U", [P, G, NCH])
        FO = sb("FO", [P, 2, PR, DECB + 1])
        mix = ExitStack()
        scope[0] = mix
        PAR = sb("PAR", [P, 3, PR])
        s0_sb = sb("s0_sb", [P, 2, PR, DECB])
        BC = sb("BC", [P, 4, PR, GC])
        d_sb = sb("d_sb", [P, G])
        gm_sb = sb("gm_sb", [P, KD])
        sm = sb("sm", [P, 24, PR])
        PW = sb("PW", [P, 3, L + 1, PR])
        PH = sb("PH", [P, 2, 8, PR])
        tq = sb("tq", [P, 4, PR * 4])
        BB = sb("BB", [P, 2, PR, GC])
        WT = sb("WT", [P, 2, PR, NP_CH])
        E = sb("E", [P, 2, PR, L * GC])
        CL = sb("CL", [P, 2, PR, (L + 1) * GC])
        T = sb("T", [P, G, L * GC])
        F0 = sb("F0", [P, 2, PR, DECB])
        aonly = ExitStack()
        scope[0] = aonly
        xT = [sb(f"xT{b}", [P, KD, NCH]) for b in range(2)]
        sq = sb("sq", [P, KD, NCH])
        red = [sb(f"red{b}", [P, NCH]) for b in range(2)]
        std = [sb(f"std{b}", [P, NCH]) for b in range(2)]
        rst = [sb(f"rst{b}", [P, NCH]) for b in range(2)]
        uT = [sb(f"uT{b}", [P, CB, NCH]) for b in range(2)]
        w1 = sb("w1", [P, KD, W])
        p1 = sb("p1", [P, (L + 1) * PR * GC])
        p2 = p1
        aonly.close()
        bonly = ExitStack()
        scope[0] = bonly
        Kst = sb("Kst", [GC, G, L * GC])
        ES = [sb(f"ES{b}", [P, 2, P]) for b in range(2)]
        NS = [sb(f"NS{b}", [P, 2, P]) for b in range(2)]
        TS = [sb(f"TS{b}", [P, 2, P]) for b in range(2)]
        MZ = [sb(f"MZ{b}", [P, 2, 2, P]) for b in range(2)]
        Sp = [sb(f"Sp{b}", [P, 2, NCH + 1]) for b in range(2)]
        r1 = sb("r1", [P, 2, NP_CH])
        r2 = sb("r2", [P, 2, NP_CH])
        z = sb("z", [P, 2, NP_CH])
        yt = [sb(f"yt{b}", [P, NCH]) for b in range(2)]
        w2a = sb("w2a", [P, CB - 1, 2 * D])
        bonly.close()
        mix.close()

        cst = ExitStack()
        scope[0] = cst
        w2b = sb("w2b", [P, 1, 2 * D])
        w2H = sb("w2H", [P, CB, 2 * D], F32R)
        w2L = sb("w2L", [P, CB, 2 * D], F32R)
        ysH = [sb(f"ysH{b}", [P, CB, P], F32R) for b in range(2)]
        ysL = [sb(f"ysL{b}", [P, CB, P], F32R) for b in range(2)]
        ys = [sb(f"ys{b}", [P, CB, P]) for b in range(2)]
        xr = [sb(f"xr{b}", [P, D]) for b in range(2)]
        sg = sb("sg", [P, D])
        x2 = [sb(f"x2{b}", [P, D]) for b in range(2)]
        xn = [sb(f"xn{b}", [P, D]) for b in range(2)]
        junk = sb("junk", [P, D])
        xnT = sb("xnT", [P, KD, P])
        ssq = sb("ssq", [P, TT])
        nv = sb("nv", [P, 8])
        nvi = sb("nvi", [P, 2], I32)
        cst.close()
        umix.close()

        dst = ExitStack()
        scope[0] = dst
        R3 = [sb(f"R3{i}", [P, TT, 4]) for i in range(10)]
        R1 = [sb(f"R1{i}", [P, TT]) for i in range(12)]
        L4 = sb("L4", [P, TT, NG, NEG])
        E1 = sb("E1", [P, TT, NG, NEG])
        E2 = sb("E2", [P, TT, NG, NEG])
        EE = sb("EE", [P, TT, NG, NEG])
        cnt = sb("cnt", [P, NE, TT])
        inc_t = sb("inc_t", [P, NE, TT])
        exc_t = sb("exc_t", [P, NE, TT])
        rst_t = sb("rst_t", [P, NE, TT])
        spos = sb("spos", [P, TT, NE])
        te = sb("te", [P, 6, NE])
        tei = sb("tei", [P, 2, NE], I32)
        desc = sb("desc", [P, 4])
        iot = sb("iot", [P, P])
        tokid = sb("tokid", [P, TT])
        si = sb("si", [P, 2, 2, TT], I32)
        sf = sb("sf", [P, 2, 2, TT])
        oh_lo = [sb(f"oh_lo{b}", [P, P]) for b in range(4)]
        oh_hi = [sb(f"oh_hi{b}", [P, 2, SLOTS]) for b in range(4)]
        cw = sb("cw", [P, 2, TT])
        slot_i = sb("slot_i", [P, 2, TT], I32)
        vals = sb("vals", [P, 2, TT, 2])
        spare = sb("spare", [P, 1])
        rowf = sb("rowf", [P, 2, SLOTS])
        cmpe = sb("cmpe", [1, SLOTS, NE])
        eof = sb("eof", [1, 6, SLOTS])
        dst.close()

        est = ExitStack()
        scope[0] = est
        xg = [sb(f"xg{b}", [P, D]) for b in range(2)]
        xgH = [sb(f"xgH{b}", [P, KD, P], F32R) for b in range(2)]
        xgL = [sb(f"xgL{b}", [P, KD, P], F32R) for b in range(2)]
        sl = sb("sl", [P, DE])
        hh = [sb(f"hh{b}", [P, DE]) for b in range(2)]
        hTH = [sb(f"hTH{b}", [P, 2, P], F32R) for b in range(2)]
        hTL = [sb(f"hTL{b}", [P, 2, P], F32R) for b in range(2)]
        yo = [sb(f"yo{b}", [P, D]) for b in range(2)]
        wst = ExitStack()
        scope[0] = wst
        WR = sb("WR", [P, 2 * EW])
        WH = sb("WH", [P, 2 * EW], F32R)
        WL = sb("WL", [P, 2 * EW], F32R)
        wst.close()
        scope[0] = est
        fx = [sb(f"fx{b}", [P, D]) for b in range(NF)]
        fo = [sb(f"fo{b}", [P, D]) for b in range(NF)]
        fss = sb("fss", [P, NF])
        fnv = sb("fnv", [P, 2, NF])
        fj = sb("fj", [P, D])
        est.close()

        names = """par_in win_in con_in c_g1 c_pool dch w_scaled act_small pws_ready pool_chain tabs_ready
            x_in0 x_in1 sq_done red_done ss_done var_done std_done um_done u_evac u_stored u_in
            k_done k_evac t_in t_zero tr_done mz_done v_done cp_done sp_done y_done yp_done gelu_done fo_done
            y_stored y_in dchb mz_zero st_stored
            wout_in w2_hi w2_lo ys_done ys_hi ys_lo a_done sig_done x2_done xn_done xr_in0 xr_in1 x2_st0 x2_st1 xn_st0 xn_st1 xt_done xt_evac rl_done rl_evac ssq_done dchc
            dchd dche exp_d cnt_done one_hot_done tbl_done ctl_done d_iota d_ready exp_in
            gat0 gat1 xgt_done xgt_evac xgt_lo gu_done h_done sl_done ht_done ht_evac hi_split lo_split dn_done dn_evac wts
acc_done spare_set f_in0 f_in1 f_in2 f_in3 f_sq f_out f_st0 f_st1 f_st2 f_st3 dchf f_std""".split()
        S = {n: sem(n) for n in names}
        block = outer.enter_context(nc.Block())

        def steps(eng, n, step):
            step(0, 0)
            step(1, 1)
            with eng.Fori(1, n // 2) as i:
                step(2 * i, 0)
                step(2 * i + 1, 1)

        def early(t, n=2):
            return isinstance(t, int) and t < n

        class Chain:
            def __init__(self, eng, s):
                self.eng, self.s, self.n = eng, s, 0

            def __call__(self, ins):
                self.n += 1
                ins.then_inc(self.s, 1)
                self.eng.wait_ge(self.s, self.n)

        @block.sync
        def _(sp):
            for dst_, src in ((PAR[:, :, :], par), (s0_sb[:, :, :, :], s0), (BC[:, :, :, :], b_in),
                              (d_sb[:, :], d_in), (gm_sb[:, :], gmix)):
                sp.dma_start(dst_, src).then_inc(S["par_in"], 16)
            sp.dma_start(w1[:, :, :], w_in).then_inc(S["win_in"], 16)
            for j in range(2):
                sp.dma_start(xT[j][:, :, :], x_cols[j]).then_inc(S[f"x_in{j}"], 16)
            sp.dma_start(gf_b[:, :], gffn.partition_broadcast(P)).then_inc(S["con_in"], 16)
            sp.dma_start(gl_b[:, :], gfin.partition_broadcast(P)).then_inc(S["con_in"], 16)
            sp.dma_start(wr_sb[:, :, :], w_route).then_inc(S["con_in"], 16)
            for j in range(L):
                sp.wait_ge(S["u_evac"], CB * (j + 1))
                if j + 2 < L:
                    sp.wait_ge(S["sq_done"], j + 1)
                    sp.dma_start(xT[j % 2][:, :, :], x_cols[j + 2]).then_inc(S[f"x_in{j % 2}"], 16)
                sp.dma_start(uD[j], uT[j % 2][:, :, :]).then_inc(S["u_stored"], 16)
                sp.wait_ge(S["u_stored"], 16 * (j + 1))
                for cb in range(CB):
                    sp.dma_start(U[j * GC:(j + 1) * GC, cb * 8:(cb + 1) * 8, :],
                                 uD[j].rearrange("(g c) b k -> b c g k", c=GC)[cb]).then_inc(S["u_in"], 16)
            sp.wait_ge(S["k_evac"], 8)
            sp.wait_ge(S["t_zero"], 1)
            for j in range(L):
                sp.dma_start(T[j * GC:(j + 1) * GC, :, j * GC:L * GC],
                             Kst[:, :, 0:(L - j) * GC]).then_inc(S["t_in"], 16)
            sp.wait_ge(S["um_done"], CB * L)
            sp.wait_ge(S["tabs_ready"], 1)
            sp.dma_start(w2a[:, :, :], w_out[:, 0:CB - 1, :]).then_inc(S["wout_in"], 16)
            for cb in range(CB):
                sp.wait_ge(S["gelu_done"], 8 * (cb + 1))
                sp.dma_start(yD[cb], U[:, cb * 8:(cb + 1) * 8, :]).then_inc(S["y_stored"], 16)
                if cb == CB - 1:
                    sp.wait_ge(S["fo_done"], PR)
                    sp.wait_ge(S["y_done"], G)
                    sp.dma_start(w2b[:, :, :], w_out[:, CB - 1:CB, :]).then_inc(S["wout_in"], 16)
                sp.wait_ge(S["y_stored"], 16 * (cb + 1))
                for g in range(8):
                    sp.dma_start(U[g * GC:(g + 1) * GC, cb * 8:(cb + 1) * 8, :],
                                 yD[cb].rearrange("(i c) g k -> g c i k", c=GC)[g]).then_inc(S["y_in"], 16)
            sp.dma_start(st_out, FO[:, :, :, :]).then_inc(S["st_stored"], 16)

            def c_load(t, b, rows=P):
                if not early(t):
                    sp.wait_ge(S["x2_done"], t - 1)
                sp.dma_start(cut(xr[b], rows)[:, :], x_rows[ds(t * P, rows), :]).then_inc(S[f"xr_in{b}"], 16)

            def c_store(t, b, rows=P):
                sp.wait_ge(S["x2_done"], t + 1)
                sp.dma_start(x2D[ds(t * P, rows), :], cut(x2[b], rows)[:, :]).then_inc(S[f"x2_st{b}"], 16)
                sp.wait_ge(S["xn_done"], t + 1)
                sp.dma_start(xnD[ds(t * P, rows), :], cut(xn[b], rows)[:, :]).then_inc(S[f"xn_st{b}"], 16)

            c_load(0, 0)
            c_load(1, 1)
            sp.dma_start(x2D[NT:NT + P, :], gl_b[:, :]).then_inc(S["spare_set"], 16)
            c_store(0, 0)
            c_load(2, 0)
            c_store(1, 1)
            c_load(3, 1)
            with sp.Fori(1, TF // 2 - 1) as i:
                c_store(2 * i, 0)
                c_load(2 * i + 2, 0)
                c_store(2 * i + 1, 1)
                c_load(2 * i + 3, 1)
            c_store(TF - 2, 0)
            c_load(TF, 0, LAST)
            c_store(TF - 1, 1)
            c_store(TF, 0, LAST)

            sp.wait_ge(S["ctl_done"], 1)
            for e in range(NE):
                if e >= 1:
                    sp.wait_ge(S["wts"], 32 * e)
                if e >= 2:
                    sp.wait_ge(S["lo_split"], CUTS * (e - 1))
                at = e % 2 * EW
                sp.dma_start(WR[:, at:at + KD * 2 * DE], w_gu[e]).then_inc(S["wts"], 16)
                sp.dma_start(WR[:, at + KD * 2 * DE:at + EW], w_dn[e]).then_inc(S["wts"], 16)

            def f_load(t, b, rows=P):
                sp.dma_start(cut(fx[b], rows)[:, :], x2D[ds(t * P, rows), :]).then_inc(S[f"f_in{b}"], 16)

            def f_store(t, b, rows=P):
                sp.wait_ge(S["f_out"], t + 1)
                sp.dma_start(y_out[ds(t * P, rows), :], cut(fo[b], rows)[:, :]).then_inc(S[f"f_st{b}"], 16)

            sp.wait_ge(S["acc_done"], 16 * SLOTS)
            for b in range(NF):
                f_load(b, b)
            with sp.Fori(0, TF // NF - 1) as i:
                for b in range(NF):
                    f_store(NF * i + b, b)
                    f_load(NF * i + (b + NF), b)
            f_store(TF - NF, 0)
            f_load(TF, 0, LAST)
            for b in range(1, NF):
                f_store(TF - NF + b, b)
            f_store(TF, 0, LAST)
            for b in range(NF):
                sp.wait_ge(S[f"f_st{b}"], 16 * (TF // NF + (b == 0)))

        @block.gpsimd
        def _(pool):
            ch = Chain(pool, S["pool_chain"])
            ch(pool.memset(ident[:, :], 0.0))
            ch(pool.affine_select(out=ident[:, :], in_=ident[:, :], compare_op=ALU.not_equal, fill=1.0, base=0,
                                  pattern=[[-1, P]], channel_multiplier=1))
            ch(pool.memset(epsc[:, :], EPS))
            pool.memset(ones[:, :], 1.0).then_inc(S["c_pool"], 1)
            ch(pool.memset(upper[:, :], 1.0))
            ch(pool.affine_select(out=upper[:, :], in_=upper[:, :], compare_op=ALU.is_gt, fill=0.0, base=0,
                                  pattern=[[1, P]], channel_multiplier=-1))
            pool.memset(T[:, :, :], 0.0).then_inc(S["t_zero"], 1)
            pool.wait_ge(S["pws_ready"], 1)

            def cmul(ore, oim, are, aim, bre, bim, ta, tb):
                ch(pool.tensor_tensor(ta, are, bre, ALU.mult))
                ch(pool.tensor_tensor(ore, aim, bim, ALU.mult))
                ch(pool.tensor_tensor(ore, ta, ore, ALU.subtract))
                ch(pool.tensor_tensor(ta, are, bim, ALU.mult))
                ch(pool.tensor_tensor(oim, aim, bre, ALU.mult))
                ch(pool.tensor_tensor(oim, ta, oim, ALU.add))

            def v4(ap):
                return ap.rearrange("p r (d c) -> p r d c", c=GC)

            def t4(n, m):
                return p1[:, 0:n * m * GC].rearrange("p (r d c) -> p r d c", d=m, c=GC)

            def over_c(ap, m):
                return ap.rearrange("p d r -> p r d").unsqueeze(3).to_broadcast([P, PR, m, GC])

            def over_d(ap, m):
                return ap.unsqueeze(2).to_broadcast([P, PR, m, GC])

            m = L + 1
            cre, cim = over_d(BC[:, 2, :, :], m), over_d(BC[:, 3, :, :], m)
            wre, wimn = over_c(PW[:, 0, :, :], m), over_c(PW[:, 2, :, :], m)
            lre, lim = v4(CL[:, 0, :, :]), v4(CL[:, 1, :, :])
            ta = t4(PR, m)
            ch(pool.tensor_tensor(ta, cre, wre, ALU.mult))
            ch(pool.tensor_tensor(lre, cim, wimn, ALU.mult))
            ch(pool.tensor_tensor(lre, lre, ta, ALU.add))
            ch(pool.tensor_tensor(ta, cre, wimn, ALU.mult))
            ch(pool.tensor_tensor(lim, cim, wre, ALU.mult))
            ch(pool.tensor_tensor(lim, ta, lim, ALU.subtract))
            for j in range(L):
                bre, bim = BB[:, 0, :, :], BB[:, 1, :, :]
                pre = PW[:, 0, L - 1 - j, :].unsqueeze(2).to_broadcast([P, PR, GC])
                pim = PW[:, 1, L - 1 - j, :].unsqueeze(2).to_broadcast([P, PR, GC])
                tj = p1[:, 0:PR * GC].rearrange("p (r c) -> p r c", c=GC)
                cmul(E[:, 0, :, j * GC:(j + 1) * GC], E[:, 1, :, j * GC:(j + 1) * GC], bre, bim, pre, pim, tj, None)
            ch(pool.memset(WT[:, 0, :, 0:1], 1.0))
            ch(pool.memset(WT[:, 1, :, 0:1], 0.0))
            for l in range(8):
                n = 1 << l
                pre = PH[:, 0, l, :].unsqueeze(2).to_broadcast([P, PR, n])
                pim = PH[:, 1, l, :].unsqueeze(2).to_broadcast([P, PR, n])
                tl = p1[:, 0:PR * n].rearrange("p (r k) -> p r k", k=n)
                cmul(WT[:, 0, :, n:2 * n], WT[:, 1, :, n:2 * n], WT[:, 0, :, 0:n], WT[:, 1, :, 0:n], pre, pim, tl, None)
            pre = PW[:, 0, L, :].unsqueeze(2).to_broadcast([P, PR, DECB])
            pim = PW[:, 1, L, :].unsqueeze(2).to_broadcast([P, PR, DECB])
            cmul(F0[:, 0, :, :], F0[:, 1, :, :], s0_sb[:, 0, :, :], s0_sb[:, 1, :, :], pre, pim,
                 p1[:, 0:PR * DECB].rearrange("p (r k) -> p r k", k=DECB), None)
            pool.memset(p1[:, 0:1], 0.0).then_inc(S["tabs_ready"], 1)

            pool.wait_ge(S["um_done"], CB * L)
            pool.wait_ge(S["u_evac"], CB * L)
            pool.wait_ge(S["u_stored"], 16 * L)
            pool.wait_ge(S["k_done"], 8)
            for b in range(2):
                pool.memset(MZ[b][:, :, :, :], 0.0).then_inc(S["mz_zero"], 1)
                pool.memset(Sp[b][:, :, DECB:DECB + 1], 0.0).then_inc(S["mz_zero"], 1)
            pool.wait_ge(S["t_in"], 16 * L)

            def b_copy(r, b):
                if not early(r):
                    pool.wait_ge(S["tr_done"], r - 1)
                pool.tensor_copy(ES[b][:, :, :], E[:, :, ds(r, 1), :].rearrange("p a o k -> p a (o k)")).then_inc(S["cp_done"], 1)
                if not early(r):
                    pool.wait_ge(S["y_done"], 2 * r - 2)
                pool.tensor_copy(NS[b][:, :, :], CL[:, :, ds(r, 1), GC:(L + 1) * GC].rearrange("p a o k -> p a (o k)")).then_inc(S["cp_done"], 1)
                pool.tensor_copy(TS[b][:, :, :], T[:, ds(2 * r, 2), :]).then_inc(S["cp_done"], 1)
                pool.tensor_copy(Sp[b][:, :, 0:DECB], s0_sb[:, :, ds(r, 1), :].rearrange("p a o k -> p a (o k)")).then_inc(S["cp_done"], 1)
            steps(pool, PR, b_copy)

            pool.wait_ge(S["y_in"], 16 * CB * 8)
            yflat = U[:, :, :].rearrange("p (b i) k -> p b (i k)", b=CB)

            def c_copy(t, b, rows=P):
                if not early(t):
                    pool.wait_ge(S["ys_lo"], t - 1)
                pool.tensor_copy(ys[b][:, :, 0:rows], yflat[:, :, ds(t * P, rows)]).then_inc(S["ys_done"], 1)
            steps(pool, TF, c_copy)
            c_copy(TF, 0, LAST)

            pool.wait_ge(S["rl_evac"], TT)
            pool.wait_ge(S["st_stored"], 16)
            pool.wait_ge(S["xn_done"], TT)
            for b in range(2):
                pool.wait_ge(S[f"xn_st{b}"], 16 * (TF // 2 + 1 - b))
                pool.wait_ge(S[f"x2_st{b}"], 16 * (TF // 2 + 1 - b))
            pool.iota(iot[:, :], [[1, P]], base=0, channel_multiplier=0, allow_small_or_imprecise_dtypes=True).then_inc(S["d_iota"], 1)
            pool.iota(tokid[:, :], [[P, TT]], base=1, channel_multiplier=1, allow_small_or_imprecise_dtypes=True).then_inc(S["d_iota"], 1)
            pool.iota(spare[:, :], [[0, 1]], base=NT + 1, channel_multiplier=1, allow_small_or_imprecise_dtypes=True).then_inc(S["d_iota"], 1)
            pool.iota(desc[:, :], [[-1, 4]], base=4, channel_multiplier=0, allow_small_or_imprecise_dtypes=True).then_inc(S["d_iota"], 1)

            pool.wait_ge(S["ctl_done"], 1)

            pool.wait_ge(S["spare_set"], 16)
            for t in range(SLOTS + 4):
                if t < SLOTS:
                    if t >= 2:
                        pool.wait_ge(S["xgt_done"], 2 * t - 2)
                    pool.indirect_dma_start(xg[t % 2][:, :], None, xnD,
                                            bass.IndirectOffsetOnAxis(ap=token_of[:, t:t + 1], axis=0)).then_inc(S[f"gat{t % 2}"], 16)
                s = t - 4
                if s >= 0:
                    pool.wait_ge(S["dn_evac"], s + 1)
                    if s >= 1:
                        pool.wait_ge(S["acc_done"], 16 * s)
                    pool.indirect_dma_start(x2D, bass.IndirectOffsetOnAxis(ap=sum_of[:, s:s + 1], axis=0), yo[s % 2][:, :], None,
                                            compute_op=ALU.add).then_inc(S["acc_done"], 16)

        @block.scalar
        def _(act):
            act.wait_ge(S["par_in"], 80)
            act.activation(sm[:, 0, :], PAR[:, 2, :], ACT.Exp).then_inc(S["act_small"], 1)
            act.wait_ge(S["dch"], 2)
            act.activation(sm[:, 3, :], sm[:, 1, :], ACT.Exp).then_inc(S["act_small"], 1)
            act.activation(sm[:, 4, :], sm[:, 1, :], ACT.Exp, scale=float(L)).then_inc(S["act_small"], 1)
            act.wait_ge(S["c_g1"], 1)
            act.activation(sm[:, 8, :], sm[:, 6, :], ACT.Sin).then_inc(S["act_small"], 1)
            act.activation(sm[:, 9, :], sm[:, 7, :], ACT.Sin).then_inc(S["act_small"], 1)

            def a_step(j, b):
                i = j // 2 if isinstance(j, int) else None
                act.wait_ge(S[f"x_in{b}"], 8 * (j - b) + 16)
                if not (isinstance(j, int) and j == 0):
                    act.wait_ge(S["red_done"], j)
                act.activation(sq[:, :, :], xT[b][:, :, :], ACT.Square).then_inc(S["sq_done"], 1)
                act.wait_ge(S["var_done"], j + 1)
                act.activation(std[b][:, :], rst[b][:, :], ACT.Sqrt).then_inc(S["std_done"], 1)
            for j in range(L):
                a_step(j, j % 2)

            for n in range(8):
                act.wait_ge(S["k_done"], n + 1)
                if n == 0:
                    act.wait_ge(S["u_stored"], 16 * L)
                    act.wait_ge(S["u_evac"], CB * L)
                    act.wait_ge(S["tabs_ready"], 1)
                act.activation(Kst[:, :, :].rearrange("c (r h) k -> c r h k", h=2)[:, n % 4 * 4:n % 4 * 4 + 4, n // 4, :], pbig[0:GC, n, :].rearrange("p (g k) -> p g k", g=4),
                               ACT.Copy).then_inc(S["k_evac"], 1)

            act.wait_ge(S["mz_zero"], 4)

            def b_mz(r, b):
                act.wait_ge(S["tr_done"], r + 1)
                if not early(r):
                    act.wait_ge(S["v_done"], r - 1)
                tr = pbig[:, 4, 0:2 * P].rearrange("p (a m) -> p a m", a=2)
                act.activation(MZ[b][:, 0, :, 0:ST], tr[:, :, 0:ST], ACT.Copy).then_inc(S["mz_done"], 1)
                act.activation(MZ[b][:, 1, :, ST:P], tr[:, :, ST:P], ACT.Copy).then_inc(S["mz_done"], 1)

            def b_gelu(r):
                for g in range(2):
                    act.wait_ge(S["yp_done"], 2 * r + g + 1)
                    act.activation(U[:, ds(2 * r + g, 1), :].rearrange("p o k -> p (o k)"), yt[g][:, :],
                                   ACT.Gelu_apprx_tanh).then_inc(S["gelu_done"], 1)

            b_mz(0, 0)
            b_mz(1, 1)
            b_mz(2, 0)
            b_gelu(0)
            b_mz(3, 1)
            b_gelu(1)
            with act.Fori(1, PR // 2 - 1) as i:
                b_mz(2 * i + 2, 0)
                b_gelu(2 * i)
                b_mz(2 * i + 3, 1)
                b_gelu(2 * i + 1)
            b_gelu(PR - 2)
            b_gelu(PR - 1)

            act.wait_ge(S["wout_in"], 32)
            act.wait_ge(S["gelu_done"], G)
            act.wait_ge(S["y_stored"], 16 * CB)
            for n in (2, 3, 0, 1):
                c = slice(n * 512, (n + 1) * 512)
                act.activation(w2H[:, 0:CB - 1, c], w2a[:, :, c], ACT.Copy).then_inc(S["w2_hi"], 1)
                act.activation(w2H[:, CB - 1:CB, c], w2b[:, :, c], ACT.Copy).then_inc(S["w2_hi"], 1)

            def c_y_hi(t, b, rows=P):
                act.wait_ge(S["ys_done"], t + 1)
                if not early(t):
                    act.wait_ge(S["a_done"], 4 * t - 4)
                act.activation(ysH[b][:, :, 0:rows], ys[b][:, :, 0:rows], ACT.Copy).then_inc(S["ys_hi"], 1)

            def c_gate(t, b, rows=P):
                if not early(t, 1):
                    act.wait_ge(S["x2_done"], t)
                for n in range(2):
                    act.wait_ge(S["a_done"], 4 * t + 3 + n)
                    act.activation(sg[0:rows, n * 512:(n + 1) * 512], pbig[0:rows, 2 + n, :], ACT.Sigmoid).then_inc(S["sig_done"], 1)
                act.wait_ge(S["x2_done"], t + 1)
                act.activation(junk[0:rows, :], x2[b][0:rows, :], ACT.Square, accum_out=ssq[0:rows, ds(t, 1)]).then_inc(S["ssq_done"], 1)

            def c_turned(t, rows=P):
                for n in range(2):
                    act.wait_ge(S["xt_done"], 2 * t + n + 1)
                    if n == 0 and not early(t, 1):
                        act.wait_ge(S["rl_done"], t)
                    act.activation(xnT[:, 4 * n:4 * n + 4, 0:rows],
                                   pbig[:, 4 + n, :].rearrange("p (a m) -> p a m", a=4)[:, :, 0:rows], ACT.Copy).then_inc(S["xt_evac"], 1)

            def c_routed(t, rows=P):
                act.wait_ge(S["rl_done"], t + 1)
                act.activation(logit[0:rows, ds(t, 1), :].rearrange("p o k -> p (o k)"), pbig[0:rows, 6, 0:20], ACT.Copy).then_inc(S["rl_evac"], 1)

            c_y_hi(0, 0)
            c_y_hi(1, 1)
            c_gate(0, 0)
            c_y_hi(2, 0)
            c_gate(1, 1)
            c_turned(0)
            with act.Fori(1, TF // 2 - 1) as i:
                c_y_hi(2 * i + 1, 1)
                c_gate(2 * i, 0)
                c_routed(2 * i - 2)
                c_turned(2 * i - 1)
                c_y_hi(2 * i + 2, 0)
                c_gate(2 * i + 1, 1)
                c_routed(2 * i - 1)
                c_turned(2 * i)
            c_y_hi(TF - 1, 1)
            c_gate(TF - 2, 0)
            c_routed(TF - 4)
            c_turned(TF - 3)
            c_y_hi(TF, 0, LAST)
            c_gate(TF - 1, 1)
            c_routed(TF - 3)
            c_turned(TF - 2)
            c_gate(TF, 0, LAST)
            c_routed(TF - 2)
            c_turned(TF - 1)
            c_routed(TF - 1)
            c_turned(TF, LAST)
            c_routed(TF, LAST)

            act.wait_ge(S["exp_in"], 1)
            act.activation(R3[1][:, :, :], R3[0][:, :, :], ACT.Exp).then_inc(S["exp_d"], 1)
            act.wait_ge(S["exp_in"], 2)
            act.activation(R1[5][:, :], R1[4][:, :], ACT.Exp).then_inc(S["exp_d"], 1)

            act.wait_ge(S["ctl_done"], 1)

            def e_x(s, b):
                if not early(s):
                    act.wait_ge(S["gu_done"], s - 1)
                for n in range(2):
                    act.wait_ge(S["xgt_done"], 2 * s + n + 1)
                    act.activation(xgH[b][:, 4 * n:4 * n + 4, :], pbig[:, 4 + n, :].rearrange("p (a m) -> p a m", a=4), ACT.Copy).then_inc(S["xgt_evac"], 1)

            def e_silu(s, b):
                act.wait_ge(S["gu_done"], s + 1)
                if not early(s, 1):
                    act.wait_ge(S["h_done"], s)
                act.activation(sl[:, :], pbig[:, 6, 0:DE], ACT.Silu).then_inc(S["sl_done"], 1)

            def e_y(s, b):
                if not early(s):
                    act.wait_ge(S["acc_done"], 16 * s - 16)
                act.wait_ge(S["dn_done"], s + 2)
                act.wait_ge(S["ctl_done"], 1)
                act.activation(yo[b][:, :].rearrange("p (a m) -> p a m", a=2), pbig[:, 0:2, :], ACT.Copy,
                               scale=cw_of[:, ds(s, 1)]).then_inc(S["dn_evac"], 1)

            def e_word(s):
                return act.value_load(ctrl[0:1, ds(C_NEXT + s, 1)], min_val=0, max_val=EW)

            def e_split(s, to, part):
                with act.If(to != SKIP):
                    if part == 0:
                        e = act.value_load(ctrl[0:1, ds(C_EXP + s, 1)], min_val=0, max_val=NE - 1)
                        act.wait_ge(S["wts"], e * 32 + 64)
                    if not early(s, 1):
                        act.wait_ge(S["dn_done"] if part else S["gu_done"], s + part)
                    act.wait_ge(S["ctl_done"], 1)
                    for c in (range(UP_CUTS), range(UP_CUTS, CUTS))[part]:
                        act.activation(WH[:, ds(to + c * CW, CW)], WR[:, ds(to + c * CW, CW)], ACT.Copy).then_inc(S["hi_split"], 1)

            act.wait_ge(S["wts"], 32)
            for c in range(CUTS):
                act.activation(WH[:, c * CW:(c + 1) * CW], WR[:, c * CW:(c + 1) * CW], ACT.Copy).then_inc(S["hi_split"], 1)
            def e_act(s, b, to, ahead=True, last=False):
                then = None
                if not last:
                    e_split(s, to, 0)
                e_silu(s, b)
                if not last:
                    e_x(s + 1, 1 - b)
                    if ahead:
                        then = e_word(s + 1)
                if not early(s, 1):
                    e_y(s - 1, 1 - b)
                if not last:
                    e_split(s, to, 1)
                return then

            e_x(0, 0)
            to = e_act(0, 0, e_word(0))
            e_act(1, 1, to, ahead=False)
            with act.Fori(0, SLOTS // 4 - 1) as i:
                to = e_word(4 * i + 2)
                for n in range(2, 6):
                    to = e_act(4 * i + n, n % 2, to, ahead=n < 5)
            e_act(SLOTS - 2, 0, e_word(SLOTS - 2), ahead=False)
            e_act(SLOTS - 1, 1, None, last=True)
            e_y(SLOTS - 1, 1)

            def f_norm(t, b, rows=P):
                act.wait_ge(S[f"f_in{b}"], 16 * (t // NF) + 16 if isinstance(t, int) else 4 * (t - b) + 16)
                act.activation(fj[0:rows, :], fx[b][0:rows, :], ACT.Square, accum_out=fss[0:rows, b:b + 1]).then_inc(S["f_sq"], 1)
                act.wait_ge(S["f_sq"], t + 1)
                if not early(t, NF):
                    act.wait_ge(S["f_out"], t - NF + 1)
                act.activation(fnv[0:rows, 0, b:b + 1], fss[0:rows, b:b + 1], ACT.Sqrt, scale=1.0 / D,
                               bias=epsc[0:rows, 0:1]).then_inc(S["f_std"], 1)
            for b in range(NF):
                f_norm(b, b)
            with act.Fori(1, TF // NF) as i:
                for b in range(NF):
                    f_norm(NF * i + b, b)
            f_norm(TF, 0, LAST)

        @block.tensor
        def _(pe):
            pe.wait_ge(S["w_scaled"], KD)
            pe.wait_ge(S["c_pool"], 1)
            for j in range(L):
                b = j % 2
                pe.wait_ge(S[f"x_in{b}"], 16 * (j // 2 + 1))
                for cb in range(CB):
                    if j >= 1:
                        pe.wait_ge(S["u_evac"], CB * (j - 1) + cb + 1)
                    for k in range(KD):
                        mm = pe.matmul(pbig[:, cb, 0:NCH], w1[:, k, cb * P:(cb + 1) * P], xT[b][:, k, :],
                                       start=(k == 0), stop=(k == KD - 1))
                    mm.then_inc(S["um_done"], 1)
                    if cb == 0:
                        pe.wait_ge(S["red_done"], j + 1)
                        pe.matmul(pbig[:, 4 + b, 0:NCH], ones[:, :], red[b][:, :], start=True, stop=True).then_inc(S["ss_done"], 1)
            pe.wait_ge(S["tabs_ready"], 1)
            pe.wait_ge(S["u_evac"], CB * L)
            for n in range(8):
                h = n // 4 * ST
                for q in range(4):
                    r = n % 4 * 4 + q
                    for a in range(2):
                        mm = pe.matmul(pbig[0:GC, n, q * P:(q + 1) * P], BB[h:h + ST, a, r, :],
                                       CL[h:h + ST, a, r, 0:L * GC], start=(a == 0), stop=(a == 1))
                mm.then_inc(S["k_done"], 1)

            pe.wait_ge(S["k_evac"], 8)
            pe.wait_ge(S["u_in"], 16 * L * CB)

            def b_state(r, b):
                pe.wait_ge(S["cp_done"], 4 * r + 1)
                if not early(r, 1):
                    pe.wait_ge(S["mz_done"], 2 * r)
                for a in range(2):
                    mm = pe.transpose(pbig[:, 4, a * P:(a + 1) * P], ES[b][:, a, :], ident[:, :])
                mm.then_inc(S["tr_done"], 1)
                pe.wait_ge(S["mz_done"], 2 * r + 2)
                if not early(r):
                    pe.wait_ge(S["fo_done"], r - 1)
                for a in range(2):
                    for g in range(2):
                        mm = pe.matmul(pbig[:, 2 * b + a, 0:NCH], MZ[b][:, g, a, :],
                                       U[:, ds(2 * r + g, 1), :].rearrange("p o k -> p (o k)"),
                                       start=(g == 0), stop=(g == 1))
                mm.then_inc(S["v_done"], 1)

            def b_out(r, b):
                pe.wait_ge(S["cp_done"], 4 * r + 4)
                pe.wait_ge(S["sp_done"], r + 1)
                for g in range(2):
                    if not early(r, 1):
                        pe.wait_ge(S["yp_done"], 2 * r - 1 + g)
                    h = g * ST
                    out = pbig[:, 5 + g, 0:NCH]
                    pe.matmul(out, TS[b][:, g, :], U[:, ds(2 * r + g, 1), :].rearrange("p o k -> p (o k)"), start=True, stop=False)
                    pe.matmul(out, NS[b][h:h + ST, 0, :], Sp[b][h:h + ST, 0, 0:NCH], start=False, stop=False)
                    pe.matmul(out, NS[b][h:h + ST, 1, :], Sp[b][h:h + ST, 1, 0:NCH], start=False, stop=True).then_inc(S["y_done"], 1)

            b_state(0, 0)
            b_state(1, 1)
            b_out(0, 0)
            b_state(2, 0)
            b_out(1, 1)
            b_state(3, 1)
            with pe.Fori(1, PR // 2 - 1) as i:
                b_out(2 * i, 0)
                b_state(2 * i + 2, 0)
                b_out(2 * i + 1, 1)
                b_state(2 * i + 3, 1)
            b_out(PR - 2, 0)
            b_out(PR - 1, 1)

            pe.wait_ge(S["yp_done"], G)
            pe.wait_ge(S["con_in"], 48)

            def c_proj(t, b, ns, rows=P):
                if 2 in ns:
                    pe.wait_ge(S["ys_lo"], t + 1)
                for n in ns:
                    if early(t, 1):
                        pe.wait_ge(S["w2_lo"], 2 * ((2, 3, 0, 1).index(n) + 1))
                    if not early(t, 1):
                        pe.wait_ge(S["sig_done" if n >= 2 else "x2_done"], 2 * t - 3 + n if n >= 2 else t)
                    for k in range(CB):
                        c = slice(n * 512, (n + 1) * 512)
                        pe.matmul(pbig[0:rows, n, :], ysH[b][:, k, 0:rows], w2H[:, k, c], start=(k == 0), stop=False)
                        pe.matmul(pbig[0:rows, n, :], ysH[b][:, k, 0:rows], w2L[:, k, c], start=False, stop=False)
                        mm = pe.matmul(pbig[0:rows, n, :], ysL[b][:, k, 0:rows], w2H[:, k, c], start=False, stop=(k == CB - 1))
                    mm.then_inc(S["a_done"], 1)

            def c_turn(t, b, rows=P):
                pe.wait_ge(S["xn_done"], t + 1)
                for n in range(2):
                    if not early(t, 1):
                        pe.wait_ge(S["xt_evac"], 2 * t - 1 + n)
                    for k in range(4):
                        mm = pe.transpose(pbig[:, 4 + n, k * P:k * P + rows], xn[b][0:rows, (4 * n + k) * P:(4 * n + k + 1) * P],
                                          ident[0:rows, 0:rows])
                    mm.then_inc(S["xt_done"], 1)

            def c_logit(t, rows=P):
                pe.wait_ge(S["xt_evac"], 2 * t + 2)
                if not early(t, 1):
                    pe.wait_ge(S["rl_evac"], t)
                for k in range(KD):
                    mm = pe.matmul(pbig[0:rows, 6, 0:20], xnT[:, k, 0:rows], wr_sb[:, k, :], start=(k == 0), stop=(k == KD - 1))
                mm.then_inc(S["rl_done"], 1)

            def c_step(t, b, rows=P, prev=2):
                c_proj(t, b, (2, 3), rows)
                if prev > 1:
                    c_logit(t - 2)
                c_proj(t, b, (0, 1), rows)
                if prev > 0:
                    c_turn(t - 1, 1 - b)

            c_step(0, 0, prev=0)
            c_step(1, 1, prev=1)
            with pe.Fori(1, TF // 2) as i:
                c_step(2 * i, 0)
                c_step(2 * i + 1, 1)
            c_step(TF, 0, LAST)
            c_logit(TF - 1)
            c_turn(TF, 0, LAST)
            c_logit(TF, LAST)

            pe.wait_ge(S["d_ready"], 1)
            pe.matmul(pbig[:, 0, 0:TT * NE], upper[:, :], EE[:, :, :, :].rearrange("p t g e -> p (t g e)"), start=True, stop=True)
            pe.matmul(pbig[:, 1, 0:TT * NE], ones[:, :], EE[:, :, :, :].rearrange("p t g e -> p (t g e)"), start=True, stop=True).then_inc(S["cnt_done"], 1)
            for n in range(2 * TT):
                pe.wait_ge(S["one_hot_done"], n + 1)
                mm = pe.matmul(pbig[:, 2, 0:2 * SLOTS], oh_lo[n % 4][:, :], oh_hi[n % 4][:, :, :].rearrange("p a s -> p (a s)"), start=(n == 0), stop=(n == 2 * TT - 1))
                mm.then_inc(S["tbl_done"], 1)

            pe.wait_ge(S["ctl_done"], 1)
            pe.nop().then_inc(S["dn_done"], 1)

            def e_turn(s, b):
                pe.wait_ge(S[f"gat{b}"], 8 * (s - b) + 16)
                for n in range(2):
                    if not early(s, 1):
                        pe.wait_ge(S["xgt_evac"], 2 * s - 1 + n)
                        pe.wait_ge(S["xgt_lo"], 2 * s - 1 + n)
                    for k in range(4):
                        mm = pe.transpose(pbig[:, 4 + n, k * P:(k + 1) * P], xg[b][:, (4 * n + k) * P:(4 * n + k + 1) * P], ident[:, :])
                    mm.then_inc(S["xgt_done"], 1)

            def e_up(s, b, off, e, maybe):
                pe.wait_ge(S["xgt_evac"], 2 * s + 2)
                if not early(s, 1):
                    pe.wait_ge(S["h_done"], s)
                pe.wait_ge(S["lo_split"], e * CUTS + UP_CUTS)
                pe.wait_ge(S["ctl_done"], 1)
                if maybe:
                    with pe.If(off != SKIP):
                        e_up_products(s, b, off)
                    with pe.Else():
                        pe.nop().then_inc(S["gu_done"], 1)
                else:
                    e_up_products(s, b, off)

            def e_up_products(s, b, off):
                for k in range(KD):
                    w = ds(off + k * 2 * DE, 2 * DE)
                    pe.matmul(pbig[:, 6, :], xgH[b][:, k, :], WH[:, w], start=(k == 0), stop=False)
                    pe.matmul(pbig[:, 6, :], xgH[b][:, k, :], WL[:, w], start=False, stop=False)
                pe.wait_ge(S["xgt_lo"], 2 * s + 2)
                for k in range(KD):
                    mm = pe.matmul(pbig[:, 6, :], xgL[b][:, k, :], WH[:, ds(off + k * 2 * DE, 2 * DE)], start=False, stop=(k == KD - 1))
                mm.then_inc(S["gu_done"], 1)

            def e_hturn(s, b):
                pe.wait_ge(S["h_done"], s + 1)
                if not early(s, 1):
                    pe.wait_ge(S["ht_evac"], s)
                for k in range(2):
                    mm = pe.transpose(pbig[:, 7, k * P:(k + 1) * P], hh[b][:, k * P:(k + 1) * P], ident[:, :])
                mm.then_inc(S["ht_done"], 1)

            def e_down(s, b, off, e, maybe):
                pe.wait_ge(S["ht_evac"], s + 1)
                if not early(s, 1):
                    pe.wait_ge(S["dn_evac"], s)
                pe.wait_ge(S["lo_split"], e * CUTS + CUTS)
                pe.wait_ge(S["ctl_done"], 1)
                if maybe:
                    with pe.If(off != SKIP):
                        e_down_products(s, b, off)
                    with pe.Else():
                        pe.nop().then_inc(S["dn_done"], 1)
                else:
                    e_down_products(s, b, off)

            def e_down_products(s, b, off):
                for n in range(2):
                    for k in range(2):
                        w = ds(off + (KD * 2 * DE + k * D + n * 512), 512)
                        pe.matmul(pbig[:, n, :], hTH[b][:, k, :], WH[:, w], start=(k == 0), stop=False)
                        pe.matmul(pbig[:, n, :], hTH[b][:, k, :], WL[:, w], start=False, stop=False)
                        mm = pe.matmul(pbig[:, n, :], hTL[b][:, k, :], WH[:, w], start=False, stop=(k == 1))
                mm.then_inc(S["dn_done"], 1)

            def words(s):
                return (pe.value_load(ctrl[0:1, ds(C_AT + s, 1)], min_val=0, max_val=EW),
                        pe.value_load(ctrl[0:1, ds(C_EXP + s, 1)], min_val=0, max_val=NE - 1))

            def e_step(s, b, before, last=False, maybe=False):
                now = words(s)
                if before:
                    e_hturn(s - 1, 1 - b)
                e_up(s, b, *now, maybe)
                if not last:
                    e_turn(s + 1, 1 - b)
                if before:
                    e_down(s - 1, 1 - b, *before, maybe)
                return now

            e_turn(0, 0)
            now = e_step(0, 0, None)
            e_step(1, 1, now)
            half = FULL // 4
            for lo, hi, maybe in ((0, half, False), (half, SLOTS // 4 - 1, True)):
                with pe.Fori(lo, hi) as i:
                    now = words(4 * i + 1)
                    for n in range(2, 6):
                        now = e_step(4 * i + n, n % 2, now, maybe=maybe)
            now = e_step(SLOTS - 2, 0, words(SLOTS - 3), maybe=True)
            now = e_step(SLOTS - 1, 1, now, last=True, maybe=True)
            e_hturn(SLOTS - 1, 1)
            e_down(SLOTS - 1, 1, *now, True)

        @block.vector
        def _(dve):
            ch = Chain(dve, S["dch"])
            tt, ts, stt = dve.tensor_tensor, dve.tensor_scalar, dve.scalar_tensor_tensor
            dve.wait_ge(S["par_in"], 80)
            lr, li = PAR[:, 0, :], PAR[:, 1, :]
            dve.wait_ge(S["act_small"], 1)
            dt_, lrdt, ang, mag, mag8 = (sm[:, k, :] for k in range(5))
            ch(tt(lrdt, lr, dt_, ALU.mult))
            ch(tt(ang, li, dt_, ALU.mult))
            n_, r_, rh, sn, sh, cs, t_ = sm[:, 5, :], sm[:, 6, :], sm[:, 7, :], sm[:, 8, :], sm[:, 9, :], sm[:, 10, :], sm[:, 11, :]
            ch(ts(n_, ang, INV_2PI, ROUND, ALU.mult, ALU.add))
            ch(ts(n_, n_, ROUND, None, ALU.subtract))
            ch(stt(r_, n_, -PI_HI, ang, ALU.mult, ALU.add))
            ch(stt(r_, n_, -PI_MID, r_, ALU.mult, ALU.add))
            ch(stt(r_, n_, -PI_LO, r_, ALU.mult, ALU.add))
            ch(ts(r_, r_, PI_IN, -PI_IN, ALU.min, ALU.max))
            ch(ts(rh, r_, 0.5, None, ALU.mult))
            dve.memset(t_, 0.0).then_inc(S["c_g1"], 1)
            dve.wait_ge(S["win_in"], 16)
            for k in range(KD):
                ts(w1[:, k, :], w1[:, k, :], gm_sb[:, k:k + 1], None, ALU.mult).then_inc(S["w_scaled"], 1)
            dve.wait_ge(S["act_small"], 5)
            ch(tt(t_, sh, sh, ALU.mult))
            ch(ts(cs, t_, -2.0, 1.0, ALU.mult, ALU.add))

            def cmul(ore, oim, are, aim, bre, bim, ta, tb):
                ch(tt(ta, are, bre, ALU.mult))
                ch(tt(tb, aim, bim, ALU.mult))
                ch(tt(ore, ta, tb, ALU.subtract))
                ch(tt(ta, are, bim, ALU.mult))
                ch(tt(tb, aim, bre, ALU.mult))
                ch(tt(oim, ta, tb, ALU.add))

            def unit(re, im, ore, oim):
                ta, tb = tq[:, 2, 0:PR], tq[:, 3, 0:PR]
                ch(tt(ta, re, re, ALU.mult))
                ch(tt(tb, im, im, ALU.mult))
                ch(tt(ta, ta, tb, ALU.add))
                ch(ts(ta, ta, -0.5, 1.5, ALU.mult, ALU.add))
                ch(tt(ore, re, ta, ALU.mult))
                ch(tt(oim, im, ta, ALU.mult))

            q0, q1 = tq[:, 0, 0:PR], tq[:, 1, 0:PR]
            ch(dve.memset(PW[:, 0, 0, :], 1.0))
            ch(dve.memset(PW[:, 1, 0, :], 0.0))
            ch(tt(PW[:, 0, 1, :], mag, cs, ALU.mult))
            ch(tt(PW[:, 1, 1, :], mag, sn, ALU.mult))
            for lo in (1, 2, 4):
                def bc(a):
                    return PW[:, a, lo:lo + 1, :].to_broadcast([P, lo, PR])
                v0 = tq[:, 0, 0:lo * PR].rearrange("p (d r) -> p d r", r=PR)
                v1 = tq[:, 1, 0:lo * PR].rearrange("p (d r) -> p d r", r=PR)
                cmul(PW[:, 0, lo + 1:2 * lo + 1, :], PW[:, 1, lo + 1:2 * lo + 1, :], PW[:, 0, 1:lo + 1, :], PW[:, 1, 1:lo + 1, :],
                     bc(0), bc(1), v0, v1)
            ch(ts(PW[:, 2, :, :], PW[:, 1, :, :], -1.0, None, ALU.mult))
            den, nr, cr, ci = sm[:, 12, :], sm[:, 13, :], sm[:, 14, :], sm[:, 15, :]
            ch(tt(q0, lr, lr, ALU.mult))
            ch(tt(q1, li, li, ALU.mult))
            ch(tt(q0, q0, q1, ALU.add))
            ch(dve.reciprocal(den, q0))
            ch(ts(nr, PW[:, 0, 1, :], -1.0, None, ALU.add))
            ch(tt(q0, nr, lr, ALU.mult))
            ch(tt(q1, PW[:, 1, 1, :], li, ALU.mult))
            ch(tt(q0, q0, q1, ALU.add))
            ch(tt(cr, q0, den, ALU.mult))
            ch(tt(q0, PW[:, 1, 1, :], lr, ALU.mult))
            ch(tt(q1, nr, li, ALU.mult))
            ch(tt(q0, q0, q1, ALU.subtract))
            ch(tt(ci, q0, den, ALU.mult))
            crb, cib = cr.unsqueeze(2).to_broadcast([P, PR, GC]), ci.unsqueeze(2).to_broadcast([P, PR, GC])
            bt0 = uT[0][:, 0, 0:PR * GC].rearrange("p (r c) -> p r c", c=GC)
            bt1 = uT[0][:, 1, 0:PR * GC].rearrange("p (r c) -> p r c", c=GC)
            cmul(BB[:, 0, :, :], BB[:, 1, :, :], BC[:, 0, :, :], BC[:, 1, :, :], crb, cib, bt0, bt1)
            ure, uim, vre, vim = (sm[:, k, :] for k in range(16, 20))
            unit(cs, sn, ure, uim)
            for k in range(3 + 7):
                cmul(vre, vim, ure, uim, ure, uim, q0, q1)
                unit(vre, vim, ure, uim)
                if k >= 2:
                    ch(dve.tensor_copy(PH[:, 0, k - 2, :], ure))
                    ch(dve.tensor_copy(PH[:, 1, k - 2, :], uim))
            dve.memset(t_, 0.0).then_inc(S["pws_ready"], 1)

            for j in range(L):
                b = j % 2
                dve.wait_ge(S["sq_done"], j + 1)
                dve.tensor_reduce(red[b][:, :], sq[:, :, :].rearrange("p k n -> p n k"), AX, ALU.add).then_inc(S["red_done"], 1)
                dve.wait_ge(S["ss_done"], j + 1)
                ts(rst[b][:, :], pbig[:, 4 + b, 0:NCH], 1.0 / D, EPS, ALU.mult, ALU.add).then_inc(S["var_done"], 1)
                dve.wait_ge(S["std_done"], j + 1)
                ch(dve.reciprocal(rst[b][:, :], std[b][:, :]))
                if j >= 2:
                    dve.wait_ge(S["u_stored"], 16 * (j - 1))
                for cb in range(CB):
                    dve.wait_ge(S["um_done"], CB * j + cb + 1)
                    tt(uT[b][:, cb, :], pbig[:, cb, 0:NCH], rst[b][:, :], ALU.mult).then_inc(S["u_evac"], 1)

            dve.wait_ge(S["tabs_ready"], 1)
            dve.wait_ge(S["u_stored"], 16 * L)
            dve.wait_ge(S["um_done"], CB * L)
            dve.wait_ge(S["mz_zero"], 4)
            NB = 12

            def b_scan(r, b):
                at = [0]

                def lk(ins, n=1):
                    at[0] += 1
                    ins.then_inc(S["dchb"], 1)
                    dve.wait_ge(S["dchb"], NB * r + at[0])
                dve.wait_ge(S["v_done"], r + 1)
                if not early(r):
                    dve.wait_ge(S["y_done"], 2 * r - 2)
                v = pbig[:, 2 * b:2 * b + 2, DECB:NCH]
                wc = WT[:, 0:1, ds(r, 1), :].rearrange("p a o k -> p a (o k)").to_broadcast([P, 2, NP_CH])
                ws = WT[:, 1:2, ds(r, 1), :].rearrange("p a o k -> p a (o k)").to_broadcast([P, 2, NP_CH])
                lk(tt(r1[:, :, :], v, wc, ALU.mult))
                lk(tt(r2[:, :, :], v, ws, ALU.mult))
                lk(tt(z[:, 0, :], r1[:, 0, :], r2[:, 1, :], ALU.add))
                lk(tt(z[:, 1, :], r1[:, 1, :], r2[:, 0, :], ALU.subtract))
                mg = mag8[:, ds(r, 1)].to_broadcast([P, NP_CH])
                lk(dve.tensor_tensor_scan(r1[:, 0, :], mg, z[:, 0, :], 0.0, ALU.mult, ALU.add))
                lk(dve.tensor_tensor_scan(r1[:, 1, :], mg, z[:, 1, :], 0.0, ALU.mult, ALU.add))
                lk(tt(z[:, :, :], r1[:, :, :], wc, ALU.mult))
                lk(tt(r2[:, :, :], r1[:, :, :], ws, ALU.mult))
                lk(tt(Sp[b][:, 0, DECB + 1:NCH + 1], z[:, 0, :], r2[:, 1, :], ALU.subtract))
                lk(tt(Sp[b][:, 1, DECB + 1:NCH + 1], z[:, 1, :], r2[:, 0, :], ALU.add))
                dve.nop().then_inc(S["sp_done"], 1)
                lk(tt(FO[:, :, ds(r, 1), 0:DECB].rearrange("p a o k -> p a (o k)"), pbig[:, 2 * b:2 * b + 2, 0:DECB],
                      F0[:, :, ds(r, 1), :].rearrange("p a o k -> p a (o k)"), ALU.add))
                lk(dve.tensor_copy(FO[:, :, ds(r, 1), DECB:DECB + 1].rearrange("p a o k -> p a (o k)"), Sp[b][:, :, NCH:NCH + 1]))
                dve.nop().then_inc(S["fo_done"], 1)

            def b_y(r):
                for g in range(2):
                    dve.wait_ge(S["y_done"], 2 * r + g + 1)
                    if not early(r, 1):
                        dve.wait_ge(S["gelu_done"], 2 * r - 1 + g)
                    stt(yt[g][:, :], U[:, ds(2 * r + g, 1), :].rearrange("p o k -> p (o k)"), d_sb[:, ds(2 * r + g, 1)],
                        pbig[:, 5 + g, 0:NCH], ALU.mult, ALU.add).then_inc(S["yp_done"], 1)

            b_scan(0, 0)
            b_scan(1, 1)
            b_y(0)
            with dve.Fori(1, PR // 2) as i:
                b_scan(2 * i, 0)
                b_y(2 * i - 1)
                b_scan(2 * i + 1, 1)
                b_y(2 * i)
            b_y(PR - 1)

            dve.wait_ge(S["con_in"], 48)
            dve.wait_ge(S["gelu_done"], G)
            for m, n in enumerate((2, 3, 0, 1)):
                c = slice(n * 512, (n + 1) * 512)
                dve.wait_ge(S["w2_hi"], 2 * m + 1)
                tt(w2L[:, 0:CB - 1, c], w2a[:, :, c], w2H[:, 0:CB - 1, c].bitcast(F32), ALU.subtract).then_inc(S["w2_lo"], 1)
                dve.wait_ge(S["w2_hi"], 2 * m + 2)
                tt(w2L[:, CB - 1:CB, c], w2b[:, :, c], w2H[:, CB - 1:CB, c].bitcast(F32), ALU.subtract).then_inc(S["w2_lo"], 1)

            def c_y_lo(t, b, rows=P):
                dve.wait_ge(S["ys_hi"], t + 1)
                tt(ysL[b][:, :, 0:rows], ys[b][:, :, 0:rows], ysH[b][:, :, 0:rows].bitcast(F32), ALU.subtract).then_inc(S["ys_lo"], 1)

            NC = 12

            def c_mix(t, b, rows=P):
                at = [0]

                def lk(ins):
                    at[0] += 1
                    ins.then_inc(S["dchc"], 1)
                    dve.wait_ge(S["dchc"], NC * t + at[0])
                dve.wait_ge(S[f"xr_in{b}"], 8 * (t - b) + 16)
                if not early(t):
                    dve.wait_ge(S[f"x2_st{b}"], 8 * (t - b))
                    dve.wait_ge(S[f"xn_st{b}"], 8 * (t - b))
                dve.wait_ge(S["sig_done"], 2 * t + 2)
                dve.wait_ge(S["a_done"], 4 * t + 4)
                lk(tt(x2[b][0:rows, :].rearrange("p (a m) -> p a m", a=2), pbig[0:rows, 0:2, :],
                      sg[0:rows, :].rearrange("p (a m) -> p a m", a=2), ALU.mult))
                lk(tt(x2[b][0:rows, :], x2[b][0:rows, :], xr[b][0:rows, :], ALU.add))
                dve.nop().then_inc(S["x2_done"], 1)
                dve.wait_ge(S["ssq_done"], t + 1)
                mean, y_, h_, t2 = nv[0:rows, 0:1], nv[0:rows, 1:2], nv[0:rows, 2:3], nv[0:rows, 3:4]
                lk(ts(mean, ssq[0:rows, ds(t, 1)], 1.0 / D, EPS, ALU.mult, ALU.add))
                lk(ts(nvi[0:rows, 0:1], mean.bitcast(I32), 1, None, ALU.logical_shift_right))
                lk(ts(nvi[0:rows, 1:2], nvi[0:rows, 0:1], -1.0, RSQRT_SEED, ALU.mult, ALU.add))
                lk(ts(h_, mean, -0.5, None, ALU.mult))
                yy = nvi[0:rows, 1:2].bitcast(F32)
                for k in range(3):
                    lk(stt(t2, yy, h_, yy, ALU.mult, ALU.mult))
                    lk(stt(y_, t2, 1.5, yy, ALU.add, ALU.mult))
                    yy = y_
                stt(xn[b][0:rows, :], x2[b][0:rows, :], y_, gf_b[0:rows, :], ALU.mult, ALU.mult).then_inc(S["xn_done"], 1)
            c_y_lo(0, 0)
            c_y_lo(1, 1)
            c_mix(0, 0)
            with dve.Fori(1, TF // 2) as i:
                c_y_lo(2 * i, 0)
                c_mix(2 * i - 1, 1)
                c_y_lo(2 * i + 1, 1)
                c_mix(2 * i, 0)
            c_y_lo(TF, 0, LAST)
            c_mix(TF - 1, 1)
            c_mix(TF, 0, LAST)

            dch = Chain(dve, S["dchd"])
            dve.wait_ge(S["d_iota"], 4)
            n3 = [P, TT, 4]

            def b4(ap):
                return ap.unsqueeze(2).to_broadcast(n3)

            def first_max(oh, src, mx, ta):
                dch(dve.tensor_reduce(mx, src, AX, ALU.max))
                dch(tt(ta, src, b4(mx), ALU.is_equal))
                dch(tt(ta, ta, desc[:, :].unsqueeze(1).to_broadcast(n3), ALU.mult))
                dch(dve.tensor_reduce(R1[11][:, :], ta, AX, ALU.max))
                dch(tt(oh, ta, b4(R1[11][:, :]), ALU.is_equal))

            dch(dve.memset(logit[LAST:P, TF, :], 0.0))
            lg = logit[:, :, 0:NG]
            ohg, oh1, oh2 = R3[2][:, :, :], R3[3][:, :, :], R3[4][:, :, :]
            gm = R1[0][:, :]
            first_max(ohg, lg, gm, R3[5][:, :, :])
            dch(tt(R3[0][:, :, :], lg, b4(gm), ALU.subtract))
            dve.nop().then_inc(S["exp_in"], 1)
            for g in range(NG):
                dch(tt(L4[:, :, g, :], logit[:, :, NG + g * NEG:NG + (g + 1) * NEG], ohg[:, :, g:g + 1].to_broadcast(n3), ALU.mult))
            le = R3[6][:, :, :]
            dch(dve.tensor_reduce(le, L4[:, :, :, :].rearrange("p t g e -> p t e g"), AX, ALU.add))
            m1, m2 = R1[1][:, :], R1[2][:, :]
            first_max(oh1, le, m1, R3[5][:, :, :])
            dch(stt(R3[7][:, :, :], oh1, -1e30, le, ALU.mult, ALU.add))
            first_max(oh2, R3[7][:, :, :], m2, R3[5][:, :, :])
            dch(tt(R1[4][:, :], m2, m1, ALU.subtract))
            dve.nop().then_inc(S["exp_in"], 1)
            dve.wait_ge(S["exp_d"], 2)
            sg_, gw, w1_ = R1[3][:, :], R1[6][:, :], R1[7][:, :]
            dch(dve.tensor_reduce(sg_, R3[1][:, :, :], AX, ALU.add))
            dch(ts(w1_, R1[5][:, :], 1.0, None, ALU.add))
            dch(tt(gw, sg_, w1_, ALU.mult))
            dch(dve.reciprocal(cw[:, 0, :], gw))
            dch(tt(cw[:, 1, :], cw[:, 0, :], R1[5][:, :], ALU.mult))
            for EX, oh in ((E1, oh1), (E2, oh2)):
                for g in range(NG):
                    dch(tt(EX[:, :, g, :], oh, ohg[:, :, g:g + 1].to_broadcast(n3), ALU.mult))
                dch(dve.memset(EX[LAST:P, TF, :, :], 0.0))
            dch(tt(EE[:, :, :, :], E1[:, :, :, :], E2[:, :, :, :], ALU.add))
            dve.nop().then_inc(S["d_ready"], 1)
            dch(dve.memset(rst_t[:, :, :], 1.0))
            dch(dve.memset(rst_t[:, :, 0:1], 0.0))
            dve.wait_ge(S["cnt_done"], 1)
            dch(dve.tensor_copy(cnt[:, :, :], pbig[:, 1, 0:TT * NE].rearrange("p (t e) -> p e t", e=NE)))
            flat = lambda a: a[:, :, :].rearrange("p e t -> p (e t)")
            dch(dve.tensor_tensor_scan(flat(inc_t), flat(rst_t), flat(cnt), 0.0, ALU.mult, ALU.add))
            dch(tt(exc_t[:, :, :], inc_t[:, :, :], cnt[:, :, :], ALU.subtract))
            ne, nti, ntf, cum, bas = tei[:, 0, :], tei[:, 1, :], te[:, 1, :], te[:, 2, :], te[:, 3, :]
            dch(ts(ne, inc_t[:, :, TT - 1], float(P - 1), None, ALU.add))
            dch(ts(nti, ne, 7, None, ALU.logical_shift_right))
            dch(ts(ntf, nti, 1.0, None, ALU.max))
            dch(dve.memset(te[:, 0, :], 1.0))
            dch(dve.tensor_tensor_scan(cum, te[:, 0, :], ntf, 0.0, ALU.mult, ALU.add))
            beg = te[:, 4, :]
            dch(tt(beg, cum, ntf, ALU.subtract))
            dch(ts(bas, beg, float(P), 1.0, ALU.mult, ALU.add))
            dch(tt(exc_t[:, :, :], exc_t[:, :, :], bas.unsqueeze(2).to_broadcast([P, NE, TT]), ALU.add))
            dch(tt(spos[:, :, :], pbig[:, 0, 0:TT * NE].rearrange("p (t e) -> p t e", e=NE), exc_t[:, :, :].rearrange("p e t -> p t e"), ALU.add))
            for c, EX in enumerate((E1, E2)):
                ef = EX[:, :, :, :].rearrange("p t g e -> p t (g e)")
                dch(tt(ef, ef, spos[:, :, :], ALU.mult))
                dch(dve.tensor_reduce(R1[8 + c][:, :], ef, AX, ALU.add))
                dch(ts(slot_i[:, c, :], R1[8 + c][:, :], -1.0, None, ALU.add))
                dch(ts(si[:, c, 0, :], slot_i[:, c, :], 7, None, ALU.arith_shift_right))
                dch(ts(si[:, c, 1, :], slot_i[:, c, :], P - 1, None, ALU.bitwise_and))
                dch(dve.tensor_copy(vals[:, c, :, 0], tokid[:, :]))
                dch(dve.tensor_copy(vals[:, c, :, 1], cw[:, c, :]))
            dch(dve.tensor_copy(sf[:, :, :, :], si[:, :, :, :]))
            for n in range(2 * TT):
                c, t = n % 2, n // 2
                if n >= 4:
                    dve.wait_ge(S["tbl_done"], n - 3)
                dch(ts(oh_lo[n % 4][:, :], iot[:, :], sf[:, c, 1, t:t + 1], None, ALU.is_equal))
                stt(oh_hi[n % 4][:, :, :], iot[:, 0:SLOTS].unsqueeze(1).to_broadcast([P, 2, SLOTS]), sf[:, c, 0, t:t + 1],
                    vals[:, c, t, :].unsqueeze(2).to_broadcast([P, 2, SLOTS]), ALU.is_equal, ALU.mult).then_inc(S["one_hot_done"], 1)
            dch(tt(cmpe[:, :, :], cum[0:1, :].unsqueeze(1).to_broadcast([1, SLOTS, NE]), iot[0:1, 0:SLOTS].unsqueeze(2).to_broadcast([1, SLOTS, NE]), ALU.is_le))
            e_ = eof[:, 0, :]
            dch(dve.tensor_reduce(e_, cmpe[:, :, :], AX, ALU.add))
            dch(ts(e_, e_, float(NE - 1), None, ALU.min))
            def word(c):
                return ctrl[:, c:c + SLOTS]
            dch(dve.tensor_copy(word(C_EXP), e_))
            dch(ts(word(C_AT), word(C_EXP), 1, None, ALU.bitwise_and))
            f_, n_ = eof[:, 1, :], eof[:, 2, :]
            dch(tt(cmpe[:, :, :], beg[0:1, :].unsqueeze(1).to_broadcast([1, SLOTS, NE]), iot[0:1, 0:SLOTS].unsqueeze(2).to_broadcast([1, SLOTS, NE]), ALU.is_equal))
            dch(dve.tensor_reduce(f_, cmpe[:, :, 0:NE - 1], AX, ALU.add))
            dch(ts(n_, word(C_AT), -float(EW), float(EW - SKIP), ALU.mult, ALU.add))
            dch(tt(n_, n_, f_, ALU.mult))
            dch(ts(word(C_NEXT), n_, float(SKIP), None, ALU.add))
            dch(ts(n_, iot[0:1, 0:SLOTS], cum[0:1, NE - 1:NE], float(SKIP - EW), ALU.is_ge, ALU.mult))
            dch(stt(word(C_AT), word(C_AT), float(EW), n_, ALU.mult, ALU.add))
            dve.wait_ge(S["tbl_done"], 2 * TT)
            held = pbig[:, 2, 0:SLOTS]
            dch(ts(token_of[:, :], held, 1.0, -1.0, ALU.max, ALU.add))
            dch(ts(rowf[:, 0, :], held, 0.0, spare[:, 0:1], ALU.is_equal, ALU.mult))
            dch(stt(rowf[:, 1, :], held, -1.0, rowf[:, 0, :], ALU.add, ALU.add))
            dch(dve.tensor_copy(sum_of[:, :], rowf[:, 1, :]))
            dch(dve.tensor_copy(cw_of[:, :], pbig[:, 2, SLOTS:2 * SLOTS]))
            dve.nop().then_inc(S["ctl_done"], 1)

            def e_x_lo(s, b):
                for n in range(2):
                    dve.wait_ge(S["xgt_evac"], 2 * s + n + 1)
                    if n == 0 and not early(s):
                        dve.wait_ge(S["gu_done"], s - 1)
                    tt(xgL[b][:, 4 * n:4 * n + 4, :], pbig[:, 4 + n, :].rearrange("p (a m) -> p a m", a=4),
                       xgH[b][:, 4 * n:4 * n + 4, :].bitcast(F32), ALU.subtract).then_inc(S["xgt_lo"], 1)

            def e_h(s, b):
                dve.wait_ge(S["sl_done"], s + 1)
                if not early(s):
                    dve.wait_ge(S["ht_done"], s - 1)
                tt(hh[b][:, :], sl[:, :], pbig[:, 6, DE:2 * DE], ALU.mult).then_inc(S["h_done"], 1)

            def e_ht(s, b):
                dve.wait_ge(S["ht_done"], s + 1)
                if not early(s):
                    dve.wait_ge(S["dn_done"], s)
                ht = pbig[:, 7, 0:2 * P].rearrange("p (a m) -> p a m", a=2)
                dve.tensor_copy(hTH[b][:, :, :], ht).then_inc(S["dche"], 1)
                dve.wait_ge(S["dche"], s + 1)
                tt(hTL[b][:, :, :], ht, hTH[b][:, :, :].bitcast(F32), ALU.subtract).then_inc(S["ht_evac"], 1)

            def e_word(s):
                return dve.value_load(ctrl[0:1, ds(C_NEXT + s, 1)], min_val=0, max_val=EW)

            def e_split(s, to, part):
                with dve.If(to != SKIP):
                    e = dve.value_load(ctrl[0:1, ds(C_EXP + s, 1)], min_val=0, max_val=NE - 1)
                    for c in (range(UP_CUTS), range(UP_CUTS, CUTS))[part]:
                        dve.wait_ge(S["hi_split"], e * CUTS + (CUTS + c + 1))
                        dve.wait_ge(S["ctl_done"], 1)
                        w = ds(to + c * CW, CW)
                        tt(WL[:, w], WR[:, w], WH[:, w].bitcast(F32), ALU.subtract).then_inc(S["lo_split"], 1)

            for c in range(CUTS):
                dve.wait_ge(S["hi_split"], c + 1)
                w = ds(c * CW, CW)
                tt(WL[:, w], WR[:, w], WH[:, w].bitcast(F32), ALU.subtract).then_inc(S["lo_split"], 1)
            e_x_lo(0, 0)

            def e_step(s, b, to, ahead=True, last=False):
                then = None
                if not last:
                    e_split(s, to, 0)
                e_h(s, b)
                if not last:
                    e_x_lo(s + 1, 1 - b)
                    if ahead:
                        then = e_word(s + 1)
                e_ht(s, b)
                if not last:
                    e_split(s, to, 1)
                return then

            to = e_step(0, 0, e_word(0))
            e_step(1, 1, to, ahead=False)
            with dve.Fori(0, SLOTS // 4 - 1) as i:
                to = e_word(4 * i + 2)
                for n in range(2, 6):
                    to = e_step(4 * i + n, n % 2, to, ahead=n < 5)
            e_step(SLOTS - 2, 0, e_word(SLOTS - 2), ahead=False)
            e_step(SLOTS - 1, 1, None, last=True)

            def f_scale(t, b, rows=P):
                dve.wait_ge(S["f_std"], t + 1)
                dve.reciprocal(fnv[0:rows, 1, b:b + 1], fnv[0:rows, 0, b:b + 1]).then_inc(S["dchf"], 1)
                dve.wait_ge(S["dchf"], t + 1)
                if not early(t, NF):
                    dve.wait_ge(S[f"f_st{b}"], 16 * (t // NF) if isinstance(t, int) else 4 * (t - b))
                stt(fo[b][0:rows, :], fx[b][0:rows, :], fnv[0:rows, 1, b:b + 1], gl_b[0:rows, :], ALU.mult, ALU.mult).then_inc(S["f_out"], 1)
            for b in range(NF):
                f_scale(b, b)
            with dve.Fori(1, TF // NF) as i:
                for b in range(NF):
                    f_scale(NF * i + b, b)
            f_scale(TF, 0, LAST)


def kernel(**inputs):
    import numpy as np
    import concourse.bacc as bacc
    from concourse.bass_utils import run_bass_kernel_spmd as run

    a = {k: np.asarray(v) for k, v in inputs.items()}

    def order(p, s):
        rows = np.concatenate([s.reshape(NCH - NP_CH, L, -1), p.reshape(NP_CH, L, -1)], 0)
        return np.ascontiguousarray(rows.transpose(1, 0, 2))

    def states(x):
        x = x.reshape(x.shape[:-2] + (PR, 2, ST))
        x = np.moveaxis(x, (-2, -1, -3), (0, 1, 2))
        x = x.reshape((P, PR) + x.shape[3:])
        return x

    x = order(a["x_prompt"], a["x_sample"])
    x_rows = x.reshape(NT, D)
    x_cols = x.reshape(L, NCH, KD, P).transpose(0, 3, 2, 1)
    s0 = np.stack([states(a["state_ssm_re"]), states(a["state_ssm_im"])], 1)
    step = np.broadcast_to(a["ssm_log_step"][:, None], (G, ST))
    par = np.stack([states(v) for v in (a["ssm_lambda_re"], a["ssm_lambda_im"], step)], 1)

    def chans(v):
        return v.reshape(PR, 2, ST, GC).transpose(1, 2, 0, 3).reshape(P, PR, GC)

    bc = np.stack([chans(a["ssm_b_re"]), chans(a["ssm_b_im"]),
                   chans(a["ssm_c_re"].transpose(0, 2, 1)), chans(a["ssm_c_im"].transpose(0, 2, 1))], 1)
    dd = np.broadcast_to(a["ssm_d"].T[None], (L, GC, G)).reshape(P, G)
    route = np.concatenate([a["moe_router_group"][0], a["moe_router_expert"][0]], 1)
    gu = np.stack([a["moe_w_gate"][0], a["moe_w_up"][0]], 2)
    arrays = {
        "x_rows": x_rows, "x_cols": x_cols, "s0": s0, "par": par, "bc": bc, "dd": dd,
        "gmix": a["norm_mix"][0].reshape(KD, P).T, "gffn": a["norm_ffn"][0], "gfin": a["norm_final"],
        "w_in": a["ssm_w_in"].reshape(KD, P, W).transpose(1, 0, 2),
        "w_out": a["ssm_w_out"].reshape(CB, P, 2 * D).transpose(1, 0, 2),
        "route": route.reshape(KD, P, 20).transpose(1, 0, 2),
        "w_gu": gu.reshape(NE, KD, P, 2 * DE).transpose(0, 2, 1, 3).reshape(NE, P, KD * 2 * DE),
        "w_dn": a["moe_w_down"][0].reshape(NE, DE // P, P, D).transpose(0, 2, 1, 3).reshape(NE, P, DE // P * D),
    }
    arrays = {k: np.ascontiguousarray(v) for k, v in arrays.items()}
    nc = bacc.Bacc("TRN2", target_bir_lowering=False, num_devices=1)
    ins = {k: nc.dram_tensor(f"in_{k}", v.shape, mybir.dt.from_np(v.dtype), kind="ExternalInput").ap()
           for k, v in arrays.items()}
    y_out = nc.dram_tensor("out_y", (NT, D), F32, kind="ExternalOutput").ap()
    st_out = nc.dram_tensor("out_st", (P, 2, PR, DECB + 1), F32, kind="ExternalOutput").ap()
    hybrid_kernel(nc, ins["x_rows"], ins["x_cols"], ins["s0"], ins["par"], ins["bc"], None, ins["dd"], ins["gmix"],
                  ins["gffn"], ins["gfin"], ins["w_in"], ins["w_out"], ins["route"], ins["w_gu"], ins["w_dn"], y_out, st_out)
    r = run(nc, [{f"in_{k}": v for k, v in arrays.items()}], core_ids=[0])
    y = np.asarray(r.results[0]["out_y"]).reshape(L, NCH, D).transpose(1, 0, 2)
    st = np.asarray(r.results[0]["out_st"]).reshape(2, ST, 2, PR, DECB + 1)
    st = st.transpose(2, 4, 3, 0, 1).reshape(2, DECB + 1, G, ST)
    c = np.ascontiguousarray
    return (c(y[DECB:].reshape(1, SEQ, D)), c(y[:DECB].reshape(DECB, DECS, D)),
            c(st[0, DECB:]), c(st[1, DECB:]), c(st[0, :DECB]), c(st[1, :DECB]), None)
```

```python
from contextlib import ExitStack

import concourse.bass as bass
from concourse import mybir

F32 = mybir.dt.float32
I32 = mybir.dt.int32
U32 = mybir.dt.uint32
F32R = mybir.dt.float32r
ALU = mybir.AluOpType
ACT = mybir.ActivationFunctionType
AX = mybir.AxisListType.X
ds = bass.ds

P = 128
D = 1024
SEQ, DECB, DECS = 2048, 8, 8
L = 8
NCH = DECB + SEQ // L
NP_CH = SEQ // L
NT = NCH * L
KD = D // P
W = 512
G, GC, ST = 32, 16, 64
PR = G // 2
CB = W // P
TT = -(-NT // P)
TF = NT // P
LAST = NT - TF * P
NG, NEG, NE = 4, 4, 16
DE = 256
SLOTS = (2 * NT + NE * (P - 1)) // P
EPS = 1e-6
INV_2PI = 0.15915494309189535
ROUND = 12582912.0
PI_HI, PI_MID, PI_LO = 6.28125, 0.0019350051879882812, 3.0199159819e-07
PI_IN = 3.1415925
RSQRT_SEED = 1597463007.0
EW = KD * 2 * DE + (DE // P) * D
CUTS, UP_CUTS = 3, 2
CW = EW // CUTS
FULL = 2 * NT // P
C_EXP, C_AT, C_NEXT, C_USED = (i * SLOTS for i in range(4))
SKIP = 1
NF = 4


def hybrid_kernel(nc, x_rows, x_cols, s0, par, b_in, c_in, d_in, gmix, gffn, gfin, w_in, w_out, w_route,
                  w_gu, w_dn, y_out, st_out):
    uD = nc.dram_tensor("u_by_step", (L, P, CB, NCH), F32, kind="Internal").ap()
    yD = nc.dram_tensor("y_by_block", (CB, P, 8, NCH), F32, kind="Internal").ap()
    x2D = nc.dram_tensor("x_sums", (NT + P, D), F32, kind="Internal").ap()
    xnD = nc.dram_tensor("x_normed", (NT, D), F32, kind="Internal").ap()

    outer = ExitStack()
    with outer:
        scope = [outer]

        def sb(name, shape, dt=F32):
            return scope[0].enter_context(nc.sbuf_tensor(name, shape, dt))

        def sem(name):
            return outer.enter_context(nc.semaphore(name))

        def cut(ap, n):
            return ap[0:n]

        pbig = outer.enter_context(nc.psum_tensor("pbig", [P, 8, 512], F32))

        ident = sb("ident", [P, P])
        ones = sb("ones", [P, P])
        upper = sb("upper", [P, P])
        gf_b = sb("gf_b", [P, D])
        gl_b = sb("gl_b", [P, D])
        wr_sb = sb("wr_sb", [P, KD, 20])
        logit = sb("logit", [P, TT, 20])
        token_of = sb("token_of", [P, SLOTS], U32)
        sum_of = sb("sum_of", [P, SLOTS], U32)
        cw_of = sb("cw_of", [P, SLOTS])
        ctrl = sb("ctrl", [1, 3 * SLOTS + 1], I32)
        epsc = sb("epsc", [P, 1])

        umix = ExitStack()
        scope[0] = umix
        U = sb("U", [P, G, NCH])
        FO = sb("FO", [P, 2, PR, DECB + 1])
        mix = ExitStack()
        scope[0] = mix
        PAR = sb("PAR", [P, 3, PR])
        s0_sb = sb("s0_sb", [P, 2, PR, DECB])
        BC = sb("BC", [P, 4, PR, GC])
        d_sb = sb("d_sb", [P, G])
        gm_sb = sb("gm_sb", [P, KD])
        sm = sb("sm", [P, 10, PR])
        PW = sb("PW", [P, 3, L + 1, PR])
        PH = sb("PH", [P, 2, 8, PR])
        tq = sb("tq", [P, 2, PR * 4])
        BB = sb("BB", [P, 2, PR, GC])
        WT = sb("WT", [P, 2, PR, NP_CH])
        E = sb("E", [P, 2, PR, L * GC])
        CL = sb("CL", [P, 2, PR, (L + 1) * GC])
        T = sb("T", [P, G, L * GC])
        F0 = sb("F0", [P, 2, PR, DECB])
        aonly = ExitStack()
        scope[0] = aonly
        xT = [sb(f"xT{b}", [P, KD, NCH]) for b in range(2)]
        uT = [sb(f"uT{b}", [P, CB, NCH]) for b in range(2)]
        sq = sb("sq", [P, KD, NCH])
        AN = uT[1][:, :, :].rearrange("p b k -> p (b k)")[:, 0:5 * 9 * PR].rearrange("p (f l r) -> p f l r", f=5, l=9)
        red = [sb(f"red{b}", [P, NCH]) for b in range(2)]
        rst = [sb(f"rst{b}", [P, NCH]) for b in range(2)]
        w1 = sb("w1", [P, KD, W])
        p1 = sb("p1", [P, (L + 1) * PR * GC // 2])
        Kp = [sb(f"Kp{b}", [GC, 8, L * GC]) for b in range(2)]
        kd = sb("kd", [GC, 8, GC])
        aonly.close()
        bonly = ExitStack()
        scope[0] = bonly
        r1 = [sb(f"r1{b}", [P, 2, NP_CH]) for b in range(2)]
        r2 = [sb(f"r2{b}", [P, 2, NP_CH]) for b in range(2)]
        z = [sb(f"z{b}", [P, 2, NP_CH]) for b in range(2)]
        ES = [sb(f"ES{b}", [P, 2, P]) for b in range(2)]
        NS = [sb(f"NS{b}", [P, 2, P]) for b in range(2)]
        TS = [sb(f"TS{b}", [P, 2, P]) for b in range(2)]
        MZ = [sb(f"MZ{b}", [P, 2, 2, P]) for b in range(2)]
        Sp = [sb(f"Sp{b}", [P, 2, NCH + 1]) for b in range(2)]
        w2 = sb("w2", [P, CB, 2 * D])
        bonly.close()
        mix.close()

        cst = ExitStack()
        scope[0] = cst
        w2H = sb("w2H", [P, CB, 2 * D], F32R)
        w2L = sb("w2L", [P, CB, 2 * D], F32R)
        ysH = [sb(f"ysH{b}", [P, CB, P], F32R) for b in range(2)]
        ysL = [sb(f"ysL{b}", [P, CB, P], F32R) for b in range(2)]
        ys = [sb(f"ys{b}", [P, CB, P]) for b in range(2)]
        xr = [sb(f"xr{b}", [P, D]) for b in range(2)]
        sg = sb("sg", [P, D])
        x2 = [sb(f"x2{b}", [P, D]) for b in range(2)]
        xn = [sb(f"xn{b}", [P, D]) for b in range(2)]
        junk = sb("junk", [P, D])
        xnT = sb("xnT", [P, KD, P])
        ssq = sb("ssq", [P, TT])
        nv = sb("nv", [P, 8])
        nvi = sb("nvi", [P, 2], I32)
        cst.close()
        umix.close()

        wst = ExitStack()
        scope[0] = wst
        WR = sb("WR", [P, 2 * EW])
        WH = sb("WH", [P, 2 * EW], F32R)
        WL = sb("WL", [P, 2 * EW], F32R)

        dst = ExitStack()
        scope[0] = dst
        R3 = [sb(f"R3{i}", [P, TT, 4]) for i in range(10)]
        R1 = [sb(f"R1{i}", [P, TT]) for i in range(12)]
        L4 = sb("L4", [P, TT, NG, NEG])
        E1 = sb("E1", [P, TT, NG, NEG])
        E2 = sb("E2", [P, TT, NG, NEG])
        EE = sb("EE", [P, TT, NG, NEG])
        cnt = sb("cnt", [P, NE, TT])
        inc_t = sb("inc_t", [P, NE, TT])
        exc_t = sb("exc_t", [P, NE, TT])
        rst_t = sb("rst_t", [P, NE, TT])
        spos = sb("spos", [P, TT, NE])
        te = sb("te", [P, 6, NE])
        tei = sb("tei", [P, 2, NE], I32)
        desc = sb("desc", [P, 4])
        iot = sb("iot", [P, P])
        tokid = sb("tokid", [P, TT])
        si = sb("si", [P, 2, 2, TT], I32)
        sf = sb("sf", [P, 2, 2, TT])
        oh_lo = sb("oh_lo", [P, 2, TT, P])
        oh_hi = sb("oh_hi", [P, 2, TT, 2, SLOTS])
        cw = sb("cw", [P, 2, TT])
        slot_i = sb("slot_i", [P, 2, TT], I32)
        spare = sb("spare", [P, 1])
        rowf = sb("rowf", [P, 2, SLOTS])
        cmpe = oh_hi[0:1, 0, 0:SLOTS * NE // (2 * SLOTS), :, :].rearrange("p t a s -> p (t a s)").rearrange("p (s e) -> p s e", e=NE)
        eof = sb("eof", [1, 6, SLOTS])
        dst.close()

        est = ExitStack()
        scope[0] = est
        xg = [sb(f"xg{b}", [P, D]) for b in range(2)]
        xgH = [sb(f"xgH{b}", [P, KD, P], F32R) for b in range(2)]
        xgL = [sb(f"xgL{b}", [P, KD, P], F32R) for b in range(2)]
        sl = sb("sl", [P, DE])
        hh = [sb(f"hh{b}", [P, DE]) for b in range(2)]
        hTH = [sb(f"hTH{b}", [P, 2, P], F32R) for b in range(2)]
        hTL = [sb(f"hTL{b}", [P, 2, P], F32R) for b in range(2)]
        yo = [sb(f"yo{b}", [P, D]) for b in range(2)]
        est.close()
        wst.close()
        est = ExitStack()
        scope[0] = est
        fx = [sb(f"fx{b}", [P, D]) for b in range(NF)]
        fo = [sb(f"fo{b}", [P, D]) for b in range(NF)]
        fss = sb("fss", [P, NF])
        fnv = sb("fnv", [P, 2, NF])
        fj = sb("fj", [P, D])
        est.close()

        names = """par_in win_in con_in c_g1 c_pool dch w_scaled act_small pws_ready pool_chain cl_ready tabs_ready
            x_in0 x_in1 sq_done red_done ss_done var_done std_done um_done u_evac u_stored u_in
            k_done k_evac t_in t_zero tr_done mz_done v_done v_used es_done cp_done z_done scan_done turned_on sp_done k_full y_done gelu_done fo_done
            y_stored y_in dchb mz_zero st_stored
            wout_in w2_hi w2_lo ys_done ys_hi ys_lo a_done sig_done x2_done xn_done xr_in0 xr_in1 x2_st0 x2_st1 xn_st0 xn_st1 xt_done xt_evac rl_done rl_evac ssq_done dchc
            dchd dche exp_d cnt_done one_hot_done tbl_done ctl_done d_iota d_ready exp_in
            gat0 gat1 xgt_done xgt_evac xgt_lo gu_done h_done sl_done ht_done ht_evac hi_split lo_split dn_done dn_evac wts
acc_done spare_set f_in0 f_in1 f_in2 f_in3 f_sq f_out f_st0 f_st1 f_st2 f_st3 dchf f_std""".split()
        S = {n: sem(n) for n in names}
        block = outer.enter_context(nc.Block())

        def steps(eng, n, step):
            step(0, 0)
            step(1, 1)
            with eng.Fori(1, n // 2) as i:
                step(2 * i, 0)
                step(2 * i + 1, 1)

        def early(t, n=2):
            return isinstance(t, int) and t < n

        def used(eng, t):
            return eng.value_load(ctrl[0:1, ds(C_AT + t, 1)], min_val=0, max_val=EW) != SKIP

        class Chain:
            def __init__(self, eng, s):
                self.eng, self.s, self.n = eng, s, 0

            def __call__(self, ins):
                self.n += 1
                ins.then_inc(self.s, 1)
                self.eng.wait_ge(self.s, self.n)

        @block.sync
        def _(sp):
            for dst_, src in ((PAR[:, :, :], par), (s0_sb[:, :, :, :], s0), (BC[:, :, :, :], b_in),
                              (d_sb[:, :], d_in), (gm_sb[:, :], gmix)):
                sp.dma_start(dst_, src).then_inc(S["par_in"], 16)
            sp.dma_start(w1[:, :, :], w_in).then_inc(S["win_in"], 16)
            for j in range(2):
                sp.dma_start(xT[j][:, :, :], x_cols[j]).then_inc(S[f"x_in{j}"], 16)
            sp.dma_start(gf_b[:, :], gffn.partition_broadcast(P)).then_inc(S["con_in"], 16)
            sp.dma_start(gl_b[:, :], gfin.partition_broadcast(P)).then_inc(S["con_in"], 16)
            sp.dma_start(wr_sb[:, :, :], w_route).then_inc(S["con_in"], 16)
            for j in range(L):
                sp.wait_ge(S["u_evac"], CB * (j + 1))
                if j + 2 < L:
                    sp.wait_ge(S["sq_done"], j + 1)
                    sp.dma_start(xT[j % 2][:, :, :], x_cols[j + 2]).then_inc(S[f"x_in{j % 2}"], 16)
                sp.dma_start(uD[j], uT[j % 2][:, :, :]).then_inc(S["u_stored"], 16)
                sp.wait_ge(S["u_stored"], 16 * (j + 1))
                for cb in range(CB):
                    sp.dma_start(U[j * GC:(j + 1) * GC, cb * 8:(cb + 1) * 8, :],
                                 uD[j].rearrange("(g c) b k -> b c g k", c=GC)[cb]).then_inc(S["u_in"], 16)
                if j >= L - 4:
                    n = j - (L - 4)
                    sp.wait_ge(S["k_full"], n + 1)
                    sp.wait_ge(S["t_zero"], 1)
                    for i in range(L):
                        sp.dma_start(T[i * GC:(i + 1) * GC, n * 8:(n + 1) * 8, i * GC:L * GC],
                                     Kp[n % 2][:, :, 0:(L - i) * GC]).then_inc(S["t_in"], 16)
            sp.wait_ge(S["um_done"], CB * L)
            sp.wait_ge(S["tabs_ready"], 1)
            sp.wait_ge(S["t_in"], 16 * L * 4)
            sp.dma_start(w2[:, :, :], w_out).then_inc(S["wout_in"], 16)
            for cb in range(CB):
                sp.wait_ge(S["gelu_done"], 8 * (cb + 1))
                sp.dma_start(yD[cb], U[:, cb * 8:(cb + 1) * 8, :]).then_inc(S["y_stored"], 16)
                if cb == CB - 1:
                    sp.wait_ge(S["fo_done"], 2 * PR)
                    sp.wait_ge(S["y_done"], G)
                sp.wait_ge(S["y_stored"], 16 * (cb + 1))
                for g in range(8):
                    sp.dma_start(U[g * GC:(g + 1) * GC, cb * 8:(cb + 1) * 8, :],
                                 yD[cb].rearrange("(i c) g k -> g c i k", c=GC)[g]).then_inc(S["y_in"], 16)
            sp.dma_start(st_out, FO[:, :, :, :]).then_inc(S["st_stored"], 16)

            def c_load(t, b, rows=P):
                if not early(t):
                    sp.wait_ge(S["x2_done"], t - 1)
                sp.dma_start(cut(xr[b], rows)[:, :], x_rows[ds(t * P, rows), :]).then_inc(S[f"xr_in{b}"], 16)

            def c_store(t, b, rows=P):
                sp.wait_ge(S["x2_done"], t + 1)
                sp.dma_start(x2D[ds(t * P, rows), :], cut(x2[b], rows)[:, :]).then_inc(S[f"x2_st{b}"], 16)
                sp.wait_ge(S["xn_done"], t + 1)
                sp.dma_start(xnD[ds(t * P, rows), :], cut(xn[b], rows)[:, :]).then_inc(S[f"xn_st{b}"], 16)

            c_load(0, 0)
            c_load(1, 1)
            sp.dma_start(x2D[NT:NT + P, :], gl_b[:, :]).then_inc(S["spare_set"], 16)
            c_store(0, 0)
            c_load(2, 0)
            c_store(1, 1)
            c_load(3, 1)
            with sp.Fori(1, TF // 2 - 1) as i:
                c_store(2 * i, 0)
                c_load(2 * i + 2, 0)
                c_store(2 * i + 1, 1)
                c_load(2 * i + 3, 1)
            c_store(TF - 2, 0)
            c_load(TF, 0, LAST)
            c_store(TF - 1, 1)
            c_store(TF, 0, LAST)

            sp.wait_ge(S["d_iota"], 4)
            for e in range(NE):
                if e >= 1:
                    sp.wait_ge(S["wts"], 32 * e)
                if e >= 2:
                    sp.wait_ge(S["lo_split"], CUTS * (e - 1))
                at = e % 2 * EW
                sp.dma_start(WR[:, at:at + KD * 2 * DE], w_gu[e]).then_inc(S["wts"], 16)
                sp.dma_start(WR[:, at + KD * 2 * DE:at + EW], w_dn[e]).then_inc(S["wts"], 16)

            def f_load(t, b, rows=P):
                sp.dma_start(cut(fx[b], rows)[:, :], x2D[ds(t * P, rows), :]).then_inc(S[f"f_in{b}"], 16)

            def f_store(t, b, rows=P):
                sp.wait_ge(S["f_out"], t + 1)
                sp.dma_start(y_out[ds(t * P, rows), :], cut(fo[b], rows)[:, :]).then_inc(S[f"f_st{b}"], 16)

            used = sp.value_load(ctrl[0:1, C_USED:C_USED + 1], min_val=FULL, max_val=SLOTS)
            sp.wait_ge(S["acc_done"], used * 16)
            for b in range(NF):
                f_load(b, b)
            with sp.Fori(0, TF // NF - 1) as i:
                for b in range(NF):
                    f_store(NF * i + b, b)
                    f_load(NF * i + (b + NF), b)
            f_store(TF - NF, 0)
            f_load(TF, 0, LAST)
            for b in range(1, NF):
                f_store(TF - NF + b, b)
            f_store(TF, 0, LAST)
            for b in range(NF):
                sp.wait_ge(S[f"f_st{b}"], 16 * (TF // NF + (b == 0)))

        @block.gpsimd
        def _(pool):
            ch = Chain(pool, S["pool_chain"])
            ch(pool.memset(ident[:, :], 0.0))
            ch(pool.affine_select(out=ident[:, :], in_=ident[:, :], compare_op=ALU.not_equal, fill=1.0, base=0,
                                  pattern=[[-1, P]], channel_multiplier=1))
            ch(pool.memset(epsc[:, :], EPS))
            pool.memset(ones[:, :], 1.0).then_inc(S["c_pool"], 1)
            ch(pool.memset(upper[:, :], 1.0))
            ch(pool.affine_select(out=upper[:, :], in_=upper[:, :], compare_op=ALU.is_gt, fill=0.0, base=0,
                                  pattern=[[1, P]], channel_multiplier=-1))
            pool.memset(T[:, :, :], 0.0).then_inc(S["t_zero"], 1)
            pool.wait_ge(S["pws_ready"], 1)

            def cmul(ore, oim, are, aim, bre, bim, ta, tb):
                ch(pool.tensor_tensor(ta, are, bre, ALU.mult))
                ch(pool.tensor_tensor(ore, aim, bim, ALU.mult))
                ch(pool.tensor_tensor(ore, ta, ore, ALU.subtract))
                ch(pool.tensor_tensor(ta, are, bim, ALU.mult))
                ch(pool.tensor_tensor(oim, aim, bre, ALU.mult))
                ch(pool.tensor_tensor(oim, ta, oim, ALU.add))

            m, hp = L + 1, PR // 2

            def v4(ap):
                return ap.rearrange("p r (d c) -> p r d c", c=GC)

            def over_c(ap, h):
                return ap[:, :, h].rearrange("p d r -> p r d").unsqueeze(3).to_broadcast([P, hp, m, GC])

            def over_d(ap, h):
                return ap[:, h, :].unsqueeze(2).to_broadcast([P, hp, m, GC])

            for h in (slice(0, hp), slice(hp, PR)):
                cre, cim = over_d(BC[:, 2, :, :], h), over_d(BC[:, 3, :, :], h)
                wre, wimn = over_c(PW[:, 0, :, :], h), over_c(PW[:, 2, :, :], h)
                lre, lim = v4(CL[:, 0, h, :]), v4(CL[:, 1, h, :])
                ta = p1[:, :].rearrange("p (r d c) -> p r d c", d=m, c=GC)
                ch(pool.tensor_tensor(ta, cre, wre, ALU.mult))
                ch(pool.tensor_tensor(lre, cim, wimn, ALU.mult))
                ch(pool.tensor_tensor(lre, lre, ta, ALU.add))
                ch(pool.tensor_tensor(ta, cre, wimn, ALU.mult))
                ch(pool.tensor_tensor(lim, cim, wre, ALU.mult))
                ch(pool.tensor_tensor(lim, ta, lim, ALU.subtract))
            pool.memset(p1[:, 0:1], 0.0).then_inc(S["cl_ready"], 1)
            pool.wait_ge(S["cl_ready"], 1)
            for j in range(L):
                bre, bim = BB[:, 0, :, :], BB[:, 1, :, :]
                pre = PW[:, 0, L - 1 - j, :].unsqueeze(2).to_broadcast([P, PR, GC])
                pim = PW[:, 1, L - 1 - j, :].unsqueeze(2).to_broadcast([P, PR, GC])
                tj = p1[:, 0:PR * GC].rearrange("p (r c) -> p r c", c=GC)
                cmul(E[:, 0, :, j * GC:(j + 1) * GC], E[:, 1, :, j * GC:(j + 1) * GC], bre, bim, pre, pim, tj, None)
            ch(pool.memset(WT[:, 0, :, 0:1], 1.0))
            ch(pool.memset(WT[:, 1, :, 0:1], 0.0))
            for l in range(8):
                n = 1 << l
                for h in ((slice(0, PR),) if n < NP_CH // 2 else (slice(0, hp), slice(hp, PR))):
                    m = h.stop - h.start
                    pre = PH[:, 0, l, h].unsqueeze(2).to_broadcast([P, m, n])
                    pim = PH[:, 1, l, h].unsqueeze(2).to_broadcast([P, m, n])
                    tl = p1[:, 0:m * n].rearrange("p (r k) -> p r k", k=n)
                    cmul(WT[:, 0, h, n:2 * n], WT[:, 1, h, n:2 * n], WT[:, 0, h, 0:n], WT[:, 1, h, 0:n], pre, pim, tl, None)
            pre = PW[:, 0, L, :].unsqueeze(2).to_broadcast([P, PR, DECB])
            pim = PW[:, 1, L, :].unsqueeze(2).to_broadcast([P, PR, DECB])
            cmul(F0[:, 0, :, :], F0[:, 1, :, :], s0_sb[:, 0, :, :], s0_sb[:, 1, :, :], pre, pim,
                 p1[:, 0:PR * DECB].rearrange("p (r k) -> p r k", k=DECB), None)
            pool.memset(p1[:, 0:1], 0.0).then_inc(S["tabs_ready"], 1)

            pool.wait_ge(S["um_done"], CB * L)
            pool.wait_ge(S["u_evac"], CB * L)
            pool.wait_ge(S["u_stored"], 16 * L)
            pool.wait_ge(S["t_in"], 16 * L * 4)
            for b in range(2):
                pool.memset(MZ[b][:, :, :, :], 0.0).then_inc(S["mz_zero"], 1)
                pool.memset(Sp[b][:, :, DECB:DECB + 1], 0.0).then_inc(S["mz_zero"], 1)

            def b_copy_e(r, b):
                if not early(r):
                    pool.wait_ge(S["tr_done"], r - 1)
                pool.tensor_copy(ES[b][:, :, :], E[:, :, ds(r, 1), :].rearrange("p a o k -> p a (o k)")).then_inc(S["es_done"], 1)

            def b_copy(r, b):
                if not early(r):
                    pool.wait_ge(S["y_done"], 2 * r - 2)
                pool.tensor_copy(NS[b][:, :, :], CL[:, :, ds(r, 1), GC:(L + 1) * GC].rearrange("p a o k -> p a (o k)")).then_inc(S["cp_done"], 1)
                pool.tensor_copy(TS[b][:, :, :], T[:, ds(2 * r, 2), :]).then_inc(S["cp_done"], 1)
                pool.tensor_copy(Sp[b][:, :, 0:DECB], s0_sb[:, :, ds(r, 1), :].rearrange("p a o k -> p a (o k)")).then_inc(S["cp_done"], 1)

            b_copy_e(0, 0)
            b_copy_e(1, 1)
            for r in range(2):
                b_copy_e(r + 2, r)
                b_copy(r, r)
            with pool.Fori(1, PR // 2 - 1) as i:
                for b in range(2):
                    b_copy_e(2 * i + (b + 2), b)
                    b_copy(2 * i + b, b)
            for b in range(2):
                b_copy(PR - 2 + b, b)

            pool.wait_ge(S["y_in"], 16 * CB * 8)
            yflat = U[:, :, :].rearrange("p (b i) k -> p b (i k)", b=CB)

            def c_copy(t, b, rows=P):
                if not early(t):
                    pool.wait_ge(S["ys_lo"], t - 1)
                pool.tensor_copy(ys[b][:, :, 0:rows], yflat[:, :, ds(t * P, rows)]).then_inc(S["ys_done"], 1)
            steps(pool, TF, c_copy)
            c_copy(TF, 0, LAST)

            pool.wait_ge(S["rl_evac"], TT)
            pool.wait_ge(S["st_stored"], 16)
            pool.wait_ge(S["xn_done"], TT)
            for b in range(2):
                pool.wait_ge(S[f"xn_st{b}"], 16 * (TF // 2 + 1 - b))
                pool.wait_ge(S[f"x2_st{b}"], 16 * (TF // 2 + 1 - b))
            pool.iota(iot[:, :], [[1, P]], base=0, channel_multiplier=0, allow_small_or_imprecise_dtypes=True).then_inc(S["d_iota"], 1)
            pool.iota(tokid[:, :], [[P, TT]], base=1, channel_multiplier=1, allow_small_or_imprecise_dtypes=True).then_inc(S["d_iota"], 1)
            pool.iota(spare[:, :], [[0, 1]], base=NT + 1, channel_multiplier=1, allow_small_or_imprecise_dtypes=True).then_inc(S["d_iota"], 1)
            pool.iota(desc[:, :], [[-1, 4]], base=4, channel_multiplier=0, allow_small_or_imprecise_dtypes=True).then_inc(S["d_iota"], 1)

            for c in range(CUTS):
                pool.wait_ge(S["hi_split"], c + 1)
                w = slice(c * CW, (c + 1) * CW)
                pool.tensor_tensor(WL[:, w], WR[:, w], WH[:, w].bitcast(F32), ALU.subtract).then_inc(S["lo_split"], 1)

            pool.wait_ge(S["ctl_done"], 1)

            def gather(t):
                if t >= 2:
                    pool.wait_ge(S["xgt_done"], 2 * t - 2)
                pool.indirect_dma_start(xg[t % 2][:, :], None, xnD,
                                        bass.IndirectOffsetOnAxis(ap=token_of[:, t:t + 1], axis=0)).then_inc(S[f"gat{t % 2}"], 16)

            def scatter(t):
                pool.wait_ge(S["dn_evac"], t + 1)
                if t >= 1:
                    pool.wait_ge(S["acc_done"], 16 * t)
                pool.indirect_dma_start(x2D, bass.IndirectOffsetOnAxis(ap=sum_of[:, t:t + 1], axis=0), yo[t % 2][:, :], None,
                                        compute_op=ALU.add).then_inc(S["acc_done"], 16)

            def if_used(transfer, t):
                if t < FULL:
                    transfer(t)
                else:
                    with pool.If(used(pool, t)):
                        transfer(t)

            pool.wait_ge(S["spare_set"], 16)
            for t in range(SLOTS + 4):
                if t < SLOTS:
                    if_used(gather, t)
                if t >= 4:
                    if_used(scatter, t - 4)

        @block.scalar
        def _(act):
            act.wait_ge(S["par_in"], 80)
            act.activation(sm[:, 0, :], PAR[:, 2, :], ACT.Exp).then_inc(S["act_small"], 1)
            act.wait_ge(S["dch"], 2)
            act.activation(sm[:, 3, :], sm[:, 1, :], ACT.Exp).then_inc(S["act_small"], 1)
            act.activation(sm[:, 4, :], sm[:, 1, :], ACT.Exp, scale=float(L)).then_inc(S["act_small"], 1)
            act.wait_ge(S["c_g1"], 1)
            act.activation(AN[:, 3, :, :], AN[:, 1, :, :], ACT.Sin).then_inc(S["act_small"], 1)
            act.activation(AN[:, 4, :, :], AN[:, 2, :, :], ACT.Sin).then_inc(S["act_small"], 1)

            def a_step(j, b):
                i = j // 2 if isinstance(j, int) else None
                act.wait_ge(S[f"x_in{b}"], 8 * (j - b) + 16)
                if not (isinstance(j, int) and j == 0):
                    act.wait_ge(S["red_done"], j)
                act.activation(sq[:, :, :], xT[b][:, :, :], ACT.Square).then_inc(S["sq_done"], 1)
                act.wait_ge(S["var_done"], j + 1)
                act.activation(rst[b][:, :], rst[b][:, :], ACT.Sqrt).then_inc(S["std_done"], 1)

            def k_out(n):
                act.wait_ge(S["k_done"], n + 1)
                if n >= 2:
                    act.wait_ge(S["t_in"], 16 * L * (n - 1))
                for h in range(2):
                    act.activation(Kp[n % 2][:, :, :].rearrange("c (r h) k -> c r h k", h=2)[:, :, h, :],
                                   pbig[0:GC, 6 + h, :].rearrange("p (g k) -> p g k", g=4), ACT.Copy).then_inc(S["k_evac"], 1)
            for j in range(L):
                a_step(j, j % 2)
                if j >= L - 4:
                    k_out(j - (L - 4))

            act.wait_ge(S["mz_zero"], 4)

            def b_mz(r, b):
                act.wait_ge(S["tr_done"], r + 1)
                if not early(r):
                    act.wait_ge(S["v_done"], r - 1)
                tr = pbig[:, 4, 0:2 * P].rearrange("p (a m) -> p a m", a=2)
                act.activation(MZ[b][:, 0, :, 0:ST], tr[:, :, 0:ST], ACT.Copy).then_inc(S["mz_done"], 1)
                act.activation(MZ[b][:, 1, :, ST:P], tr[:, :, ST:P], ACT.Copy).then_inc(S["mz_done"], 1)

            def b_gelu(r):
                for g in range(2):
                    act.wait_ge(S["y_done"], 2 * r + g + 1)
                    act.activation(U[:, ds(2 * r + g, 1), :].rearrange("p o k -> p (o k)"), pbig[:, 5 + g, 0:NCH],
                                   ACT.Gelu_apprx_tanh).then_inc(S["gelu_done"], 1)

            b_mz(0, 0)
            b_mz(1, 1)
            for r in range(2):
                b_mz(2 + r, r)
            for r in range(2):
                b_gelu(r)
            with act.Fori(1, PR // 2 - 1) as i:
                for b in range(2):
                    b_mz(2 * i + (b + 2), b)
                for b in range(2):
                    b_gelu(2 * i + b)
            b_gelu(PR - 2)
            b_gelu(PR - 1)

            act.wait_ge(S["wout_in"], 16)
            act.wait_ge(S["gelu_done"], G)
            act.wait_ge(S["fo_done"], 2 * PR)
            for n in (2, 3, 0, 1):
                c = slice(n * 512, (n + 1) * 512)
                act.activation(w2H[:, :, c], w2[:, :, c], ACT.Copy).then_inc(S["w2_hi"], 1)

            def c_y_hi(t, b, rows=P):
                act.wait_ge(S["ys_done"], t + 1)
                if not early(t):
                    act.wait_ge(S["a_done"], 4 * t - 4)
                act.activation(ysH[b][:, :, 0:rows], ys[b][:, :, 0:rows], ACT.Copy).then_inc(S["ys_hi"], 1)

            def c_gate(t, b, rows=P):
                if not early(t, 1):
                    act.wait_ge(S["x2_done"], t)
                for n in range(2):
                    act.wait_ge(S["a_done"], 4 * t + 3 + n)
                    act.activation(sg[0:rows, n * 512:(n + 1) * 512], pbig[0:rows, 2 + n, :], ACT.Sigmoid).then_inc(S["sig_done"], 1)
                act.wait_ge(S["x2_done"], t + 1)
                act.activation(junk[0:rows, :], x2[b][0:rows, :], ACT.Square, accum_out=ssq[0:rows, ds(t, 1)]).then_inc(S["ssq_done"], 1)

            def c_turned(t, rows=P):
                for n in range(2):
                    act.wait_ge(S["xt_done"], 2 * t + n + 1)
                    if n == 0 and not early(t, 1):
                        act.wait_ge(S["rl_done"], t)
                    act.activation(xnT[:, 4 * n:4 * n + 4, 0:rows],
                                   pbig[:, 4 + n, :].rearrange("p (a m) -> p a m", a=4)[:, :, 0:rows], ACT.Copy).then_inc(S["xt_evac"], 1)

            def c_routed(t, rows=P):
                act.wait_ge(S["rl_done"], t + 1)
                act.activation(logit[0:rows, ds(t, 1), :].rearrange("p o k -> p (o k)"), pbig[0:rows, 6, 0:20], ACT.Copy).then_inc(S["rl_evac"], 1)

            c_y_hi(0, 0)
            c_y_hi(1, 1)
            c_gate(0, 0)
            c_y_hi(2, 0)
            c_gate(1, 1)
            c_turned(0)
            with act.Fori(1, TF // 2 - 1) as i:
                c_y_hi(2 * i + 1, 1)
                c_gate(2 * i, 0)
                c_routed(2 * i - 2)
                c_turned(2 * i - 1)
                c_y_hi(2 * i + 2, 0)
                c_gate(2 * i + 1, 1)
                c_routed(2 * i - 1)
                c_turned(2 * i)
            c_y_hi(TF - 1, 1)
            c_gate(TF - 2, 0)
            c_routed(TF - 4)
            c_turned(TF - 3)
            c_y_hi(TF, 0, LAST)
            c_gate(TF - 1, 1)
            c_routed(TF - 3)
            c_turned(TF - 2)
            c_gate(TF, 0, LAST)
            c_routed(TF - 2)
            c_turned(TF - 1)
            c_routed(TF - 1)
            c_turned(TF, LAST)
            c_routed(TF, LAST)

            act.wait_ge(S["exp_in"], 1)
            act.activation(R3[1][:, :, :], R3[0][:, :, :], ACT.Exp).then_inc(S["exp_d"], 1)
            act.wait_ge(S["exp_in"], 2)
            act.activation(R1[5][:, :], R1[4][:, :], ACT.Exp).then_inc(S["exp_d"], 1)

            act.wait_ge(S["wts"], 32)
            for c in range(CUTS):
                act.activation(WH[:, c * CW:(c + 1) * CW], WR[:, c * CW:(c + 1) * CW], ACT.Copy).then_inc(S["hi_split"], 1)
            act.wait_ge(S["ctl_done"], 1)

            def e_x(s, b):
                if not early(s):
                    act.wait_ge(S["gu_done"], s - 1)
                for n in range(2):
                    act.wait_ge(S["xgt_done"], 2 * s + n + 1)
                    act.activation(xgH[b][:, 4 * n:4 * n + 4, :], pbig[:, 4 + n, :].rearrange("p (a m) -> p a m", a=4), ACT.Copy).then_inc(S["xgt_evac"], 1)

            def e_silu(s, b):
                act.wait_ge(S["gu_done"], s + 1)
                if not early(s, 1):
                    act.wait_ge(S["h_done"], s)
                act.activation(sl[:, :], pbig[:, 6, 0:DE], ACT.Silu).then_inc(S["sl_done"], 1)

            def e_y(s, b, maybe=False):
                if maybe:
                    with act.If(used(act, s)):
                        e_y_out(s, b)
                    with act.Else():
                        act.wait_ge(S["dn_done"], s + 2)
                        act.wait_ge(S["dn_evac"], s)
                        act.nop().then_inc(S["dn_evac"], 1)
                else:
                    e_y_out(s, b)

            def e_y_out(s, b):
                act.wait_ge(S["dn_done"], s + 2)
                if not early(s):
                    act.wait_ge(S["acc_done"], 16 * s - 16)
                act.wait_ge(S["ctl_done"], 1)
                act.activation(yo[b][:, :].rearrange("p (a m) -> p a m", a=2), pbig[:, 0:2, :], ACT.Copy,
                               scale=cw_of[:, ds(s, 1)]).then_inc(S["dn_evac"], 1)

            def e_word(s):
                return act.value_load(ctrl[0:1, ds(C_NEXT + s, 1)], min_val=0, max_val=EW)

            def e_split(s, to, part):
                with act.If(to != SKIP):
                    if part == 0:
                        e = act.value_load(ctrl[0:1, ds(C_EXP + s, 1)], min_val=0, max_val=NE - 1)
                        act.wait_ge(S["wts"], e * 32 + 64)
                    if not early(s, 1):
                        act.wait_ge(S["dn_done"] if part else S["gu_done"], s + part)
                    act.wait_ge(S["ctl_done"], 1)
                    for c in (range(UP_CUTS), range(UP_CUTS, CUTS))[part]:
                        act.activation(WH[:, ds(to + c * CW, CW)], WR[:, ds(to + c * CW, CW)], ACT.Copy).then_inc(S["hi_split"], 1)

            def e_act(s, b, to, ahead=True, last=False, maybe=False):
                then = None
                if not last:
                    e_split(s, to, 0)
                e_silu(s, b)
                if not last:
                    e_x(s + 1, 1 - b)
                    if ahead:
                        then = e_word(s + 1)
                if not early(s, 1):
                    e_y(s - 1, 1 - b, maybe)
                if not last:
                    e_split(s, to, 1)
                return then

            e_x(0, 0)
            to = e_act(0, 0, e_word(0))
            e_act(1, 1, to, ahead=False)
            def four(i, maybe):
                to = e_word(4 * i + 2)
                for n in range(2, 6):
                    to = e_act(4 * i + n, n % 2, to, ahead=n < 5, maybe=maybe)

            with act.Fori(0, FULL // 4) as i:
                four(i, False)
            with act.Fori(FULL // 4, SLOTS // 4 - 1) as i:
                with act.If(used(act, 4 * i + 1)):
                    four(i, True)
            with act.If(used(act, SLOTS - 3)):
                e_act(SLOTS - 2, 0, e_word(SLOTS - 2), ahead=False, maybe=True)
                e_act(SLOTS - 1, 1, None, last=True, maybe=True)
                e_y(SLOTS - 1, 1, True)

            def f_norm(t, b, rows=P):
                act.wait_ge(S[f"f_in{b}"], 16 * (t // NF) + 16 if isinstance(t, int) else 4 * (t - b) + 16)
                act.activation(fj[0:rows, :], fx[b][0:rows, :], ACT.Square, accum_out=fss[0:rows, b:b + 1]).then_inc(S["f_sq"], 1)
                act.wait_ge(S["f_sq"], t + 1)
                if not early(t, NF):
                    act.wait_ge(S["f_out"], t - NF + 1)
                act.activation(fnv[0:rows, 0, b:b + 1], fss[0:rows, b:b + 1], ACT.Sqrt, scale=1.0 / D,
                               bias=epsc[0:rows, 0:1]).then_inc(S["f_std"], 1)
            for b in range(NF):
                f_norm(b, b)
            with act.Fori(1, TF // NF) as i:
                for b in range(NF):
                    f_norm(NF * i + b, b)
            f_norm(TF, 0, LAST)

        @block.tensor
        def _(pe):
            def k_groups(n):
                pe.wait_ge(S["cl_ready"], 1)
                if n >= 1:
                    pe.wait_ge(S["k_evac"], 2 * n)
                for h in range(2):
                    for q in range(4):
                        r = 4 * n + q
                        for a in range(2):
                            mm = pe.matmul(pbig[0:GC, 6 + h, q * P:(q + 1) * P], BB[h * ST:(h + 1) * ST, a, r, :],
                                           CL[h * ST:(h + 1) * ST, a, r, 0:L * GC], start=(a == 0), stop=(a == 1))
                mm.then_inc(S["k_done"], 1)

            pe.wait_ge(S["w_scaled"], KD)
            pe.wait_ge(S["c_pool"], 1)
            for j in range(L):
                b = j % 2
                if j >= L - 4:
                    k_groups(j - (L - 4))
                pe.wait_ge(S[f"x_in{b}"], 16 * (j // 2 + 1))
                for cb in range(CB):
                    if j >= 1:
                        pe.wait_ge(S["u_evac"], CB * (j - 1) + cb + 1)
                    for k in range(KD):
                        mm = pe.matmul(pbig[:, cb, 0:NCH], w1[:, k, cb * P:(cb + 1) * P], xT[b][:, k, :],
                                       start=(k == 0), stop=(k == KD - 1))
                    mm.then_inc(S["um_done"], 1)
                    if cb == 0:
                        pe.wait_ge(S["red_done"], j + 1)
                        pe.matmul(pbig[:, 4 + b, 0:NCH], ones[:, :], red[b][:, :], start=True, stop=True).then_inc(S["ss_done"], 1)
            pe.wait_ge(S["k_evac"], 8)
            pe.wait_ge(S["u_in"], 16 * L * CB)

            def b_state(r, b):
                pe.wait_ge(S["es_done"], r + 1)
                if not early(r, 1):
                    pe.wait_ge(S["mz_done"], 2 * r)
                for a in range(2):
                    mm = pe.transpose(pbig[:, 4, a * P:(a + 1) * P], ES[b][:, a, :], ident[:, :])
                mm.then_inc(S["tr_done"], 1)
                pe.wait_ge(S["mz_done"], 2 * r + 2)
                if not early(r):
                    pe.wait_ge(S["v_used"], r - 1)
                for a in range(2):
                    for g in range(2):
                        mm = pe.matmul(pbig[:, 2 * b + a, 0:NCH], MZ[b][:, g, a, :],
                                       U[:, ds(2 * r + g, 1), :].rearrange("p o k -> p (o k)"),
                                       start=(g == 0), stop=(g == 1))
                mm.then_inc(S["v_done"], 1)

            def b_out(r, b):
                pe.wait_ge(S["cp_done"], 3 * r + 3)
                pe.wait_ge(S["sp_done"], 2 * r + 2)
                for g in range(2):
                    if not early(r, 1):
                        pe.wait_ge(S["gelu_done"], 2 * r - 1 + g)
                    h = g * ST
                    out = pbig[:, 5 + g, 0:NCH]
                    pe.matmul(out, TS[b][:, g, :], U[:, ds(2 * r + g, 1), :].rearrange("p o k -> p (o k)"), start=True, stop=False)
                    pe.matmul(out, NS[b][h:h + ST, 0, :], Sp[b][h:h + ST, 0, 0:NCH], start=False, stop=False)
                    pe.matmul(out, NS[b][h:h + ST, 1, :], Sp[b][h:h + ST, 1, 0:NCH], start=False, stop=True).then_inc(S["y_done"], 1)

            for r in range(4):
                b_state(r, r % 2)
            for r in range(2):
                b_out(r, r)
            with pe.Fori(1, PR // 2 - 1) as i:
                for b in range(2):
                    b_state(2 * i + (b + 2), b)
                for b in range(2):
                    b_out(2 * i + b, b)
            b_out(PR - 2, 0)
            b_out(PR - 1, 1)

            pe.wait_ge(S["gelu_done"], G)
            pe.wait_ge(S["con_in"], 48)

            def c_proj(t, b, ns, rows=P):
                if 2 in ns:
                    pe.wait_ge(S["ys_lo"], t + 1)
                for n in ns:
                    if early(t, 1):
                        pe.wait_ge(S["w2_lo"], (2, 3, 0, 1).index(n) + 1)
                    if not early(t, 1):
                        pe.wait_ge(S["sig_done" if n >= 2 else "x2_done"], 2 * t - 3 + n if n >= 2 else t)
                    for k in range(CB):
                        c = slice(n * 512, (n + 1) * 512)
                        pe.matmul(pbig[0:rows, n, :], ysH[b][:, k, 0:rows], w2H[:, k, c], start=(k == 0), stop=False)
                        pe.matmul(pbig[0:rows, n, :], ysH[b][:, k, 0:rows], w2L[:, k, c], start=False, stop=False)
                        mm = pe.matmul(pbig[0:rows, n, :], ysL[b][:, k, 0:rows], w2H[:, k, c], start=False, stop=(k == CB - 1))
                    mm.then_inc(S["a_done"], 1)

            def c_turn(t, b, rows=P):
                pe.wait_ge(S["xn_done"], t + 1)
                for n in range(2):
                    if not early(t, 1):
                        pe.wait_ge(S["xt_evac"], 2 * t - 1 + n)
                    for k in range(4):
                        mm = pe.transpose(pbig[:, 4 + n, k * P:k * P + rows], xn[b][0:rows, (4 * n + k) * P:(4 * n + k + 1) * P],
                                          ident[0:rows, 0:rows])
                    mm.then_inc(S["xt_done"], 1)

            def c_logit(t, rows=P):
                pe.wait_ge(S["xt_evac"], 2 * t + 2)
                if not early(t, 1):
                    pe.wait_ge(S["rl_evac"], t)
                for k in range(KD):
                    mm = pe.matmul(pbig[0:rows, 6, 0:20], xnT[:, k, 0:rows], wr_sb[:, k, :], start=(k == 0), stop=(k == KD - 1))
                mm.then_inc(S["rl_done"], 1)

            def c_step(t, b, rows=P, prev=2):
                c_proj(t, b, (2, 3), rows)
                if prev > 1:
                    c_logit(t - 2)
                c_proj(t, b, (0, 1), rows)
                if prev > 0:
                    c_turn(t - 1, 1 - b)

            c_step(0, 0, prev=0)
            c_step(1, 1, prev=1)
            with pe.Fori(1, TF // 2) as i:
                c_step(2 * i, 0)
                c_step(2 * i + 1, 1)
            c_step(TF, 0, LAST)
            c_logit(TF - 1)
            c_turn(TF, 0, LAST)
            c_logit(TF, LAST)

            pe.wait_ge(S["d_ready"], 1)
            pe.matmul(pbig[:, 0, 0:TT * NE], upper[:, :], EE[:, :, :, :].rearrange("p t g e -> p (t g e)"), start=True, stop=True)
            pe.matmul(pbig[:, 1, 0:TT * NE], ones[:, :], EE[:, :, :, :].rearrange("p t g e -> p (t g e)"), start=True, stop=True).then_inc(S["cnt_done"], 1)
            for c in range(2):
                pe.wait_ge(S["one_hot_done"], c + 1)
                for t in range(TT):
                    mm = pe.matmul(pbig[:, 2, 0:2 * SLOTS], oh_lo[:, c, t, :], oh_hi[:, c, t, :, :].rearrange("p a s -> p (a s)"),
                                   start=(c == 0 and t == 0), stop=(c == 1 and t == TT - 1))
                mm.then_inc(S["tbl_done"], 1)

            pe.wait_ge(S["ctl_done"], 1)
            pe.nop().then_inc(S["dn_done"], 1)

            def e_turn(s, b, at=None):
                if at is None:
                    e_turn_rows(s, b)
                else:
                    with pe.If(at != SKIP):
                        e_turn_rows(s, b)
                    with pe.Else():
                        pe.wait_ge(S["xgt_lo"], 2 * s)
                        pe.nop().then_inc(S["xgt_done"], 2)

            def e_turn_rows(s, b):
                pe.wait_ge(S[f"gat{b}"], 8 * (s - b) + 16)
                for n in range(2):
                    if not early(s, 1):
                        pe.wait_ge(S["xgt_evac"], 2 * s - 1 + n)
                        pe.wait_ge(S["xgt_lo"], 2 * s - 1 + n)
                    for k in range(4):
                        mm = pe.transpose(pbig[:, 4 + n, k * P:(k + 1) * P], xg[b][:, (4 * n + k) * P:(4 * n + k + 1) * P], ident[:, :])
                    mm.then_inc(S["xgt_done"], 1)

            def e_up(s, b, off, e, maybe):
                pe.wait_ge(S["xgt_evac"], 2 * s + 2)
                if not early(s, 1):
                    pe.wait_ge(S["h_done"], s)
                pe.wait_ge(S["lo_split"], e * CUTS + UP_CUTS)
                pe.wait_ge(S["ctl_done"], 1)
                if maybe:
                    with pe.If(off != SKIP):
                        e_up_products(s, b, off)
                    with pe.Else():
                        pe.nop().then_inc(S["gu_done"], 1)
                else:
                    e_up_products(s, b, off)

            def e_up_products(s, b, off):
                for k in range(KD):
                    w = ds(off + k * 2 * DE, 2 * DE)
                    pe.matmul(pbig[:, 6, :], xgH[b][:, k, :], WH[:, w], start=(k == 0), stop=False)
                    pe.matmul(pbig[:, 6, :], xgH[b][:, k, :], WL[:, w], start=False, stop=False)
                pe.wait_ge(S["xgt_lo"], 2 * s + 2)
                for k in range(KD):
                    mm = pe.matmul(pbig[:, 6, :], xgL[b][:, k, :], WH[:, ds(off + k * 2 * DE, 2 * DE)], start=False, stop=(k == KD - 1))
                mm.then_inc(S["gu_done"], 1)

            def e_hturn(s, b):
                pe.wait_ge(S["h_done"], s + 1)
                if not early(s, 1):
                    pe.wait_ge(S["ht_evac"], s)
                for k in range(2):
                    mm = pe.transpose(pbig[:, 7, k * P:(k + 1) * P], hh[b][:, k * P:(k + 1) * P], ident[:, :])
                mm.then_inc(S["ht_done"], 1)

            def e_down(s, b, off, e, maybe):
                pe.wait_ge(S["ht_evac"], s + 1)
                if not early(s, 1):
                    pe.wait_ge(S["dn_evac"], s)
                pe.wait_ge(S["lo_split"], e * CUTS + CUTS)
                pe.wait_ge(S["ctl_done"], 1)
                if maybe:
                    with pe.If(off != SKIP):
                        e_down_products(s, b, off)
                    with pe.Else():
                        pe.nop().then_inc(S["dn_done"], 1)
                else:
                    e_down_products(s, b, off)

            def e_down_products(s, b, off):
                for n in range(2):
                    for k in range(2):
                        w = ds(off + (KD * 2 * DE + k * D + n * 512), 512)
                        pe.matmul(pbig[:, n, :], hTH[b][:, k, :], WH[:, w], start=(k == 0), stop=False)
                        pe.matmul(pbig[:, n, :], hTH[b][:, k, :], WL[:, w], start=False, stop=False)
                        mm = pe.matmul(pbig[:, n, :], hTL[b][:, k, :], WH[:, w], start=False, stop=(k == 1))
                mm.then_inc(S["dn_done"], 1)

            def words(s):
                return (pe.value_load(ctrl[0:1, ds(C_AT + s, 1)], min_val=0, max_val=EW),
                        pe.value_load(ctrl[0:1, ds(C_EXP + s, 1)], min_val=0, max_val=NE - 1))

            def e_step(s, b, before, last=False, maybe=False, turned=False):
                now = words(s)
                if before and not turned:
                    e_hturn(s - 1, 1 - b)
                e_up(s, b, *now, maybe)
                if not last:
                    e_turn(s + 1, 1 - b, words(s + 1)[0] if maybe else None)
                if before:
                    e_down(s - 1, 1 - b, *before, maybe)
                return now

            e_turn(0, 0)
            now = e_step(0, 0, None)
            e_step(1, 1, now)
            def four(i, maybe):
                now = words(4 * i + 1)
                for n in range(2, 6):
                    now = e_step(4 * i + n, n % 2, now, maybe=maybe, turned=maybe and n == 2)

            with pe.Fori(0, FULL // 4) as i:
                four(i, False)
            e_hturn(FULL // 4 * 4 + 1, 1)
            with pe.Fori(FULL // 4, SLOTS // 4 - 1) as i:
                with pe.If(used(pe, 4 * i + 1)):
                    four(i, True)
                    e_hturn(4 * i + 5, 1)
            with pe.If(used(pe, SLOTS - 3)):
                now = e_step(SLOTS - 2, 0, words(SLOTS - 3), maybe=True, turned=True)
                now = e_step(SLOTS - 1, 1, now, last=True, maybe=True)
                e_hturn(SLOTS - 1, 1)
                e_down(SLOTS - 1, 1, *now, True)

        @block.vector
        def _(dve):
            ch = Chain(dve, S["dch"])
            tt, ts, stt = dve.tensor_tensor, dve.tensor_scalar, dve.scalar_tensor_tensor
            dve.wait_ge(S["par_in"], 80)
            lr, li = PAR[:, 0, :], PAR[:, 1, :]
            dve.wait_ge(S["act_small"], 1)
            dt_, lrdt, ang, mag, mag8 = (sm[:, k, :] for k in range(5))
            ch(tt(lrdt, lr, dt_, ALU.mult))
            ch(tt(ang, li, dt_, ALU.mult))
            x_, r_, rh, sn, sh = (AN[:, k, :, :] for k in range(5))
            for l in range(9):
                n = ts(AN[:, 0, l, :], ang, float(L << (l - 1)) if l else 1.0, None, ALU.mult)
            ch(n)
            n_ = rh
            ch(ts(n_, x_, INV_2PI, ROUND, ALU.mult, ALU.add))
            ch(ts(n_, n_, ROUND, None, ALU.subtract))
            ch(stt(r_, n_, -PI_HI, x_, ALU.mult, ALU.add))
            ch(stt(r_, n_, -PI_MID, r_, ALU.mult, ALU.add))
            ch(stt(r_, n_, -PI_LO, r_, ALU.mult, ALU.add))
            ch(ts(r_, r_, PI_IN, -PI_IN, ALU.min, ALU.max))
            ts(rh, r_, 0.5, None, ALU.mult).then_inc(S["c_g1"], 1)
            dve.wait_ge(S["act_small"], 5)
            ch(tt(x_, sh, sh, ALU.mult))
            ch(ts(x_, x_, -2.0, 1.0, ALU.mult, ALU.add))
            dve.tensor_copy(PH[:, 0, :, :], AN[:, 0, 1:9, :])
            ch(dve.tensor_copy(PH[:, 1, :, :], AN[:, 3, 1:9, :]))
            cs, sn = AN[:, 0, 0, :], AN[:, 3, 0, :]
            dve.wait_ge(S["win_in"], 16)
            for k in range(KD):
                ts(w1[:, k, :], w1[:, k, :], gm_sb[:, k:k + 1], None, ALU.mult).then_inc(S["w_scaled"], 1)

            def cmul(ore, oim, are, aim, bre, bim, ta, tb):
                ch(tt(ta, are, bre, ALU.mult))
                ch(tt(tb, aim, bim, ALU.mult))
                ch(tt(ore, ta, tb, ALU.subtract))
                ch(tt(ta, are, bim, ALU.mult))
                ch(tt(tb, aim, bre, ALU.mult))
                ch(tt(oim, ta, tb, ALU.add))

            q0, q1 = tq[:, 0, 0:PR], tq[:, 1, 0:PR]
            ch(dve.memset(PW[:, 0, 0, :], 1.0))
            ch(dve.memset(PW[:, 1, 0, :], 0.0))
            ch(tt(PW[:, 0, 1, :], mag, cs, ALU.mult))
            ch(tt(PW[:, 1, 1, :], mag, sn, ALU.mult))
            for lo in (1, 2, 4):
                def bc(a):
                    return PW[:, a, lo:lo + 1, :].to_broadcast([P, lo, PR])
                v0 = tq[:, 0, 0:lo * PR].rearrange("p (d r) -> p d r", r=PR)
                v1 = tq[:, 1, 0:lo * PR].rearrange("p (d r) -> p d r", r=PR)
                cmul(PW[:, 0, lo + 1:2 * lo + 1, :], PW[:, 1, lo + 1:2 * lo + 1, :], PW[:, 0, 1:lo + 1, :], PW[:, 1, 1:lo + 1, :],
                     bc(0), bc(1), v0, v1)
            ch(ts(PW[:, 2, :, :], PW[:, 1, :, :], -1.0, None, ALU.mult))
            den, nr, cr, ci = sm[:, 5, :], sm[:, 6, :], sm[:, 7, :], sm[:, 8, :]
            ch(tt(q0, lr, lr, ALU.mult))
            ch(tt(q1, li, li, ALU.mult))
            ch(tt(q0, q0, q1, ALU.add))
            ch(dve.reciprocal(den, q0))
            ch(ts(nr, PW[:, 0, 1, :], -1.0, None, ALU.add))
            ch(tt(q0, nr, lr, ALU.mult))
            ch(tt(q1, PW[:, 1, 1, :], li, ALU.mult))
            ch(tt(q0, q0, q1, ALU.add))
            ch(tt(cr, q0, den, ALU.mult))
            ch(tt(q0, PW[:, 1, 1, :], lr, ALU.mult))
            ch(tt(q1, nr, li, ALU.mult))
            ch(tt(q0, q0, q1, ALU.subtract))
            ch(tt(ci, q0, den, ALU.mult))
            crb, cib = cr.unsqueeze(2).to_broadcast([P, PR, GC]), ci.unsqueeze(2).to_broadcast([P, PR, GC])
            bt0 = uT[0][:, 0, 0:PR * GC].rearrange("p (r c) -> p r c", c=GC)
            bt1 = uT[0][:, 1, 0:PR * GC].rearrange("p (r c) -> p r c", c=GC)
            cmul(BB[:, 0, :, :], BB[:, 1, :, :], BC[:, 0, :, :], BC[:, 1, :, :], crb, cib, bt0, bt1)
            dve.memset(sm[:, 9, :], 0.0).then_inc(S["pws_ready"], 1)

            for j in range(L):
                b = j % 2
                dve.wait_ge(S["sq_done"], j + 1)
                dve.tensor_reduce(red[b][:, :], sq[:, :, :].rearrange("p k n -> p n k"), AX, ALU.add).then_inc(S["red_done"], 1)
                dve.wait_ge(S["ss_done"], j + 1)
                ts(rst[b][:, :], pbig[:, 4 + b, 0:NCH], 1.0 / D, EPS, ALU.mult, ALU.add).then_inc(S["var_done"], 1)
                dve.wait_ge(S["std_done"], j + 1)
                ch(dve.reciprocal(rst[b][:, :], rst[b][:, :]))
                if j >= 2:
                    dve.wait_ge(S["u_stored"], 16 * (j - 1))
                for cb in range(CB):
                    dve.wait_ge(S["um_done"], CB * j + cb + 1)
                    tt(uT[b][:, cb, :], pbig[:, cb, 0:NCH], rst[b][:, :], ALU.mult).then_inc(S["u_evac"], 1)
                if j >= L - 4:
                    n = j - (L - 4)
                    ch(tt(kd[:, :, :], ident[0:GC, 0:GC].unsqueeze(1).to_broadcast([GC, 8, GC]),
                          d_sb[0:GC, n * 8:(n + 1) * 8].unsqueeze(2).to_broadcast([GC, 8, GC]), ALU.mult))
                    dve.wait_ge(S["k_evac"], 2 * n + 2)
                    tt(Kp[n % 2][:, :, 0:GC], Kp[n % 2][:, :, 0:GC], kd[:, :, :], ALU.add).then_inc(S["k_full"], 1)

            dve.wait_ge(S["tabs_ready"], 1)
            dve.wait_ge(S["u_stored"], 16 * L)
            dve.wait_ge(S["um_done"], CB * L)
            dve.wait_ge(S["mz_zero"], 4)
            def b_scans(i, first=False):
                pairs = [(2 * i + b, b) for b in range(2)]
                turn = [[WT[:, a:a + 1, ds(r, 1), :].rearrange("p a o k -> p a (o k)").to_broadcast([P, 2, NP_CH]) for a in range(2)]
                        for r, b in pairs]
                for r, b in pairs:
                    dve.wait_ge(S["v_done"], r + 1)
                    v = pbig[:, 2 * b:2 * b + 2, DECB:NCH]
                    tt(r1[b][:, :, :], v, turn[b][0], ALU.mult).then_inc(S["dchb"], 1)
                    tt(r2[b][:, :, :], v, turn[b][1], ALU.mult).then_inc(S["dchb"], 1)
                for r, b in pairs:
                    dve.wait_ge(S["dchb"], 2 * r + 2)
                    tt(FO[:, :, ds(r, 1), 0:DECB].rearrange("p a o k -> p a (o k)"), pbig[:, 2 * b:2 * b + 2, 0:DECB],
                       F0[:, :, ds(r, 1), :].rearrange("p a o k -> p a (o k)"), ALU.add).then_inc(S["v_used"], 1)
                    tt(z[b][:, 0, :], r1[b][:, 0, :], r2[b][:, 1, :], ALU.add).then_inc(S["z_done"], 1)
                    tt(z[b][:, 1, :], r1[b][:, 1, :], r2[b][:, 0, :], ALU.subtract).then_inc(S["z_done"], 1)
                for r, b in pairs:
                    dve.wait_ge(S["z_done"], 2 * r + 2)
                    mg = mag8[:, ds(r, 1)].to_broadcast([P, NP_CH])
                    for a in range(2):
                        dve.tensor_tensor_scan(r1[b][:, a, :], mg, z[b][:, a, :], 0.0, ALU.mult, ALU.add).then_inc(S["scan_done"], 1)
                for r, b in pairs:
                    dve.wait_ge(S["scan_done"], 2 * r + 2)
                    tt(z[b][:, :, :], r1[b][:, :, :], turn[b][0], ALU.mult).then_inc(S["turned_on"], 1)
                    tt(r2[b][:, :, :], r1[b][:, :, :], turn[b][1], ALU.mult).then_inc(S["turned_on"], 1)
                for r, b in pairs:
                    dve.wait_ge(S["turned_on"], 2 * r + 2)
                    if not first:
                        dve.wait_ge(S["y_done"], 2 * r - 2)
                    tt(Sp[b][:, 0, DECB + 1:NCH + 1], z[b][:, 0, :], r2[b][:, 1, :], ALU.subtract).then_inc(S["sp_done"], 1)
                    tt(Sp[b][:, 1, DECB + 1:NCH + 1], z[b][:, 1, :], r2[b][:, 0, :], ALU.add).then_inc(S["sp_done"], 1)
                for r, b in pairs:
                    dve.wait_ge(S["sp_done"], 2 * r + 2)
                    dve.tensor_copy(FO[:, :, ds(r, 1), DECB:DECB + 1].rearrange("p a o k -> p a (o k)"), Sp[b][:, :, NCH:NCH + 1]).then_inc(S["fo_done"], 2)

            b_scans(0, first=True)
            with dve.Fori(1, PR // 2) as i:
                b_scans(i)

            dve.wait_ge(S["con_in"], 48)
            dve.wait_ge(S["gelu_done"], G)
            for m, n in enumerate((2, 3, 0, 1)):
                c = slice(n * 512, (n + 1) * 512)
                dve.wait_ge(S["w2_hi"], m + 1)
                tt(w2L[:, :, c], w2[:, :, c], w2H[:, :, c].bitcast(F32), ALU.subtract).then_inc(S["w2_lo"], 1)

            def c_y_lo(t, b, rows=P):
                dve.wait_ge(S["ys_hi"], t + 1)
                tt(ysL[b][:, :, 0:rows], ys[b][:, :, 0:rows], ysH[b][:, :, 0:rows].bitcast(F32), ALU.subtract).then_inc(S["ys_lo"], 1)

            NC = 12

            def c_mix(t, b, rows=P):
                at = [0]

                def lk(ins):
                    at[0] += 1
                    ins.then_inc(S["dchc"], 1)
                    dve.wait_ge(S["dchc"], NC * t + at[0])
                dve.wait_ge(S[f"xr_in{b}"], 8 * (t - b) + 16)
                if not early(t):
                    dve.wait_ge(S[f"x2_st{b}"], 8 * (t - b))
                    dve.wait_ge(S[f"xn_st{b}"], 8 * (t - b))
                dve.wait_ge(S["sig_done"], 2 * t + 2)
                dve.wait_ge(S["a_done"], 4 * t + 4)
                lk(tt(x2[b][0:rows, :].rearrange("p (a m) -> p a m", a=2), pbig[0:rows, 0:2, :],
                      sg[0:rows, :].rearrange("p (a m) -> p a m", a=2), ALU.mult))
                lk(tt(x2[b][0:rows, :], x2[b][0:rows, :], xr[b][0:rows, :], ALU.add))
                dve.nop().then_inc(S["x2_done"], 1)
                dve.wait_ge(S["ssq_done"], t + 1)
                mean, y_, h_, t2 = nv[0:rows, 0:1], nv[0:rows, 1:2], nv[0:rows, 2:3], nv[0:rows, 3:4]
                lk(ts(mean, ssq[0:rows, ds(t, 1)], 1.0 / D, EPS, ALU.mult, ALU.add))
                lk(ts(nvi[0:rows, 0:1], mean.bitcast(I32), 1, None, ALU.logical_shift_right))
                lk(ts(nvi[0:rows, 1:2], nvi[0:rows, 0:1], -1.0, RSQRT_SEED, ALU.mult, ALU.add))
                lk(ts(h_, mean, -0.5, None, ALU.mult))
                yy = nvi[0:rows, 1:2].bitcast(F32)
                for k in range(3):
                    lk(stt(t2, yy, h_, yy, ALU.mult, ALU.mult))
                    lk(stt(y_, t2, 1.5, yy, ALU.add, ALU.mult))
                    yy = y_
                stt(xn[b][0:rows, :], x2[b][0:rows, :], y_, gf_b[0:rows, :], ALU.mult, ALU.mult).then_inc(S["xn_done"], 1)
            c_y_lo(0, 0)
            c_y_lo(1, 1)
            c_mix(0, 0)
            with dve.Fori(1, TF // 2) as i:
                c_y_lo(2 * i, 0)
                c_mix(2 * i - 1, 1)
                c_y_lo(2 * i + 1, 1)
                c_mix(2 * i, 0)
            c_y_lo(TF, 0, LAST)
            c_mix(TF - 1, 1)
            c_mix(TF, 0, LAST)

            dch = Chain(dve, S["dchd"])
            dve.wait_ge(S["d_iota"], 4)
            n3 = [P, TT, 4]

            def b4(ap):
                return ap.unsqueeze(2).to_broadcast(n3)

            def first_max(oh, src, mx, ta):
                dch(dve.tensor_reduce(mx, src, AX, ALU.max))
                dch(tt(ta, src, b4(mx), ALU.is_equal))
                dch(tt(ta, ta, desc[:, :].unsqueeze(1).to_broadcast(n3), ALU.mult))
                dch(dve.tensor_reduce(R1[11][:, :], ta, AX, ALU.max))
                dch(tt(oh, ta, b4(R1[11][:, :]), ALU.is_equal))

            dch(dve.memset(logit[LAST:P, TF, :], 0.0))
            lg = logit[:, :, 0:NG]
            ohg, oh1, oh2 = R3[2][:, :, :], R3[3][:, :, :], R3[4][:, :, :]
            gm = R1[0][:, :]
            first_max(ohg, lg, gm, R3[5][:, :, :])
            dch(tt(R3[0][:, :, :], lg, b4(gm), ALU.subtract))
            dve.nop().then_inc(S["exp_in"], 1)
            for g in range(NG):
                dch(tt(L4[:, :, g, :], logit[:, :, NG + g * NEG:NG + (g + 1) * NEG], ohg[:, :, g:g + 1].to_broadcast(n3), ALU.mult))
            le = R3[6][:, :, :]
            dch(dve.tensor_reduce(le, L4[:, :, :, :].rearrange("p t g e -> p t e g"), AX, ALU.add))
            m1, m2 = R1[1][:, :], R1[2][:, :]
            first_max(oh1, le, m1, R3[5][:, :, :])
            dch(stt(R3[7][:, :, :], oh1, -1e30, le, ALU.mult, ALU.add))
            first_max(oh2, R3[7][:, :, :], m2, R3[5][:, :, :])
            dch(tt(R1[4][:, :], m2, m1, ALU.subtract))
            dve.nop().then_inc(S["exp_in"], 1)
            dve.wait_ge(S["exp_d"], 2)
            sg_, gw, w1_ = R1[3][:, :], R1[6][:, :], R1[7][:, :]
            dch(dve.tensor_reduce(sg_, R3[1][:, :, :], AX, ALU.add))
            dch(ts(w1_, R1[5][:, :], 1.0, None, ALU.add))
            dch(tt(gw, sg_, w1_, ALU.mult))
            dch(dve.reciprocal(cw[:, 0, :], gw))
            dch(tt(cw[:, 1, :], cw[:, 0, :], R1[5][:, :], ALU.mult))
            for EX, oh in ((E1, oh1), (E2, oh2)):
                for g in range(NG):
                    dch(tt(EX[:, :, g, :], oh, ohg[:, :, g:g + 1].to_broadcast(n3), ALU.mult))
                dch(dve.memset(EX[LAST:P, TF, :, :], 0.0))
            dch(tt(EE[:, :, :, :], E1[:, :, :, :], E2[:, :, :, :], ALU.add))
            dve.nop().then_inc(S["d_ready"], 1)
            dch(dve.memset(rst_t[:, :, :], 1.0))
            dch(dve.memset(rst_t[:, :, 0:1], 0.0))
            dve.wait_ge(S["cnt_done"], 1)
            dch(dve.tensor_copy(cnt[:, :, :], pbig[:, 1, 0:TT * NE].rearrange("p (t e) -> p e t", e=NE)))
            flat = lambda a: a[:, :, :].rearrange("p e t -> p (e t)")
            dch(dve.tensor_tensor_scan(flat(inc_t), flat(rst_t), flat(cnt), 0.0, ALU.mult, ALU.add))
            dch(tt(exc_t[:, :, :], inc_t[:, :, :], cnt[:, :, :], ALU.subtract))
            ne, nti, ntf, cum, bas = tei[:, 0, :], tei[:, 1, :], te[:, 1, :], te[:, 2, :], te[:, 3, :]
            dch(ts(ne, inc_t[:, :, TT - 1], float(P - 1), None, ALU.add))
            dch(ts(nti, ne, 7, None, ALU.logical_shift_right))
            dch(ts(ntf, nti, 1.0, None, ALU.max))
            dch(dve.memset(te[:, 0, :], 1.0))
            dch(dve.tensor_tensor_scan(cum, te[:, 0, :], ntf, 0.0, ALU.mult, ALU.add))
            beg = te[:, 4, :]
            dch(tt(beg, cum, ntf, ALU.subtract))
            dch(ts(bas, beg, float(P), 1.0, ALU.mult, ALU.add))
            dch(tt(exc_t[:, :, :], exc_t[:, :, :], bas.unsqueeze(2).to_broadcast([P, NE, TT]), ALU.add))
            dch(tt(spos[:, :, :], pbig[:, 0, 0:TT * NE].rearrange("p (t e) -> p t e", e=NE), exc_t[:, :, :].rearrange("p e t -> p t e"), ALU.add))
            for c, EX in enumerate((E1, E2)):
                ef = EX[:, :, :, :].rearrange("p t g e -> p t (g e)")
                dch(tt(ef, ef, spos[:, :, :], ALU.mult))
                dch(dve.tensor_reduce(R1[8 + c][:, :], ef, AX, ALU.add))
                dch(ts(slot_i[:, c, :], R1[8 + c][:, :], -1.0, None, ALU.add))
                dch(ts(si[:, c, 0, :], slot_i[:, c, :], 7, None, ALU.arith_shift_right))
                dch(ts(si[:, c, 1, :], slot_i[:, c, :], P - 1, None, ALU.bitwise_and))
            dch(dve.tensor_copy(sf[:, :, :, :], si[:, :, :, :]))
            for c in range(2):
                def over(ap, n):
                    return ap.unsqueeze(2).to_broadcast([P, TT, n])
                tiles, places = (iot[:, 0:n].unsqueeze(1).to_broadcast([P, TT, n]) for n in (SLOTS, P))
                tok, wgt = oh_hi[:, c, :, 0, :], oh_hi[:, c, :, 1, :]
                dch(tt(wgt, tiles, over(sf[:, c, 0, :], SLOTS), ALU.is_equal))
                dch(tt(tok, wgt, over(tokid[:, :], SLOTS), ALU.mult))
                dch(tt(wgt, wgt, over(cw[:, c, :], SLOTS), ALU.mult))
                tt(oh_lo[:, c, :, :], places, over(sf[:, c, 1, :], P), ALU.is_equal).then_inc(S["one_hot_done"], 1)
            dve.wait_ge(S["one_hot_done"], 2)
            dve.wait_ge(S["tbl_done"], 1)
            dch(tt(cmpe[:, :, :], cum[0:1, :].unsqueeze(1).to_broadcast([1, SLOTS, NE]), iot[0:1, 0:SLOTS].unsqueeze(2).to_broadcast([1, SLOTS, NE]), ALU.is_le))
            e_ = eof[:, 0, :]
            dch(dve.tensor_reduce(e_, cmpe[:, :, :], AX, ALU.add))
            dch(ts(e_, e_, float(NE - 1), None, ALU.min))
            def word(c):
                return ctrl[:, c:c + SLOTS]
            dch(dve.tensor_copy(word(C_EXP), e_))
            dch(ts(word(C_AT), word(C_EXP), 1, None, ALU.bitwise_and))
            f_, n_ = eof[:, 1, :], eof[:, 2, :]
            dch(tt(cmpe[:, :, :], beg[0:1, :].unsqueeze(1).to_broadcast([1, SLOTS, NE]), iot[0:1, 0:SLOTS].unsqueeze(2).to_broadcast([1, SLOTS, NE]), ALU.is_equal))
            dch(dve.tensor_reduce(f_, cmpe[:, :, 0:NE - 1], AX, ALU.add))
            dch(ts(n_, word(C_AT), -float(EW), float(EW - SKIP), ALU.mult, ALU.add))
            dch(tt(n_, n_, f_, ALU.mult))
            dch(ts(word(C_NEXT), n_, float(SKIP), None, ALU.add))
            dch(ts(n_, iot[0:1, 0:SLOTS], cum[0:1, NE - 1:NE], float(SKIP - EW), ALU.is_ge, ALU.mult))
            dch(stt(word(C_AT), word(C_AT), float(EW), n_, ALU.mult, ALU.add))
            dch(dve.tensor_copy(ctrl[:, C_USED:C_USED + 1], cum[0:1, NE - 1:NE]))
            dve.wait_ge(S["tbl_done"], 2)
            held = pbig[:, 2, 0:SLOTS]
            dch(ts(token_of[:, :], held, 1.0, -1.0, ALU.max, ALU.add))
            dch(ts(rowf[:, 0, :], held, 0.0, spare[:, 0:1], ALU.is_equal, ALU.mult))
            dch(stt(rowf[:, 1, :], held, -1.0, rowf[:, 0, :], ALU.add, ALU.add))
            dch(dve.tensor_copy(sum_of[:, :], rowf[:, 1, :]))
            dch(dve.tensor_copy(cw_of[:, :], pbig[:, 2, SLOTS:2 * SLOTS]))
            dve.nop().then_inc(S["ctl_done"], 1)

            def e_x_lo(s, b):
                for n in range(2):
                    dve.wait_ge(S["xgt_evac"], 2 * s + n + 1)
                    if n == 0 and not early(s):
                        dve.wait_ge(S["gu_done"], s - 1)
                    tt(xgL[b][:, 4 * n:4 * n + 4, :], pbig[:, 4 + n, :].rearrange("p (a m) -> p a m", a=4),
                       xgH[b][:, 4 * n:4 * n + 4, :].bitcast(F32), ALU.subtract).then_inc(S["xgt_lo"], 1)

            def e_h(s, b):
                dve.wait_ge(S["sl_done"], s + 1)
                if not early(s):
                    dve.wait_ge(S["ht_done"], s - 1)
                tt(hh[b][:, :], sl[:, :], pbig[:, 6, DE:2 * DE], ALU.mult).then_inc(S["h_done"], 1)

            def e_ht(s, b):
                dve.wait_ge(S["ht_done"], s + 1)
                if not early(s):
                    dve.wait_ge(S["dn_done"], s)
                ht = pbig[:, 7, 0:2 * P].rearrange("p (a m) -> p a m", a=2)
                dve.tensor_copy(hTH[b][:, :, :], ht).then_inc(S["dche"], 1)
                dve.wait_ge(S["dche"], s + 1)
                tt(hTL[b][:, :, :], ht, hTH[b][:, :, :].bitcast(F32), ALU.subtract).then_inc(S["ht_evac"], 1)

            def e_word(s):
                return dve.value_load(ctrl[0:1, ds(C_NEXT + s, 1)], min_val=0, max_val=EW)

            def e_split(s, to, part):
                with dve.If(to != SKIP):
                    e = dve.value_load(ctrl[0:1, ds(C_EXP + s, 1)], min_val=0, max_val=NE - 1)
                    for c in (range(UP_CUTS), range(UP_CUTS, CUTS))[part]:
                        dve.wait_ge(S["hi_split"], e * CUTS + (CUTS + c + 1))
                        dve.wait_ge(S["ctl_done"], 1)
                        w = ds(to + c * CW, CW)
                        tt(WL[:, w], WR[:, w], WH[:, w].bitcast(F32), ALU.subtract).then_inc(S["lo_split"], 1)

            dve.wait_ge(S["lo_split"], CUTS)
            e_x_lo(0, 0)

            def e_step(s, b, to, ahead=True, last=False):
                then = None
                if not last:
                    e_split(s, to, 0)
                e_h(s, b)
                if not last:
                    e_x_lo(s + 1, 1 - b)
                    if ahead:
                        then = e_word(s + 1)
                e_ht(s, b)
                if not last:
                    e_split(s, to, 1)
                return then

            to = e_step(0, 0, e_word(0))
            e_step(1, 1, to, ahead=False)
            def four(i):
                to = e_word(4 * i + 2)
                for n in range(2, 6):
                    to = e_step(4 * i + n, n % 2, to, ahead=n < 5)

            with dve.Fori(0, FULL // 4) as i:
                four(i)
            with dve.Fori(FULL // 4, SLOTS // 4 - 1) as i:
                with dve.If(used(dve, 4 * i + 1)):
                    four(i)
            with dve.If(used(dve, SLOTS - 3)):
                e_step(SLOTS - 2, 0, e_word(SLOTS - 2), ahead=False)
                e_step(SLOTS - 1, 1, None, last=True)

            def f_scale(t, b, rows=P):
                dve.wait_ge(S["f_std"], t + 1)
                dve.reciprocal(fnv[0:rows, 1, b:b + 1], fnv[0:rows, 0, b:b + 1]).then_inc(S["dchf"], 1)
                dve.wait_ge(S["dchf"], t + 1)
                if not early(t, NF):
                    dve.wait_ge(S[f"f_st{b}"], 16 * (t // NF) if isinstance(t, int) else 4 * (t - b))
                stt(fo[b][0:rows, :], fx[b][0:rows, :], fnv[0:rows, 1, b:b + 1], gl_b[0:rows, :], ALU.mult, ALU.mult).then_inc(S["f_out"], 1)
            for b in range(NF):
                f_scale(b, b)
            with dve.Fori(1, TF // NF) as i:
                for b in range(NF):
                    f_scale(NF * i + b, b)
            f_scale(TF, 0, LAST)


def kernel(**inputs):
    import numpy as np
    import concourse.bacc as bacc
    from concourse.bass_utils import run_bass_kernel_spmd as run

    a = {k: np.asarray(v) for k, v in inputs.items()}

    def order(p, s):
        rows = np.concatenate([s.reshape(NCH - NP_CH, L, -1), p.reshape(NP_CH, L, -1)], 0)
        return np.ascontiguousarray(rows.transpose(1, 0, 2))

    def states(x):
        x = x.reshape(x.shape[:-2] + (PR, 2, ST))
        x = np.moveaxis(x, (-2, -1, -3), (0, 1, 2))
        x = x.reshape((P, PR) + x.shape[3:])
        return x

    x = order(a["x_prompt"], a["x_sample"])
    x_rows = x.reshape(NT, D)
    x_cols = x.reshape(L, NCH, KD, P).transpose(0, 3, 2, 1)
    s0 = np.stack([states(a["state_ssm_re"]), states(a["state_ssm_im"])], 1)
    step = np.broadcast_to(a["ssm_log_step"][:, None], (G, ST))
    par = np.stack([states(v) for v in (a["ssm_lambda_re"], a["ssm_lambda_im"], step)], 1)

    def chans(v):
        return v.reshape(PR, 2, ST, GC).transpose(1, 2, 0, 3).reshape(P, PR, GC)

    bc = np.stack([chans(a["ssm_b_re"]), chans(a["ssm_b_im"]),
                   chans(a["ssm_c_re"].transpose(0, 2, 1)), chans(a["ssm_c_im"].transpose(0, 2, 1))], 1)
    dd = np.broadcast_to(a["ssm_d"].T[None], (L, GC, G)).reshape(P, G)
    route = np.concatenate([a["moe_router_group"][0], a["moe_router_expert"][0]], 1)
    gu = np.stack([a["moe_w_gate"][0], a["moe_w_up"][0]], 2)
    arrays = {
        "x_rows": x_rows, "x_cols": x_cols, "s0": s0, "par": par, "bc": bc, "dd": dd,
        "gmix": a["norm_mix"][0].reshape(KD, P).T, "gffn": a["norm_ffn"][0], "gfin": a["norm_final"],
        "w_in": a["ssm_w_in"].reshape(KD, P, W).transpose(1, 0, 2),
        "w_out": a["ssm_w_out"].reshape(CB, P, 2 * D).transpose(1, 0, 2),
        "route": route.reshape(KD, P, 20).transpose(1, 0, 2),
        "w_gu": gu.reshape(NE, KD, P, 2 * DE).transpose(0, 2, 1, 3).reshape(NE, P, KD * 2 * DE),
        "w_dn": a["moe_w_down"][0].reshape(NE, DE // P, P, D).transpose(0, 2, 1, 3).reshape(NE, P, DE // P * D),
    }
    arrays = {k: np.ascontiguousarray(v) for k, v in arrays.items()}
    nc = bacc.Bacc("TRN2", target_bir_lowering=False, num_devices=1)
    ins = {k: nc.dram_tensor(f"in_{k}", v.shape, mybir.dt.from_np(v.dtype), kind="ExternalInput").ap()
           for k, v in arrays.items()}
    y_out = nc.dram_tensor("out_y", (NT, D), F32, kind="ExternalOutput").ap()
    st_out = nc.dram_tensor("out_st", (P, 2, PR, DECB + 1), F32, kind="ExternalOutput").ap()
    hybrid_kernel(nc, ins["x_rows"], ins["x_cols"], ins["s0"], ins["par"], ins["bc"], None, ins["dd"], ins["gmix"],
                  ins["gffn"], ins["gfin"], ins["w_in"], ins["w_out"], ins["route"], ins["w_gu"], ins["w_dn"], y_out, st_out)
    r = run(nc, [{f"in_{k}": v for k, v in arrays.items()}], core_ids=[0])
    y = np.asarray(r.results[0]["out_y"]).reshape(L, NCH, D).transpose(1, 0, 2)
    st = np.asarray(r.results[0]["out_st"]).reshape(2, ST, 2, PR, DECB + 1)
    st = st.transpose(2, 4, 3, 0, 1).reshape(2, DECB + 1, G, ST)
    c = np.ascontiguousarray
    return (c(y[DECB:].reshape(1, SEQ, D)), c(y[:DECB].reshape(DECB, DECS, D)),
            c(st[0, DECB:]), c(st[1, DECB:]), c(st[0, :DECB]), c(st[1, :DECB]), None)
```
